# Optimizing a Trainium2 kernel written in Bass

```python
import jax, jax.numpy as jnp
from jax import lax
import numpy as np

D_MODEL = 1024
BATCH = 1
SEQ = 1024
DEPTH = 1
DEC_BATCH = 8
DEC_SEQ = 8
PAST_LEN = 2048
PAGE_SIZE = 128

H_ATT = 8
DH_ATT = 64
H_IDX = 8
D_IDX = 64
TOPK_MAX = 256
Q_BLOCK = 128
LRU_W = 512
LRU_BLOCKS = 8
LRU_BS = LRU_W // LRU_BLOCKS
CONV_W = 4
LRU_C = 8.0
H_MEM = 4
DH_MEM = 128
N_MEM = 256
D_FF = 2816
N_BRANCH = 3
EPS = 1e-6
IN_SIZES = (H_ATT * DH_ATT, H_ATT * DH_ATT, H_ATT * DH_ATT, H_IDX * D_IDX, D_IDX, H_IDX,
            LRU_W, LRU_W, H_MEM * DH_MEM, N_BRANCH * D_MODEL)
D_IN = sum(IN_SIZES)

kernel_name = "hybrid_dsa_rglru_memxattn_macaron_step"

def rmsnorm(x, g):
    xf = x.astype(jnp.float32)
    y = xf * lax.rsqrt(jnp.mean(xf * xf, axis=-1, keepdims=True) + EPS)
    return (y * g.astype(jnp.float32)).astype(x.dtype)

def swiglu(x, g, w_in, w_out):
    gate, up = jnp.split(rmsnorm(x, g) @ w_in, 2, axis=-1)
    return (jax.nn.silu(gate) * up) @ w_out

def split_in(h, w_in):
    offs, acc = [], 0
    for s in IN_SIZES[:-1]:
        acc += s
        offs.append(acc)
    return jnp.split(h @ w_in, offs, axis=-1)

def mix_inputs(x, lw):
    B, T = x.shape[:2]
    h = rmsnorm(x, lw["norm_mix_g"])
    q, k, v, qi, ki, wi, lx, lg, qm, gates = split_in(h, lw["w_in"])
    q = rmsnorm(q.reshape(B, T, H_ATT, DH_ATT), lw["q_norm_g"])
    k = rmsnorm(k.reshape(B, T, H_ATT, DH_ATT), lw["k_norm_g"])
    v = v.reshape(B, T, H_ATT, DH_ATT)
    qi = qi.reshape(B, T, H_IDX, D_IDX)
    qm = rmsnorm(qm.reshape(B, T, H_MEM, DH_MEM), lw["mem_q_norm_g"])
    return q, k, v, qi, ki, wi, lx, lg, qm, gates

def indexer_scores(qi, wi, kidx):
    dots = jnp.einsum("bthd,bsd->bths", qi, kidx, preferred_element_type=jnp.float32)
    w = wi.astype(jnp.float32) * (H_IDX ** -0.5 * D_IDX ** -0.5)
    return jnp.einsum("bths,bth->bts", jax.nn.relu(dots), w)

def sparse_core(q, k_sel, v_sel, valid):
    s = jnp.einsum("bthd,btkhd->bthk", q, k_sel, preferred_element_type=jnp.float32) * (DH_ATT ** -0.5)
    s = jnp.where(valid[:, :, None, :], s, -jnp.inf)
    p = jax.nn.softmax(s, axis=-1).astype(v_sel.dtype)
    o = jnp.einsum("bthk,btkhd->bthd", p, v_sel)
    return o.reshape(o.shape[0], o.shape[1], H_ATT * DH_ATT)

def dsa_prompt(q, k, v, qi, wi, kidx):
    B, S = q.shape[:2]
    topk = min(TOPK_MAX, S // 4)
    n_blk = S // Q_BLOCK
    bidx = jnp.arange(B)[:, None, None]
    key_pos = jnp.arange(S)

    def block(i):
        t0 = i * Q_BLOCK
        qb = lax.dynamic_slice_in_dim(q, t0, Q_BLOCK, axis=1)
        qib = lax.dynamic_slice_in_dim(qi, t0, Q_BLOCK, axis=1)
        wib = lax.dynamic_slice_in_dim(wi, t0, Q_BLOCK, axis=1)
        qpos = t0 + jnp.arange(Q_BLOCK)
        causal = key_pos[None, :] <= qpos[:, None]
        sc = jnp.where(causal[None], indexer_scores(qib, wib, kidx), -jnp.inf)
        _, idx = lax.top_k(sc, topk)
        valid = idx <= qpos[None, :, None]
        return sparse_core(qb, k[bidx, idx], v[bidx, idx], valid)

    o = lax.map(block, jnp.arange(n_blk))
    return jnp.moveaxis(o, 0, 1).reshape(B, S, H_ATT * DH_ATT)

def dsa_sample(q, k, v, qi, wi, kidx, cache_k, cache_v, cache_kidx, page_table):
    B, T = q.shape[:2]
    past = page_table.shape[1] * PAGE_SIZE
    n_keys = past + T
    topk = min(TOPK_MAX, n_keys // 4)
    kidx_past = cache_kidx[page_table].reshape(B, past, D_IDX)
    kidx_all = jnp.concatenate([kidx_past, kidx.astype(kidx_past.dtype)], axis=1)
    qpos = past + jnp.arange(T)
    causal = jnp.arange(n_keys)[None, :] <= qpos[:, None]
    sc = jnp.where(causal[None], indexer_scores(qi, wi, kidx_all), -jnp.inf)
    _, idx = lax.top_k(sc, topk)
    valid = idx <= qpos[None, :, None]
    bidx = jnp.arange(B)[:, None, None]
    pidx = jnp.minimum(idx, past - 1)
    phys = page_table[bidx, pidx // PAGE_SIZE]
    off = pidx % PAGE_SIZE
    nidx = jnp.clip(idx - past, 0, T - 1)
    is_new = (idx >= past)[..., None, None]
    k_sel = jnp.where(is_new, k[bidx, nidx].astype(cache_k.dtype), cache_k[phys, off])
    v_sel = jnp.where(is_new, v[bidx, nidx].astype(cache_v.dtype), cache_v[phys, off])
    return sparse_core(q, k_sel, v_sel, valid)

def rglru_branch(lx, lg, conv_buf, h_prev, lw):
    f32 = jnp.float32
    B, T = lx.shape[:2]
    xpad = jnp.concatenate([conv_buf.astype(lx.dtype), lx], axis=1)
    conv = lw["conv_b"].astype(f32)
    for j in range(CONV_W):
        conv = conv + xpad[:, j:j + T].astype(f32) * lw["conv_w"][j].astype(f32)
    new_buf = xpad[:, T:]
    xb = conv.reshape(B, T, LRU_BLOCKS, LRU_BS)
    r = jax.nn.sigmoid(jnp.einsum("btni,nij->btnj", xb, lw["lru_wa"].astype(f32)).reshape(B, T, LRU_W)
                       + lw["lru_ba"].astype(f32))
    i = jax.nn.sigmoid(jnp.einsum("btni,nij->btnj", xb, lw["lru_wi"].astype(f32)).reshape(B, T, LRU_W)
                       + lw["lru_bi"].astype(f32))
    log_a = -LRU_C * r * jax.nn.softplus(-lw["lru_lambda"].astype(f32))
    a = jnp.exp(log_a)
    b = jnp.sqrt(-jnp.expm1(2.0 * log_a)) * (i * conv)
    b = b.at[:, 0].add(a[:, 0] * h_prev.astype(f32))

    def comb(c1, c2):
        a1, b1 = c1
        a2, b2 = c2
        return a1 * a2, a2 * b1 + b2

    _, h = lax.associative_scan(comb, (a, b), axis=1)
    y = h * jax.nn.gelu(lg.astype(f32))
    return y.astype(lx.dtype), new_buf, h[:, -1].astype(lx.dtype)

def mem_kv(mem, lw):
    B, M = mem.shape[:2]
    mk, mv = jnp.split(rmsnorm(mem, lw["norm_mem_g"]) @ lw["w_mem_kv"], 2, axis=-1)
    mk = rmsnorm(mk.reshape(B, M, H_MEM, DH_MEM), lw["mem_k_norm_g"])
    return mk, mv.reshape(B, M, H_MEM, DH_MEM)

def mem_attend(qm, mk, mv):
    s = jnp.einsum("bthd,bmhd->bthm", qm, mk, preferred_element_type=jnp.float32) * (DH_MEM ** -0.5)
    p = jax.nn.softmax(s, axis=-1).astype(mv.dtype)
    o = jnp.einsum("bthm,bmhd->bthd", p, mv)
    return o.reshape(o.shape[0], o.shape[1], H_MEM * DH_MEM)

def merge(o_att, o_lru, o_mem, gates, lw):
    g = jax.nn.sigmoid(gates.astype(jnp.float32)).astype(o_att.dtype)
    g = g.reshape(gates.shape[0], gates.shape[1], N_BRANCH, D_MODEL)
    m = (g[:, :, 0] * (o_att @ lw["w_attn_o"]) + g[:, :, 1] * (o_lru @ lw["w_lru_o"])
         + g[:, :, 2] * (o_mem @ lw["w_mem_o"]))
    return m @ lw["w_out"]

def layer_prompt(x, mem, lw):
    x = x + 0.5 * swiglu(x, lw["norm_ffn1_g"], lw["w_ffn1_in"], lw["w_ffn1_out"])
    q, k, v, qi, ki, wi, lx, lg, qm, gates = mix_inputs(x, lw)
    o_att = dsa_prompt(q, k, v, qi, wi, ki)
    B = x.shape[0]
    buf0 = jnp.zeros((B, CONV_W - 1, LRU_W), x.dtype)
    h0 = jnp.zeros((B, LRU_W), jnp.float32)
    o_lru, conv_buf, h_last = rglru_branch(lx, lg, buf0, h0, lw)
    mk, mv = mem_kv(mem, lw)
    o_mem = mem_attend(qm, mk, mv)
    x = x + merge(o_att, o_lru, o_mem, gates, lw)
    x = x + 0.5 * swiglu(x, lw["norm_ffn2_g"], lw["w_ffn2_in"], lw["w_ffn2_out"])
    return x, (k, v, ki, mk, mv, conv_buf, h_last)

def layer_sample(x, ck, cv, cki, page_table, cmk, cmv, sconv, sh, lw):
    x = x + 0.5 * swiglu(x, lw["norm_ffn1_g"], lw["w_ffn1_in"], lw["w_ffn1_out"])
    q, k, v, qi, ki, wi, lx, lg, qm, gates = mix_inputs(x, lw)
    o_att = dsa_sample(q, k, v, qi, wi, ki, ck, cv, cki, page_table)
    o_lru, conv_buf, h_last = rglru_branch(lx, lg, sconv, sh, lw)
    o_mem = mem_attend(qm, cmk, cmv)
    x = x + merge(o_att, o_lru, o_mem, gates, lw)
    x = x + 0.5 * swiglu(x, lw["norm_ffn2_g"], lw["w_ffn2_in"], lw["w_ffn2_out"])
    return x, (k, v, ki, conv_buf, h_last)

def setup_inputs(seed: int = 0) -> dict:
    key = jax.random.key(seed)
    keys = iter(jax.random.split(key, 64))
    f32 = jnp.float32

    def normal(shape, scale):
        return scale * jax.random.normal(next(keys), shape, f32)

    def gain(shape):
        return 1.0 + 0.05 * jax.random.normal(next(keys), shape, f32)

    L = DEPTH
    n_pages = PAST_LEN // PAGE_SIZE
    n_used = DEC_BATCH * n_pages
    n_phys = n_used + max(1, n_used // 4)
    page_table = jax.random.permutation(next(keys), n_phys)[:n_used].reshape(DEC_BATCH, n_pages).astype(jnp.int32)
    hd = H_ATT * DH_ATT
    md = H_MEM * DH_MEM
    a0 = jax.random.uniform(next(keys), (L, LRU_W), f32, 0.9, 0.999)
    p = jnp.exp(jnp.log(a0) / LRU_C)
    lru_lambda = jnp.log(p) - jnp.log1p(-p)
    return {
        "x_prompt": normal((BATCH, SEQ, D_MODEL), 1.0),
        "x_sample": normal((DEC_BATCH, DEC_SEQ, D_MODEL), 1.0),
        "cache_k": normal((L, n_phys, PAGE_SIZE, H_ATT, DH_ATT), 1.0),
        "cache_v": normal((L, n_phys, PAGE_SIZE, H_ATT, DH_ATT), 1.0),
        "cache_kidx": normal((L, n_phys, PAGE_SIZE, D_IDX), 1.0),
        "page_table": page_table,
        "cache_mem_k": normal((L, DEC_BATCH, N_MEM, H_MEM, DH_MEM), 1.0),
        "cache_mem_v": normal((L, DEC_BATCH, N_MEM, H_MEM, DH_MEM), 1.0),
        "state_conv": normal((L, DEC_BATCH, CONV_W - 1, LRU_W), 1.0),
        "state_h": normal((L, DEC_BATCH, LRU_W), 0.5),
        "mem_prompt": normal((BATCH, N_MEM, D_MODEL), 1.0),
        "norm_ffn1_g": gain((L, D_MODEL)),
        "w_ffn1_in": normal((L, D_MODEL, 2 * D_FF), D_MODEL ** -0.5),
        "w_ffn1_out": normal((L, D_FF, D_MODEL), D_FF ** -0.5),
        "norm_mix_g": gain((L, D_MODEL)),
        "w_in": normal((L, D_MODEL, D_IN), D_MODEL ** -0.5),
        "q_norm_g": gain((L, DH_ATT)),
        "k_norm_g": gain((L, DH_ATT)),
        "w_attn_o": normal((L, hd, D_MODEL), hd ** -0.5),
        "conv_w": normal((L, CONV_W, LRU_W), CONV_W ** -0.5),
        "conv_b": normal((L, LRU_W), 0.01),
        "lru_wa": normal((L, LRU_BLOCKS, LRU_BS, LRU_BS), LRU_BS ** -0.5),
        "lru_ba": normal((L, LRU_W), 0.01),
        "lru_wi": normal((L, LRU_BLOCKS, LRU_BS, LRU_BS), LRU_BS ** -0.5),
        "lru_bi": normal((L, LRU_W), 0.01),
        "lru_lambda": lru_lambda,
        "w_lru_o": normal((L, LRU_W, D_MODEL), LRU_W ** -0.5),
        "norm_mem_g": gain((L, D_MODEL)),
        "w_mem_kv": normal((L, D_MODEL, 2 * md), D_MODEL ** -0.5),
        "mem_q_norm_g": gain((L, DH_MEM)),
        "mem_k_norm_g": gain((L, DH_MEM)),
        "w_mem_o": normal((L, md, D_MODEL), md ** -0.5),
        "w_out": normal((L, D_MODEL, D_MODEL), D_MODEL ** -0.5),
        "norm_ffn2_g": gain((L, D_MODEL)),
        "w_ffn2_in": normal((L, D_MODEL, 2 * D_FF), D_MODEL ** -0.5),
        "w_ffn2_out": normal((L, D_FF, D_MODEL), D_FF ** -0.5),
    }

def reference(x_prompt, x_sample, cache_k, cache_v, cache_kidx, page_table, cache_mem_k, cache_mem_v,
              state_conv, state_h, mem_prompt, norm_ffn1_g, w_ffn1_in, w_ffn1_out, norm_mix_g, w_in,
              q_norm_g, k_norm_g, w_attn_o, conv_w, conv_b, lru_wa, lru_ba, lru_wi, lru_bi, lru_lambda,
              w_lru_o, norm_mem_g, w_mem_kv, mem_q_norm_g, mem_k_norm_g, w_mem_o, w_out, norm_ffn2_g,
              w_ffn2_in, w_ffn2_out):
    xp, xs = x_prompt, x_sample
    p_states, s_states = [], []
    for l in range(DEPTH):
        lw = {
            "norm_ffn1_g": norm_ffn1_g[l], "w_ffn1_in": w_ffn1_in[l], "w_ffn1_out": w_ffn1_out[l],
            "norm_mix_g": norm_mix_g[l], "w_in": w_in[l], "q_norm_g": q_norm_g[l], "k_norm_g": k_norm_g[l],
            "w_attn_o": w_attn_o[l], "conv_w": conv_w[l], "conv_b": conv_b[l], "lru_wa": lru_wa[l],
            "lru_ba": lru_ba[l], "lru_wi": lru_wi[l], "lru_bi": lru_bi[l], "lru_lambda": lru_lambda[l],
            "w_lru_o": w_lru_o[l], "norm_mem_g": norm_mem_g[l], "w_mem_kv": w_mem_kv[l],
            "mem_q_norm_g": mem_q_norm_g[l], "mem_k_norm_g": mem_k_norm_g[l], "w_mem_o": w_mem_o[l],
            "w_out": w_out[l], "norm_ffn2_g": norm_ffn2_g[l], "w_ffn2_in": w_ffn2_in[l],
            "w_ffn2_out": w_ffn2_out[l],
        }
        xp, st_p = layer_prompt(xp, mem_prompt, lw)
        xs, st_s = layer_sample(xs, cache_k[l], cache_v[l], cache_kidx[l], page_table, cache_mem_k[l],
                                cache_mem_v[l], state_conv[l], state_h[l], lw)
        p_states.append(st_p)
        s_states.append(st_s)
    new_k_prompt = jnp.stack([s[0] for s in p_states])
    new_v_prompt = jnp.stack([s[1] for s in p_states])
    new_kidx_prompt = jnp.stack([s[2] for s in p_states])
    new_mem_k_prompt = jnp.stack([s[3] for s in p_states])
    new_mem_v_prompt = jnp.stack([s[4] for s in p_states])
    new_conv_prompt = jnp.stack([s[5] for s in p_states])
    new_h_prompt = jnp.stack([s[6] for s in p_states])
    new_k_sample = jnp.stack([s[0] for s in s_states])
    new_v_sample = jnp.stack([s[1] for s in s_states])
    new_kidx_sample = jnp.stack([s[2] for s in s_states])
    new_conv_sample = jnp.stack([s[3] for s in s_states])
    new_h_sample = jnp.stack([s[4] for s in s_states])
    return (xp, xs, new_k_prompt, new_v_prompt, new_kidx_prompt, new_mem_k_prompt, new_mem_v_prompt,
            new_conv_prompt, new_h_prompt, new_k_sample, new_v_sample, new_kidx_sample,
            new_conv_sample, new_h_sample)


_drawn_inputs = setup_inputs


def setup_inputs(seed=0):
    import zlib

    import numpy as np

    out = dict(_drawn_inputs(seed))
    spreads = {}
    factors = {'q_norm_g': 8.0, 'lru_ba': 23.55, 'lru_bi': 8.0, 'mem_q_norm_g': 8.0, 'norm_ffn2_g': 2.891}
    for name, (base, spread) in spreads.items():
        noise = np.random.default_rng([zlib.crc32(name.encode()), seed]).standard_normal(out[name].shape)
        drawn = base * np.exp(spread * noise) if base else spread * noise
        out[name] = __import__('jax').numpy.asarray(drawn.astype(out[name].dtype))
    for name, factor in factors.items():
        out[name] = (out[name] * factor).astype(out[name].dtype)
    return out
```

```python
from contextlib import ExitStack, contextmanager

import numpy as np

import concourse.bass as bass
from concourse import mybir

F32 = mybir.dt.float32
F32R = mybir.dt.float32r
BF16 = mybir.dt.bfloat16
I32 = mybir.dt.int32
ALU = mybir.AluOpType
ACT = mybir.ActivationFunctionType
AX = mybir.AxisListType

P = 128
SEQ = 1024
DEC_B = 8
DEC_T = 8
NS = DEC_B * DEC_T
NT = SEQ + NS
D = 1024
KT = D // P
D_FF = 2816
H = 8
DH = 64
HD = H * DH
PAGE = 128
PAGES = 16
PAST = PAGE * PAGES
N_KEYS = PAST + DEC_T
TOPK = 256
H_MEM = 4
N_MEM = 256
LRU_W = 512
LT = LRU_W // P
EPS = 1e-6
BIG = -1e30
TAKEN = -3e38
BARRED = -2e38

CH = [(0, 364), (364, 362), (726, 362)]
CW = 364
TT = [(t * P, P) for t in range(SEQ // P)] + [(SEQ, NS)]

C_Q, C_K, C_V, C_QI, C_KI, C_LX, C_LG, C_QM, C_G = 0, 512, 1024, 1536, 2048, 2120, 2632, 3144, 3656

ROWS = {}
_at = 0
for _name, _n in (("g_ffn1", 8), ("g_mix", 8), ("g_ffn2", 8), ("g_mem", 8), ("conv_w", 16), ("conv_b", 4),
                  ("ba", 4), ("bi", 4), ("lam", 4), ("gq", 1), ("gk", 1), ("gmq", 1), ("gmk", 1), ("h0", 32)):
    ROWS[_name] = _at
    _at += _n
N_ROWS = _at


class Memory:

    def __init__(self, nc):
        self.nc = nc
        self.n = 0

    def at(self, name, shape, dt, offset):
        self.n += 1
        return self.nc.alloc_sbuf_tensor_at(f"{name}_{self.n}", shape, dt, offset=offset)


@contextmanager
def phase(nc):
    given = []

    def sem(name):
        given.append(nc.alloc_semaphore(name=name))
        return given[-1]

    yield sem
    nc.clear_and_free_semaphores(given)
    nc.all_engine_barrier()


AT_H = 16512
AT_W = AT_H + 2 * KT * NT * 4
AT_C = AT_W + 9 * 4096
AT_X = AT_C + 4096
AT_A = AT_X + KT * NT * 4
AT_END = 229344
AT_B = AT_END - 14592


def transposes_pe(pe, nc, jobs, ident, bank, ready, evicted, done):
    for n, job in enumerate(jobs):
        for sem, value in job["needs"]:
            pe.wait_ge(sem, value)
        if n >= len(bank):
            pe.wait_ge(evicted[n % 2], n // 2 - len(bank) // 2 + 1)
        at = 0
        for src in job["src"]:
            rows, cols = src.shape
            mm = pe.transpose(bank[n % len(bank)][0:cols, at:at + rows], src, ident[0:rows, 0:rows])
            at += job.get("step", rows)
        mm.then_inc(done, 1)


def transposes_evict(eng, copy, jobs, which, bank, done, evicted):
    for n, job in enumerate(jobs):
        if n % 2 != which:
            continue
        eng.wait_ge(done, n + 1)
        copy(job["dst"], job["psum"](bank[n % len(bank)])).then_inc(evicted[which], 1)


def norm_stage(nc, block, sem, mem, bank, x, width, chunks, gain, ones, hi, lo, tag, scratch):
    sq = mem.at(f"sq{tag}", [P, 2, width], F32, scratch)
    rs = mem.at(f"rs{tag}", [P, width], F32, scratch + 2 * width * 4)
    hn = mem.at(f"hn{tag}", [P, 2, width], F32, scratch + 3 * width * 4)
    eps = mem.at(f"eps{tag}", [P, 1], F32, scratch + 5 * width * 4)
    squared = sem(f"squared{tag}")
    summed = sem(f"summed{tag}")
    rooted = sem(f"rooted{tag}")
    inverted = sem(f"inverted{tag}")
    normed = sem(f"normed{tag}")
    high = sem(f"high{tag}")
    low = sem(f"low{tag}")
    eps_set = sem(f"eps_set{tag}")

    @block.scalar
    def _(act):
        for k in range(KT):
            if k >= 2:
                act.wait_ge(summed, k - 1)
            act.activation(sq[:, k % 2, :], x[:, k, :], ACT.Square).then_inc(squared, 1)
        act.wait_ge(summed, KT)
        act.wait_ge(eps_set, 1)
        for c, (t0, w) in enumerate(chunks):
            act.activation(rs[:, t0:t0 + w], bank[c][:, 0:w], ACT.Sqrt, bias=eps[:, 0:1],
                           scale=1.0 / D).then_inc(rooted, 1)
        for k in range(KT):
            act.wait_ge(normed, k + 1)
            act.copy(hi[:, k, :], hn[:, k % 2, :]).then_inc(high, 1)

    @block.tensor
    def _(pe):
        for k in range(KT):
            pe.wait_ge(squared, k + 1)
            for c, (t0, w) in enumerate(chunks):
                mm = pe.matmul(bank[c][:, 0:w], ones[:, :], sq[:, k % 2, t0:t0 + w],
                               start=(k == 0), stop=(k == KT - 1))
            mm.then_inc(summed, 1)

    @block.vector
    def _(dve):
        dve.memset(eps[:, :], EPS).then_inc(eps_set, 1)
        dve.wait_ge(rooted, len(chunks))
        dve.reciprocal(rs[:, :], rs[:, :]).then_inc(inverted, 1)
        dve.wait_ge(inverted, 1)
        for k in range(KT + 1):
            if k < KT:
                if k >= 2:
                    dve.wait_ge(high, k - 1)
                    dve.wait_ge(low, k - 1)
                dve.scalar_tensor_tensor(hn[:, k % 2, :], x[:, k, :], gain[:, k:k + 1], rs[:, :],
                                         ALU.mult, ALU.mult).then_inc(normed, 1)
            if k >= 1:
                dve.wait_ge(high, k)
                dve.tensor_tensor(lo[:, k - 1, :], hn[:, (k - 1) % 2, :], hi[:, k - 1, :].bitcast(F32),
                                  ALU.subtract).then_inc(low, 1)


def products(pe, out, w_hi, w_lo, a_hi, a_lo, ks, start, stop, flip=False):
    n = len(ks)
    for i, (kw, ka) in enumerate(ks):
        for j, (w, a) in enumerate(((w_hi, a_hi), (w_hi, a_lo), (w_lo, a_hi))):
            left, right = (a(ka), w(kw)) if flip else (w(kw), a(ka))
            mm = pe.matmul(out, left, right, start=(start and i == 0 and j == 0),
                           stop=(stop and i == n - 1 and j == 2))
    return mm


def ffn(nc, sem, mem, bank, x, h_hi, h_lo, raw, w_hi, w_lo, w_in, w_out, tag):
    G = D_FF // (2 * P)
    a_hi = mem.at(f"a_hi{tag}", [P, 2, NT], F32R, AT_A)
    a_lo = mem.at(f"a_lo{tag}", [P, 2, NT], F32R, AT_A + 2 * NT * 4)
    sg = mem.at(f"sg{tag}", [P, 3, CW], F32, AT_A + 4 * NT * 4)
    pr = mem.at(f"pr{tag}", [P, 3, CW], F32, AT_A + 4 * NT * 4 + 4384)
    loaded = [sem(f"unit_loaded{i}{tag}") for i in range(3)]
    high = sem(f"unit_high{tag}")
    low = sem(f"unit_low{tag}")
    gate_ready = sem(f"gate_ready{tag}")
    up_ready = sem(f"up_ready{tag}")
    silu_done = sem(f"silu_done{tag}")
    prod_done = sem(f"prod_done{tag}")
    prod_high = sem(f"prod_high{tag}")
    prod_low = sem(f"prod_low{tag}")
    out_ready = sem(f"out_ready{tag}")
    x_added = sem(f"x_added{tag}")
    RING, XC = 3, 24
    win = w_in.rearrange("(k p) n -> p k n", p=P)
    wout = w_out.rearrange("(r p) n -> p r n", p=P)

    def src(i, u):
        if u < 4:
            col = (u % 2) * D_FF + (u // 2) * P
            return win[:, :, bass.ds(i * (2 * P) + col, P)]
        return wout[:, bass.ds(i * 2 + (u - 4), 1), :]

    def wh(s):
        return lambda k: w_hi[:, s, k * P:(k + 1) * P]

    def wl(s):
        return lambda k: w_lo[:, s, k * P:(k + 1) * P]

    with nc.Block() as block:
        @block.sync
        def _(sp):
            with sp.Fori(0, G) as i:
                for u in range(6):
                    sp.wait_ge(low, i * 6 + u + 1)
                    dst = raw[:, u % 3, :]
                    dst = dst.rearrange("p (k n) -> p k n", k=KT) if u < 4 else \
                        dst.rearrange("p (a n) -> p a n", a=1)
                    sp.dma_start(dst, src(i, u)).then_inc(loaded[u % 3], 16)

        @block.gpsimd
        def _(pool):
            pool.sem_inc(low, RING)
            with pool.Fori(0, G) as i:
                for u in range(6):
                    pool.wait_ge(high, i * 6 + u + 1)
                    pool.tensor_tensor(w_lo[:, u % 3, :], raw[:, u % 3, :], w_hi[:, u % 3, :].bitcast(F32),
                                       ALU.subtract).then_inc(low, 1)

        @block.tensor
        def _(pe):
            pe.sem_inc(out_ready, XC)
            with pe.Fori(0, G) as i:
                for t in range(2):
                    for half, (ready, free) in enumerate(((gate_ready, silu_done), (up_ready, prod_done))):
                        u = 2 * t + half
                        pe.wait_ge(low, i * 6 + u + 1 + RING)
                        for c, (t0, w) in enumerate(CH):
                            pe.wait_ge(free, i * 6 + 3 * t + c + 1)
                            mm = products(pe, bank[3 * half + c][:, 0:w], wh(u % 3), wl(u % 3),
                                          lambda k: h_hi[:, k, t0:t0 + w], lambda k: h_lo[:, k, t0:t0 + w],
                                          [(k, k) for k in range(KT)], True, True)
                            mm.then_inc(ready, 1)
                pe.wait_ge(low, i * 6 + 6 + RING)
                for c, (t0, w) in enumerate(CH):
                    pe.wait_ge(prod_low, i * 6 + 3 + c + 1)
                    for j in range(KT):
                        n = 8 * c + j
                        pe.wait_ge(x_added, i * XC + n - 1 + XC)
                        o = bank[6 + n % 2][:, 0:w]
                        products(pe, o, lambda k: w_hi[:, 1, j * P:(j + 1) * P],
                                 lambda k: w_lo[:, 1, j * P:(j + 1) * P],
                                 lambda k: a_hi[:, 0, t0:t0 + w], lambda k: a_lo[:, 0, t0:t0 + w],
                                 [(0, 0)], True, False)
                        mm = products(pe, o, lambda k: w_hi[:, 2, j * P:(j + 1) * P],
                                      lambda k: w_lo[:, 2, j * P:(j + 1) * P],
                                      lambda k: a_hi[:, 1, t0:t0 + w], lambda k: a_lo[:, 1, t0:t0 + w],
                                      [(0, 0)], False, True)
                        mm.then_inc(out_ready, 1)

        def high_part(act, i, u, first=False):
            if u in (1, 2):
                act.wait_ge(out_ready, i * XC + XC)
            elif u in (3, 5):
                act.wait_ge(gate_ready, i * 6 + (3 if u == 3 else 6))
            elif u == 4:
                act.wait_ge(up_ready, i * 6 + 3)
            elif not first:
                act.wait_ge(up_ready, i * 6)
            act.wait_ge(loaded[u % 3], i * 32 + 16 * (u // 3 + 1))
            act.copy(w_hi[:, u % 3, :], raw[:, u % 3, :]).then_inc(high, 1)

        def act_round(act, i, last):
            for u in range(6):
                if not last or u < 4:
                    high_part(act, i + (u + 2) // 6, (u + 2) % 6)
                t = u // 2
                if u < 4 and u % 2 == 0:
                    for c, (t0, w) in enumerate(CH):
                        act.wait_ge(gate_ready, i * 6 + 3 * t + c + 1)
                        act.wait_ge(prod_done, i * 6 + 3 * t + c + 1)
                        act.activation(sg[:, c, 0:w], bank[c][:, 0:w], ACT.Silu).then_inc(silu_done, 1)
                elif u < 4:
                    for c, (t0, w) in enumerate(CH):
                        act.wait_ge(prod_done, i * 6 + 3 * t + c + 1 + RING)
                        act.wait_ge(out_ready, i * XC + XC)
                        act.copy(a_hi[:, t, t0:t0 + w], pr[:, c, 0:w]).then_inc(prod_high, 1)

        @block.scalar
        def _(act):
            act.sem_inc(silu_done, RING)
            high_part(act, 0, 0, True)
            high_part(act, 0, 1)
            with act.Fori(0, G - 1) as i:
                act_round(act, i, False)
            act_round(act, G - 1, True)

        @block.vector
        def _(dve):
            dve.sem_inc(prod_done, RING)
            dve.sem_inc(x_added, XC)
            with dve.Fori(0, G) as i:
                for t in range(2):
                    def product(c):
                        t0, w = CH[c]
                        dve.wait_ge(silu_done, i * 6 + 3 * t + c + 1 + RING)
                        dve.wait_ge(up_ready, i * 6 + 3 * t + c + 1)
                        dve.tensor_tensor(pr[:, c, 0:w], sg[:, c, 0:w], bank[3 + c][:, 0:w],
                                          ALU.mult).then_inc(prod_done, 1)

                    def low_part(c):
                        t0, w = CH[c]
                        dve.wait_ge(prod_high, i * 6 + 3 * t + c + 1)
                        dve.tensor_tensor(a_lo[:, t, t0:t0 + w], pr[:, c, 0:w],
                                          a_hi[:, t, t0:t0 + w].bitcast(F32),
                                          ALU.subtract).then_inc(prod_low, 1)
                    product(0)
                    product(1)
                    low_part(0)
                    low_part(1)
                    product(2)
                    low_part(2)
                for c, (t0, w) in enumerate(CH):
                    for j in range(KT):
                        n = 8 * c + j
                        dve.wait_ge(out_ready, i * XC + n + 1 + XC)
                        dve.wait_ge(x_added, i * XC + n + 1)
                        dve.scalar_tensor_tensor(x[:, j, t0:t0 + w], bank[6 + n % 2][:, 0:w], 0.5,
                                                 x[:, j, t0:t0 + w], ALU.mult, ALU.add).then_inc(x_added, 1)


def decoder_step(nc, I, O):
    ctx = ExitStack()
    with ctx:
        mem = Memory(nc)

        bank_t = ctx.enter_context(nc.psum_tensor("bank", [P, 8, 512], F32))
        bank = [bank_t[:, b, :] for b in range(8)]
        h_hi = mem.at("h_hi", [P, KT, NT], F32R, AT_H)
        h_lo = mem.at("h_lo", [P, KT, NT], F32R, AT_H + KT * NT * 4)
        raw = mem.at("raw", [P, 3, 1024], F32, AT_W)
        w_hi = mem.at("w_hi", [P, 3, 1024], F32R, AT_W + 3 * 4096)
        w_lo = mem.at("w_lo", [P, 3, 1024], F32R, AT_W + 6 * 4096)
        x = mem.at("x", [P, KT, NT], F32, AT_X)
        ident = mem.at("ident", [P, P], F32, AT_C)
        ones = mem.at("ones", [P, P], F32, AT_C + 512)
        ones_half = mem.at("ones_half", [P, P], F32, AT_C + 1024)
        ident16 = mem.at("ident16", [P, P], BF16, AT_C + 1536)
        par = mem.at("par", [P, N_ROWS], F32, AT_C + 1792)

        def column(name, k=0, n=1):
            return par[:, ROWS[name] + k:ROWS[name] + k + n]

        misc = dict(cb=mem.at("cb", [P, P], F32, AT_C + 2208), cb16=mem.at("cb16", [P, P], BF16, AT_C + 2720),
                    t8=mem.at("t8", [NS, DEC_T], F32, AT_C + 2976), cb8=mem.at("cb8", [NS, DEC_T], F32, AT_C + 3008),
                    b8=mem.at("b8", [NS, NS], F32, AT_C + 3040),
                    spread=mem.at("spread", [P, NS], F32, AT_C + 3296))
        bias = mem.at("bias", [P, 36 * P], BF16, AT_B)
        bias_s = mem.at("bias_s", [NS, PAST + DEC_T], BF16, AT_B + 9216)
        rep = mem.at("rep", [NS, DEC_B, NS], BF16, AT_B + 9216 + 4128)

        def dram(name, shape):
            return nc.dram_tensor(name, shape, F32, kind="Internal").ap()
        x_kept = dram("x_kept", (P, KT, NT))
        scratch = {name: dram(f"kept_{name}", (n, P, NT)) for name, n in
                   (("q", 4), ("k", 4), ("qm", 4), ("lx", 4), ("lg", 4), ("y", 4), ("g", 24))}

        with phase(nc) as sem:
            setup(nc, sem, mem, bank, x, ident, ones, ones_half, ident16, par, misc, I)

        def feed_forward(n):
            with phase(nc) as sem:
                with nc.Block() as block:
                    norm_stage(nc, block, sem, mem, bank, x, NT, CH, column(f"g_ffn{n}", 0, KT), ones,
                               h_hi, h_lo, f"_ffn{n}", AT_A)
                ffn(nc, sem, mem, bank, x, h_hi, h_lo, raw, w_hi, w_lo, I[f"w_ffn{n}_in"][0],
                    I[f"w_ffn{n}_out"][0], f"_ffn{n}")

        feed_forward(1)
        with phase(nc) as sem:
            kept = sem("kept")
            with nc.Block() as block:
                norm_stage(nc, block, sem, mem, bank, x, NT, CH, column("g_mix", 0, KT), ones,
                           h_hi, h_lo, "_mix", AT_A)

                @block.sync
                def _(sp):
                    sp.dma_start(x_kept, x[:, :, :]).then_inc(kept, 16)
                    sp.wait_ge(kept, 16)
        with phase(nc) as sem:
            mixing_inputs(nc, sem, mem, bank, h_hi, h_lo, raw, w_hi, w_lo, ident, I, O, scratch, bias, bias_s,
                          rep, misc)
        qT = mem.at("qT", [P, 4, NT], F32, AT_H)
        kT = mem.at("kT", [P, 4, NT], F32, AT_H + 4 * NT * 4)
        qmT = mem.at("qmT", [P, 4, NT], F32, AT_H + 8 * NT * 4)
        mkT = mem.at("mkT", [P, H_MEM, N_MEM], F32, AT_X)
        mv = mem.at("mv", [P, 2, 512], F32, AT_X + 4096)
        with phase(nc) as sem:
            recurrence(nc, sem, mem, bank, ident, column, I, O, scratch)
        with phase(nc) as sem:
            memory_keys(nc, sem, mem, bank, ident, ones, column, raw, w_hi, w_lo, mkT, mv, I, O)
        with phase(nc) as sem:
            head_norms(nc, sem, mem, bank, ident, ones, ones_half, column, qT, kT, qmT, O, scratch)
        with phase(nc) as sem:
            attention(nc, sem, mem, bank, bank_t, ident, ident16, qT, kT, qmT, mkT, mv, bias, bias_s, rep, I, O)
        with phase(nc) as sem:
            merge(nc, sem, mem, bank, x, raw, w_hi, w_lo, qT, qmT, x_kept, I, scratch)
        feed_forward(2)
        with phase(nc) as sem:
            results(nc, sem, mem, bank, x, ident, O)


def setup(nc, sem, mem, bank, x, ident, ones, ones_half, ident16, par, misc, I):
    xin = mem.at("xin", [P, 9, D], F32, AT_A)
    prow = mem.at("prow", [N_ROWS, P], F32, AT_A + 9 * D * 4)
    rows_loaded = sem("rows_loaded")
    x_loaded = [sem(f"x_loaded{t}") for t in range(9)]
    cleared = sem("cleared")
    zeroed = sem("zeroed")
    boxed = sem("boxed")
    cb, cb16, t8, cb8, b8 = misc["cb"], misc["cb16"], misc["t8"], misc["cb8"], misc["b8"]
    u8 = mem.at("u8", [NS, NS], F32, AT_A + 9 * D * 4 + 512)
    made = sem("made")
    turned = sem("turned")
    evicted = [sem("evicted_act"), sem("evicted_dve")]
    x_rows = I["x_prompt"][0].rearrange("(t p) d -> t p d", p=P)
    s_rows = I["x_sample"].rearrange("b t d -> (b t) d")
    params = [(ROWS[name], n, I[key][0].rearrange(how, c=P) if how else I[key]) for name, n, key, how in (
        ("g_ffn1", 8, "norm_ffn1_g", "(k c) -> k c"), ("g_mix", 8, "norm_mix_g", "(k c) -> k c"),
        ("g_ffn2", 8, "norm_ffn2_g", "(k c) -> k c"), ("g_mem", 8, "norm_mem_g", "(k c) -> k c"),
        ("conv_w", 16, "conv_w", "w (k c) -> (w k) c"), ("conv_b", 4, "conv_b", "(k c) -> k c"),
        ("ba", 4, "lru_ba", "(k c) -> k c"), ("bi", 4, "lru_bi", "(k c) -> k c"),
        ("lam", 4, "lru_lambda", "(k c) -> k c"), ("gmq", 1, "mem_q_norm_g", None),
        ("gmk", 1, "mem_k_norm_g", None), ("h0", 32, "state_h", "b (k c) -> (b k) c"))]
    jobs = [dict(src=[prow[:, :]], dst=par[:, :], psum=lambda b: b[:, 0:N_ROWS],
                 needs=[(made, 5), (rows_loaded, 16 * (len(params) + 4))])]
    for t, (t0, w) in enumerate(TT):
        for half in range(2):
            jobs.append(dict(
                src=[xin[0:w, t, (4 * half + q) * P:(4 * half + q + 1) * P] for q in range(4)],
                dst=x[:, 4 * half:4 * half + 4, t0:t0 + w],
                psum=lambda b, w=w: b[:, 0:4 * w].rearrange("p (q n) -> p q n", q=4),
                needs=[(x_loaded[t], 16)]))

    with nc.Block() as block:
        @block.sync
        def _(sp):
            for r, n, src in params:
                sp.dma_start(prow[r:r + n, :], src).then_inc(rows_loaded, 16)
            for name, key in (("gq", "q_norm_g"), ("gk", "k_norm_g")):
                for half in range(2):
                    sp.dma_start(prow[ROWS[name]:ROWS[name] + 1, half * DH:(half + 1) * DH],
                                 I[key]).then_inc(rows_loaded, 16)

        @block.gpsimd
        def _(pool):
            pool.memset(ident[:, :], 0.0).then_inc(cleared, 1)
            pool.memset(ident16[:, :], 0.0).then_inc(cleared, 1)
            pool.memset(ones[:, :], 1.0).then_inc(made, 1)
            pool.wait_ge(cleared, 2)
            for m in (ident, ident16):
                pool.affine_select(out=m[:, :], in_=m[:, :], compare_op=ALU.not_equal, fill=1.0, base=0,
                                   pattern=[[-1, P]], channel_multiplier=1).then_inc(made, 1)
            pool.memset(cb[:, :], 0.0).then_inc(cleared, 1)
            pool.memset(cb16[:, :], 0.0).then_inc(cleared, 1)
            pool.memset(b8[:, :], 1.0).then_inc(cleared, 1)
            pool.wait_ge(cleared, 5)
            for m, fill in ((cb, BARRED), (cb16, BIG)):
                pool.affine_select(out=m[:, :], in_=m[:, :], compare_op=ALU.is_ge, fill=fill, base=0,
                                   pattern=[[-1, P]], channel_multiplier=1)
            b8v = b8[:, :]
            pool.affine_select(out=b8v, in_=b8v, compare_op=ALU.is_ge, fill=0.0, base=0,
                               pattern=[[-8, DEC_B], [0, DEC_T]], channel_multiplier=1).then_inc(boxed, 1)
            pool.wait_ge(boxed, 1)
            pool.affine_select(out=b8v, in_=b8v, compare_op=ALU.is_ge, fill=0.0, base=7,
                               pattern=[[8, DEC_B], [0, DEC_T]], channel_multiplier=-1).then_inc(boxed, 1)
            pool.wait_ge(boxed, 2)
            pool.affine_select(out=u8[:, :], in_=b8v, compare_op=ALU.is_gt, fill=0.0, base=0,
                               pattern=[[1, NS]], channel_multiplier=-1).then_inc(boxed, 1)

        @block.tensor
        def _(pe):
            transposes_pe(pe, nc, jobs, ident, bank, None, evicted, turned)

        @block.scalar
        def _(act):
            for t, (t0, w) in enumerate(TT):
                act.dma_start(xin[0:w, t, :], x_rows[t] if t < 8 else s_rows).then_inc(x_loaded[t], 16)
            transposes_evict(act, act.copy, jobs, 0, bank, turned, evicted)

        @block.vector
        def _(dve):
            dve.memset(ones_half[:, :], 0.0).then_inc(zeroed, 1)
            dve.wait_ge(zeroed, 1)
            dve.memset(ones_half[0:DH, 0:DH], 1.0).then_inc(made, 1)
            dve.memset(ones_half[DH:P, DH:P], 1.0).then_inc(made, 1)
            dve.wait_ge(boxed, 3)
            dve.wait_ge(made, 5)
            dve.tensor_copy(misc["spread"][DH:DH + H, :].rearrange("p (h t) -> p h t", h=H),
                            ident[DH:DH + H, DH:DH + H].unsqueeze(2).to_broadcast([H, H, DEC_T]))
            dve.tensor_reduce(t8[:, :], ident[0:NS, 0:NS].rearrange("p (b t) -> p t b", b=DEC_B), AX.X, ALU.add)
            dve.tensor_reduce(cb8[:, :], u8[:, :].rearrange("p (b t) -> p t b", b=DEC_B), AX.X,
                              ALU.add).then_inc(zeroed, 1)
            dve.wait_ge(zeroed, 2)
            dve.tensor_scalar(cb8[:, :], cb8[:, :], BARRED, None, ALU.mult)
            transposes_evict(dve, dve.tensor_copy, jobs, 1, bank, turned, evicted)


def results(nc, sem, mem, bank, x, ident, O):
    rows = mem.at("rows", [P, 9, D], F32, AT_A)
    turned = sem("y_turned")
    evicted = [sem("y_evicted_act"), sem("y_evicted_dve")]
    written = sem("y_written")
    y_rows = O["y_prompt"][0].rearrange("(t p) d -> t p d", p=P)
    s_rows = O["y_sample"].rearrange("b t d -> (b t) d")
    jobs = [dict(src=[x[:, 4 * half + q, t0:t0 + w] for q in range(4)], step=P,
                 dst=rows[0:w, t, half * 512:(half + 1) * 512], psum=lambda b, w=w: b[0:w, :], needs=[])
            for t, (t0, w) in enumerate(TT) for half in range(2)]

    with nc.Block() as block:
        @block.tensor
        def _(pe):
            transposes_pe(pe, nc, jobs, ident, bank, None, evicted, turned)

        @block.scalar
        def _(act):
            transposes_evict(act, act.copy, jobs, 0, bank, turned, evicted)

        @block.vector
        def _(dve):
            transposes_evict(dve, dve.tensor_copy, jobs, 1, bank, turned, evicted)

        @block.sync
        def _(sp):
            for t, (t0, w) in enumerate(TT):
                sp.wait_ge(evicted[0], t + 1)
                sp.wait_ge(evicted[1], t + 1)
                sp.dma_start(y_rows[t] if t < 8 else s_rows, rows[0:w, t, :]).then_inc(written, 16)
            sp.wait_ge(written, 16 * len(TT))


class Indexer:

    def __init__(self):
        self.order = [7, 6, 5, 4, 3, 2, "S"]
        window = {7: (15, 25), 6: (26, 44), 5: (44, 60), 4: (60, 73), 3: (73, 83), 2: (83, 91)}
        self.jobs = []
        self.slots = {}
        self.of_block = {}
        for i in (7, 6, 5, 4, 3, 2):
            keys = (i + 1) * P
            mine = [(i, h, k0, min(512, keys - k0)) for h in range(H) for k0 in range(0, keys, 512)]
            a, b = window[i]
            self.of_block[i] = range(len(self.jobs), len(self.jobs) + len(mine))
            for n, job in enumerate(mine):
                self.slots.setdefault(a + n * (b - a) // len(mine), []).append(len(self.jobs))
                self.jobs.append(job)
        self.sample_first = 15
        self.sample_jobs = 4 * DEC_B

    def sample_step(self, q):
        s = q - self.sample_first
        return s // 2 if s >= 0 and s % 2 == 0 else -1 - self.sample_jobs


V_TILES = ((0, 4), (4, 8), (8, 9))


def bias_at(i):
    return i * (i + 1) // 2 * P


def mixing_inputs(nc, sem, mem, bank, h_hi, h_lo, raw, w_hi, w_lo, ident, I, O, scratch, bias, bias_s, rep, misc):
    w_in = I["w_in"][0].rearrange("(k p) n -> p k n", p=P)
    ix = Indexer()
    units = [("kw", 0, C_KI)] + [("qi", j, C_QI + j * P) for j in range(4)]
    for kind, col, n in (("lx", C_LX, 4), ("lg", C_LG, 4), ("q", C_Q, 4), ("k", C_K, 4), ("qm", C_QM, 4),
                         ("g", C_G, 24), ("v", C_V, 4)):
        units += [(kind, j, col + j * P) for j in range(n)]
    N = len(units)
    first_free = [n for n, (kind, _, _) in enumerate(units) if kind not in ("kw", "qi")][0]
    staged = [n for n in range(N) if n >= first_free]

    at = AT_X
    def place(name, shape, dt, size):
        nonlocal at
        t = mem.at(name, shape, dt, at)
        at += (size + 31) // 32 * 32
        assert at <= AT_B
        return t
    qi = place("qi", [P, 4, NT], F32, 4 * NT * 4)
    kw = place("kw", [P, NT], F32, NT * 4)
    ki2 = place("ki2", [P, NT], F32, NT * 4)
    kw_rows = place("kw_rows", [P, 9, DH + H], F32, 9 * (DH + H) * 4)
    stage = place("stage", [P, 2, 9 * P], F32, 2 * 9 * P * 4)
    S = place("S", [P, 2, SEQ], F32, 2 * SEQ * 4)
    S_s = place("S_s", [NS, PAST + DEC_T], F32, (PAST + DEC_T) * 4)
    relu = place("relu", [P, 4, 512], F32, 4 * 2048)
    relu_s = place("relu_s", [NS, 2, 512], F32, 2 * 2048)
    kx = place("kx", [P, 8, 4, DH], F32, 8 * 4 * DH * 4)
    kxT = place("kxT", [P, 2, 2, P], F32, 2 * 2 * P * 4)
    qi_s = place("qi_s", [P, 2, DEC_B, H, DEC_T], F32, 2 * DEC_B * NS * 4)
    wsel = place("wsel", [NS, DEC_B, NS], F32, DEC_B * NS * 4)
    qi_x = place("qi_x", [P, 4, NS], F32, 4 * NS * 4)
    top8 = place("top8", [P, 8], F32, 32)
    table = place("table", [1, DEC_B * PAGES], I32, DEC_B * PAGES * 4)
    cb, cb16, t8, cb8, b8 = misc["cb"], misc["cb16"], misc["t8"], misc["cb8"], misc["b8"]

    loaded = [sem(f"mix_loaded{i}") for i in range(3)]
    high, low = sem("mix_high"), sem("mix_low")
    ready = sem("mix_ready")
    evicted = sem("mix_evicted")
    stored = [sem(f"mix_stored{i}") for i in range(2)]
    kw_turned, kw_copied, kw_moved = sem("kw_turned"), sem("kw_copied"), sem("kw_moved")
    table_loaded = sem("table_loaded")
    kx_loaded = [sem(f"kx_loaded{i}") for i in range(8)]
    kx_turned, kx_copied = sem("kx_turned"), sem("kx_copied")
    sdots, srelu, ssum = sem("sdots"), sem("srelu"), sem("ssum")
    wsel_made = sem("wsel_made")
    v_turned, v_copied = sem("v_turned"), sem("v_copied")
    qi_placed = sem("qi_placed")
    weighed = sem("weighed")
    dots, relued, summed = sem("idx_dots"), sem("idx_relu"), sem("idx_sum")
    s_evicted = sem("s_evicted")
    sel = sem("selection")
    masked = sem("masked")

    def dst_of(n):
        kind, j, _ = units[n]
        s = (n - first_free) % 2
        if kind == "v":
            full = stage[:, s, :].rearrange("p (t c) -> p t c", c=P)
            vp = O["new_v_prompt"][0, 0].rearrange("(t p) h d -> p t (h d)", p=P)
            vs = O["new_v_sample"][0].rearrange("b t h d -> (b t) (h d)")
            return [(vp[:, :, j * P:(j + 1) * P], full[:, 0:8, :]),
                    (vs[:, j * P:(j + 1) * P], stage[0:NS, s, 8 * P:9 * P])]
        return [(scratch[kind][j], stage[:, s, 0:NT])]

    stores_before = []
    counts = [0, 0]
    for n in staged:
        s = (n - first_free) % 2
        stores_before.append(counts[s])
        counts[s] += len(dst_of(n))

    with nc.Block() as block:
        @block.sync
        def _(sp):
            def store(n):
                for dst, src in dst_of(n):
                    sp.dma_start(dst, src).then_inc(stored[(n - first_free) % 2], 16)

            for n in range(N + 3):
                if n < N:
                    if n >= 3:
                        sp.wait_ge(low, n - 2)
                    sp.dma_start(raw[:, n % 3, :].rearrange("p (k c) -> p k c", k=KT),
                                 w_in[:, :, units[n][2]:units[n][2] + P]).then_inc(loaded[n % 3], 16)
                if n == 5:
                    sp.wait_ge(evicted, 3)
                    sp.dma_start(ki2[DH:P, :], kw[0:DH, :]).then_inc(kw_moved, 16)
                    sp.wait_ge(kw_copied, 9)
                    sp.dma_start(O["new_kidx_prompt"][0, 0].rearrange("(t p) d -> p t d", p=P),
                                 kw_rows[:, 0:8, 0:DH]).then_inc(kw_moved, 16)
                    sp.dma_start(O["new_kidx_sample"][0].rearrange("b t d -> (b t) d"),
                                 kw_rows[0:NS, 8, 0:DH]).then_inc(kw_moved, 16)
                if n == 6:
                    sp.wait_ge(evicted, 15)
                    for half in range(2):
                        o = (1 - half) * DH
                        sp.dma_start(qi_x[half * DH:(half + 1) * DH, :, :], qi[o:o + DH, :, SEQ:NT]
                                     ).then_inc(kw_moved, 16)
                if n - 3 >= first_free:
                    kind, j, _ = units[n - 3]
                    if kind == "v":
                        sp.wait_ge(v_copied, 3 * (j + 1))
                    else:
                        sp.wait_ge(evicted, 3 * (n - 2))
                    store(n - 3)
            for s in range(2):
                sp.wait_ge(stored[s], 16 * counts[s])
            sp.wait_ge(kw_moved, 16 * (1 + 2 + 2))

        @block.gpsimd
        def _(pool):
            pool.dma_start(table[:, :], I["page_table"].rearrange("b g -> (b g)").rearrange(
                "(a n) -> a n", a=1)).then_inc(table_loaded, 16)

            def kidx_pages(job):
                c, b = divmod(job, DEC_B)
                if job >= 8:
                    pool.wait_ge(kx_turned, job - 7)
                for g in range(4):
                    at = b * PAGES + 4 * c + g
                    page = pool.value_load(table[0:1, at:at + 1], min_val=0,
                                         max_val=I["cache_kidx"].shape[1] - 1)
                    pool.dma_start(kx[:, job % 8, g, :],
                                 I["cache_kidx"][0][bass.ds(page, 1)].rearrange("a p d -> p (a d)")
                                 ).then_inc(kx_loaded[job % 8], 16)

            for n in range(N):
                pool.wait_ge(high, n + 1)
                pool.tensor_tensor(w_lo[:, n % 3, :], raw[:, n % 3, :], w_hi[:, n % 3, :].bitcast(F32),
                                   ALU.subtract).then_inc(low, 1)
                if n == 2:
                    pool.wait_ge(table_loaded, 16)
                if 2 <= n < 6:
                    for job in range(2 * (n - 2), 2 * (n - 1)):
                        kidx_pages(job)
                if 7 <= n:
                    for job in range(8 + 3 * (n - 7) // 2, min(8 + 3 * (n - 6) // 2, ix.sample_jobs)):
                        kidx_pages(job)

        @block.tensor
        def _(pe):
            def sample_turn(job):
                pe.wait_ge(kx_loaded[job % 8], 64 * (job // 8 + 1))
                if job == 0:
                    pe.wait_ge(wsel_made, DEC_B)
                else:
                    pe.wait_ge(kx_copied, job)
                for g in range(2):
                    mm = pe.transpose(bank[7][:, g * P:(g + 1) * P],
                                      kx[:, job % 8, 2 * g:2 * g + 2, :].rearrange("p g d -> p (g d)"), ident[:, :])
                mm.then_inc(kx_turned, 1)

            def sample_dots(job):
                b = job % DEC_B
                pe.wait_ge(kx_copied, job + 1)
                if job == 0:
                    pe.wait_ge(qi_placed, 2 * H)
                else:
                    pe.wait_ge(srelu, job)
                for g in range(4):
                    mm = pe.matmul(bank[6][0:NS, g * P:(g + 1) * P],
                                   qi_s[:, g % 2, b, :, :].rearrange("p h t -> p (h t)"),
                                   kxT[:, job % 2, g // 2, :], start=True, stop=True)
                mm.then_inc(sdots, 1)

            def sample_sum(job):
                c, b = divmod(job, DEC_B)
                pe.wait_ge(srelu, job + 1)
                if job == 0:
                    pe.wait_ge(wsel_made, DEC_B)
                elif b == 0:
                    pe.wait_ge(s_evicted, c)
                pe.matmul(bank[5][0:NS, :], wsel[:, b, :], relu_s[:, job % 2, :], start=(b == 0),
                          stop=(b == DEC_B - 1)).then_inc(ssum, 1)

            def new_dots():
                pe.wait_ge(srelu, ix.sample_jobs)
                for b in range(DEC_B):
                    mm = pe.matmul(bank[6][0:NS, 8 * b:8 * b + 8], qi_s[0:DH, 0, b, :, :].rearrange("p h t -> p (h t)"),
                                   kw[0:DH, SEQ + 8 * b:SEQ + 8 * b + 8], start=True, stop=True)
                mm.then_inc(sdots, 1)

            def new_sum():
                pe.wait_ge(srelu, ix.sample_jobs + 1)
                pe.wait_ge(s_evicted, 4)
                for b in range(DEC_B):
                    mm = pe.matmul(bank[5][0:NS, 0:DEC_T], wsel[:, b, :], relu_s[:, 0, 8 * b:8 * b + 8],
                                   start=(b == 0), stop=(b == DEC_B - 1))
                mm.then_inc(ssum, 1)

            def prompt_dots(m):
                i, h, k0, w = ix.jobs[m]
                r = (h % 2) * DH
                if m >= 2:
                    pe.wait_ge(relued, m - 1)
                if m == 0:
                    pe.wait_ge(kw_moved, 16 * (1 + 2 + 2))
                keys = (kw if r == 0 else ki2)[r:r + DH, k0:k0 + w]
                pe.matmul(bank[3 + m % 2][:, 0:w], qi[r:r + DH, h // 2, i * P:(i + 1) * P], keys,
                          start=True, stop=True).then_inc(dots, 1)

            def turn_v(n):
                j = units[n][1]
                pe.wait_ge(evicted, 3 * (n + 1))
                if j == 0:
                    pe.wait_ge(relued, len(ix.jobs))
                    pe.wait_ge(s_evicted, 5)
                else:
                    pe.wait_ge(v_copied, 3 * j)
                for g, (a, b) in enumerate(V_TILES):
                    for t in range(a, b):
                        t0, w = TT[t]
                        mm = pe.transpose(bank[3 + g][0:w, (t - a) * P:(t - a + 1) * P], qi[:, j, t0:t0 + w],
                                          ident[:, :])
                    mm.then_inc(v_turned, 1)

            for n, (kind, j, _) in enumerate(units):
                pe.wait_ge(low, n + 1)
                hi = lambda k, n=n: w_hi[:, n % 3, k * P:(k + 1) * P]
                lo = lambda k, n=n: w_lo[:, n % 3, k * P:(k + 1) * P]
                for c, (t0, w) in enumerate(CH):
                    q = 3 * n + c
                    if q >= 3:
                        pe.wait_ge(evicted, q - 2)
                    ks = [(k, k) for k in range(KT)]
                    mm = products(pe, bank[c][:, 0:w], hi, lo, lambda k: h_hi[:, k, t0:t0 + w],
                                  lambda k: h_lo[:, k, t0:t0 + w], ks, True, True)
                    mm.then_inc(ready, 1)
                    if n == 1 and c == 0:
                        pe.wait_ge(evicted, 3)
                        for t, (a, rows) in enumerate(TT):
                            if t % 2 == 0 and t >= 4:
                                pe.wait_ge(kw_copied, t - 2)
                            pe.transpose(bank[3 + t % 4][0:rows, 0:P], kw[:, a:a + rows],
                                         ident[:, :]).then_inc(kw_turned, 1)
                        pe.matmul(bank[7][0:NS, 0:NS], misc["spread"][DH:DH + H, :], kw[DH:DH + H, SEQ:NT], start=True, stop=True).then_inc(kw_turned, 1)
                    s = ix.sample_step(q)
                    if 0 <= s - 2 < ix.sample_jobs:
                        sample_sum(s - 2)
                    if s - 2 == ix.sample_jobs:
                        new_sum()
                    if 0 <= s - 1 < ix.sample_jobs:
                        sample_dots(s - 1)
                    if s - 1 == ix.sample_jobs:
                        new_dots()
                    if 0 <= s < ix.sample_jobs:
                        sample_turn(s)
                    for m in ix.slots.get(q, []):
                        prompt_dots(m)
                    if c == 0 and n >= 1 and units[n - 1][0] == "v":
                        turn_v(n - 1)
            turn_v(N - 1)

        @block.scalar
        def _(act):
            def high_part(n):
                act.wait_ge(loaded[n % 3], 16 * (n // 3 + 1))
                if n >= 3:
                    act.wait_ge(ready, 3 * (n - 2))
                act.copy(w_hi[:, n % 3, :], raw[:, n % 3, :]).then_inc(high, 1)

            def v_rows(n):
                j, m = units[n][1], n - first_free
                act.wait_ge(stored[m % 2], 16 * stores_before[m])
                for g, (a, b) in enumerate(V_TILES):
                    rows = P if b <= 8 else NS
                    act.wait_ge(v_turned, 3 * j + g + 1)
                    act.copy(stage[0:rows, m % 2, a * P:b * P], bank[3 + g][0:rows, 0:(b - a) * P]
                             ).then_inc(v_copied, 1)

            high_part(0)
            high_part(1)
            for n, (kind, j, _) in enumerate(units):
                if n + 2 < N:
                    high_part(n + 2)
                for c, (t0, w) in enumerate(CH):
                    q = 3 * n + c
                    act.wait_ge(ready, q + 1)
                    if kind == "kw":
                        dst, src, f = kw[:, t0:t0 + w], bank[c][:, 0:w], ACT.Copy
                    elif kind in ("qi", "v"):
                        dst, src, f = qi[:, j, t0:t0 + w], bank[c][:, 0:w], ACT.Copy
                    else:
                        m = n - first_free
                        if c == 0 and m >= 2:
                            act.wait_ge(stored[m % 2], 16 * (stores_before[m]))
                        f = {"g": ACT.Sigmoid, "lg": ACT.Gelu_apprx_tanh}.get(kind, ACT.Copy)
                        dst, src = stage[:, m % 2, t0:t0 + w], bank[c][:, 0:w]
                    if f == ACT.Copy:
                        act.copy(dst, src).then_inc(evicted, 1)
                    else:
                        act.activation(dst, src, f).then_inc(evicted, 1)
                    if n == 1 and c == 0:
                        for t, (a, rows) in enumerate(TT):
                            act.wait_ge(kw_turned, t + 1)
                            act.copy(kw_rows[0:rows, t, :], bank[3 + t % 4][0:rows, 0:DH + H]).then_inc(kw_copied, 1)
                    s = ix.sample_step(q)
                    if 0 <= s - 1 < ix.sample_jobs + 1:
                        job = s - 1
                        act.wait_ge(sdots, job + 1)
                        if job >= 2:
                            act.wait_ge(ssum, job - 1)
                        w2 = 512 if job < ix.sample_jobs else NS
                        act.activation(relu_s[:, job % 2, 0:w2], bank[6][0:NS, 0:w2], ACT.Relu).then_inc(srelu, 1)
                    if 0 <= s - 2 <= ix.sample_jobs and (s - 2) % DEC_B == DEC_B - 1 or s - 2 == ix.sample_jobs:
                        c4 = (s - 2) // DEC_B
                        w4 = 512 if c4 < 4 else DEC_T
                        act.wait_ge(ssum, s - 1)
                        act.copy(S_s[:, c4 * 512:c4 * 512 + w4], bank[5][0:NS, 0:w4]).then_inc(s_evicted, 1)
                    if 0 <= s < ix.sample_jobs:
                        act.wait_ge(kx_turned, s + 1)
                        if s >= 2:
                            act.wait_ge(sdots, s - 1)
                        act.copy(kxT[:, s % 2, :, :].rearrange("p g n -> p (g n)"),
                                 bank[7][:, 0:2 * P]).then_inc(kx_copied, 1)
                    for m in ix.slots.get(q, []):
                        w2 = ix.jobs[m][3]
                        act.wait_ge(dots, m + 1)
                        if m >= 4:
                            act.wait_ge(summed, m - 3)
                        act.activation(relu[:, m % 4, 0:w2], bank[3 + m % 2][:, 0:w2], ACT.Relu).then_inc(relued, 1)
                    if c == 0 and n >= 1 and units[n - 1][0] == "v":
                        v_rows(n - 1)
            v_rows(N - 1)

        @block.vector
        def _(dve):
            steps = [0]

            def after(ins):
                ins.then_inc(sel, 1)
                steps[0] += 1

            scale = H ** -0.5 * DH ** -0.5
            dve.memset(qi_s[:, :, :, :, :], 0.0).then_inc(weighed, 1)
            dve.memset(wsel[:, :, :], 0.0).then_inc(weighed, 1)
            dve.wait_ge(kw_copied, 9)
            dve.tensor_scalar(kw_rows[:, 0:8, DH:DH + H], kw_rows[:, 0:8, DH:DH + H], scale, None,
                              ALU.mult).then_inc(weighed, 1)
            dve.wait_ge(kw_turned, 10)
            dve.wait_ge(weighed, 3)
            for b in range(DEC_B):
                dve.scalar_tensor_tensor(wsel[:, b, 8 * b:8 * b + 8], bank[7][0:NS, 8 * b:8 * b + 8], scale,
                                         t8[:, :], ALU.mult, ALU.mult).then_inc(wsel_made, 1)
            for i in range(2):
                if i:
                    dve.memset(bias[:, bias_at(i):bias_at(i) + i * P], 0.0)
                dve.tensor_copy(bias[:, bias_at(i) + i * P:bias_at(i + 1)], cb16[:, :])

            dve.wait_ge(evicted, 15)
            dve.wait_ge(kw_moved, 16 * (1 + 2 + 2))
            dve.wait_ge(weighed, 2)
            for h in range(H):
                for half in range(2):
                    rows = slice(half * DH, (half + 1) * DH)
                    src = qi[rows, h // 2, SEQ:NT] if h % 2 == half else qi_x[rows, h // 2, :]
                    dve.tensor_copy(qi_s[half * DH:(half + 1) * DH, half, :, h, :],
                                    src.rearrange("p (b t) -> p b t", b=DEC_B)).then_inc(qi_placed, 1)

            def add_head(i, m):
                _, h, k0, w = ix.jobs[m]
                dst = S[:, i % 2, k0:k0 + w]
                weight = kw_rows[:, i, DH + h:DH + h + 1]
                dve.wait_ge(relued, m + 1)
                if h == 0:
                    ins = dve.tensor_scalar(dst, relu[:, m % 4, 0:w], weight, None, ALU.mult)
                else:
                    dve.wait_ge(summed, m - (ix.of_block[i][-1] + 1 - ix.of_block[i][0]) // H + 1)
                    ins = dve.scalar_tensor_tensor(dst, relu[:, m % 4, 0:w], weight, dst, ALU.mult, ALU.add)
                ins.then_inc(summed, 1)

            def bar(i):
                dve.wait_ge(summed, ix.of_block[i][-1] + 1)
                d = S[:, i % 2, i * P:(i + 1) * P]
                after(dve.tensor_tensor(d, d, cb[:, :], ALU.add))

            def sample_bar():
                dve.wait_ge(s_evicted, 5)
                new = S_s[:, PAST:PAST + DEC_T]
                after(dve.tensor_tensor(new, new, cb8[:, :], ALU.add))

            def add_jobs(p):
                if p == "S":
                    return [(sample_bar, ())]
                return [(add_head, (p, m)) for m in ix.of_block[p]] + [(bar, (p,))]

            for f, args in add_jobs(ix.order[0]):
                f(*args)
            for n, p in enumerate(ix.order):
                scores = S_s[:, :] if p == "S" else S[:, p % 2, 0:(p + 1) * P]
                rows = NS if p == "S" else P
                following = add_jobs(ix.order[n + 1]) if n + 1 < len(ix.order) else []
                rounds = TOPK // 8
                for r in range(rounds):
                    if steps[0]:
                        dve.wait_ge(sel, steps[0])
                    after(dve.max(top8[0:rows, :], scores))
                    dve.wait_ge(sel, steps[0])
                    after(dve.match_replace(scores, top8[0:rows, :], scores, TAKEN))
                    for f, args in following[len(following) * r // rounds:len(following) * (r + 1) // rounds]:
                        f(*args)
                dve.wait_ge(sel, steps[0])
                dst = bias_s[:, :] if p == "S" else bias[:, bias_at(p):bias_at(p + 1)]
                after(dve.tensor_scalar(dst, scores, BARRED * 1.25, BIG, ALU.is_gt, ALU.mult))
            for b in range(DEC_B):
                dve.tensor_scalar(rep[:, b, :].rearrange("p (h t) -> p h t", h=H),
                                  t8[:, :].unsqueeze(1).to_broadcast([NS, H, DEC_T]), b8[:, 8 * b:8 * b + 1], None,
                                  ALU.mult)
            dve.wait_ge(sel, steps[0])


def head_norms(nc, sem, mem, bank, ident, ones, ones_half, column, qT, kT, qmT, O, scratch):
    sq = mem.at("hsq", [P, 2, NT], F32, AT_X + 8192)
    rs = mem.at("hrs", [P, 2, NT], F32, AT_X + 8192 + 2 * NT * 4)
    rows = mem.at("k_rows", [P, 2, 9, P], F32, AT_X + 8192 + 4 * NT * 4)
    gains = mem.at("gains", [P, 4], F32, AT_X + 8192 + 4 * NT * 4 + 2 * 9 * P * 4)
    tiles = [("k", j) for j in range(4)] + [("q", j) for j in range(4)] + [("qm", j) for j in range(4)]
    place = {"k": kT, "q": qT, "qm": qmT}
    loaded = [sem(f"head_loaded{n}") for n in range(len(tiles))]
    set_up, squared, summed = sem("head_set"), sem("head_squared"), sem("head_summed")
    rooted, inverted, normed = sem("head_rooted"), sem("head_inverted"), sem("head_normed")
    turned, evicted = sem("k_turned"), sem("k_evicted")
    stored = [sem("k_stored0"), sem("k_stored1")]

    with nc.Block() as block:
        @block.sync
        def _(sp):
            for n, (kind, j) in enumerate(tiles):
                sp.dma_start(place[kind][:, j, :], scratch[kind][j]).then_inc(loaded[n], 16)
            kp = O["new_k_prompt"][0, 0].rearrange("(t p) h d -> p t (h d)", p=P)
            ks = O["new_k_sample"][0].rearrange("b t h d -> (b t) (h d)")
            for j in range(4):
                sp.wait_ge(evicted, 3 * (j + 1))
                sp.dma_start(kp[:, :, j * P:(j + 1) * P], rows[:, j % 2, 0:8, :]).then_inc(stored[j % 2], 16)
                sp.dma_start(ks[:, j * P:(j + 1) * P], rows[0:NS, j % 2, 8, :]).then_inc(stored[j % 2], 16)
            for s in range(2):
                sp.wait_ge(stored[s], 64)

        @block.scalar
        def _(act):
            def k_out(act, j):
                if j >= 2:
                    act.wait_ge(stored[j % 2], 32)
                for g, (a, b) in enumerate(((0, 4), (4, 8), (8, 9))):
                    act.wait_ge(turned, 3 * j + g + 1)
                    r = P if g < 2 else NS
                    act.copy(rows[0:r, j % 2, a:b, :], bank[6 + (3 * j + g) % 2][0:r, 0:(b - a) * P].rearrange(
                        "p (t c) -> p t c", c=P)).then_inc(evicted, 1)

            def root(n):
                kind = tiles[n][0]
                act.wait_ge(set_up, 1)
                if n >= 2:
                    act.wait_ge(normed, n - 1)
                for c, (t0, w) in enumerate(CH):
                    act.wait_ge(summed, 3 * n + c + 1)
                    act.activation(rs[:, n % 2, t0:t0 + w], bank[3 * (n % 2) + c][:, 0:w], ACT.Sqrt,
                                   bias=gains[:, 3:4], scale=1.0 / (P if kind == "qm" else DH)).then_inc(rooted, 1)
            for n, (kind, j) in enumerate(tiles):
                act.wait_ge(loaded[n], 16)
                if n >= 2:
                    act.wait_ge(summed, 3 * (n - 1))
                act.activation(sq[:, n % 2, :], place[kind][:, j, :], ACT.Square).then_inc(squared, 1)
                if n >= 1:
                    root(n - 1)
                if 2 <= n < 6:
                    k_out(act, n - 2)
            root(len(tiles) - 1)

        @block.tensor
        def _(pe):
            for n, (kind, j) in enumerate(tiles):
                pe.wait_ge(squared, n + 1)
                for c, (t0, w) in enumerate(CH):
                    if n >= 2:
                        pe.wait_ge(rooted, 3 * (n - 2) + c + 1)
                    pe.matmul(bank[3 * (n % 2) + c][:, 0:w], (ones if kind == "qm" else ones_half)[:, :],
                              sq[:, n % 2, t0:t0 + w], start=True, stop=True).then_inc(summed, 1)
                if 2 <= n < 6:
                    m = n - 2
                    pe.wait_ge(normed, m + 1)
                    for g, (a, b) in enumerate(((0, 4), (4, 8), (8, 9))):
                        if 3 * m + g >= 2:
                            pe.wait_ge(evicted, 3 * m + g - 1)
                        for t in range(a, b):
                            t0, w = TT[t]
                            mm = pe.transpose(bank[6 + (3 * m + g) % 2][0:w, (t - a) * P:(t - a + 1) * P],
                                              kT[:, m, t0:t0 + w], ident[:, :])
                        mm.then_inc(turned, 1)

        @block.vector
        def _(dve):
            dve.memset(gains[:, 3:4], EPS).then_inc(set_up, 1)
            dve.tensor_scalar(gains[:, 0:1], column("gq"), DH ** -0.5, None, ALU.mult).then_inc(set_up, 1)
            dve.tensor_scalar(gains[:, 1:2], column("gmq"), P ** -0.5, None, ALU.mult).then_inc(set_up, 1)
            dve.wait_ge(set_up, 3)
            for n, (kind, j) in enumerate(tiles):
                gain = {"k": column("gk"), "q": gains[:, 0:1], "qm": gains[:, 1:2]}[kind]
                dve.wait_ge(rooted, 3 * (n + 1))
                dve.reciprocal(rs[:, n % 2, :], rs[:, n % 2, :]).then_inc(inverted, 1)
                dve.wait_ge(inverted, n + 1)
                t = place[kind][:, j, :]
                dve.scalar_tensor_tensor(t, t, gain, rs[:, n % 2, :], ALU.mult, ALU.mult).then_inc(normed, 1)


def recurrence(nc, sem, mem, bank, ident, column, I, O, scratch):
    at = AT_A
    def place(name, shape, size):
        nonlocal at
        t = mem.at(name, shape, F32, at)
        at += (size + 31) // 32 * 32
        assert at <= AT_B
        return t
    XP = 3 + SEQ
    xp = place("xp", [P, 2, XP], 2 * XP * 4)
    xs = place("xs", [P, 2, DEC_B, 3 + DEC_T], 2 * 88 * 4)
    conv = place("conv", [P, NT], NT * 4)
    r = place("r", [P, NT], NT * 4)
    ig = place("ig", [P, NT], NT * 4)
    a = place("a", [P, NT], NT * 4)
    th = place("th", [P, NT], NT * 4)
    hh = place("hh", [P, NT], NT * 4)
    gl = place("gl", [P, 2, NT], 2 * NT * 4)
    wab = place("wab", [P, 2, 4, P], 8 * P * 4)
    at = AT_X + 8192
    state = place("state", [24, LRU_W], LRU_W * 4)
    tail = place("tail", [P, LT, 36], LT * 36 * 4)
    tails = place("tails", [36, LRU_W], LRU_W * 4)
    sp4 = place("sp4", [P, 8, LT], 8 * LT * 4)
    x_in = [sem("lx_in0"), sem("lx_in1")]
    w_in, w_zero = sem("lru_w_in"), sem("lru_w_zero")
    state_in, state_turned, state_out = sem("state_in"), sem("state_turned"), sem("state_out")
    lam1, lam = sem("lam_exp"), sem("lam")
    step = sem("lru_step")
    conv_done, gates, gated, powers, rooted, y_done, y_out = (sem("conv_done"), sem("lru_gates"), sem("lru_gated"),
                                                              sem("lru_powers"), sem("lru_rooted"), sem("y_done"),
                                                              sem("y_out"))
    squares = sem("lru_squares")
    tail_turned, tail_copied, tail_out = sem("tail_turned"), sem("tail_copied"), sem("tail_out")

    with nc.Block() as block:
        @block.sync
        def _(sp):
            sp.wait_ge(w_zero, 1)
            for g, name in enumerate(("lru_wa", "lru_wi")):
                w = I[name][0].rearrange("(j e) i o -> e i j o", e=2)
                for e in range(2):
                    sp.dma_start(wab[e * DH:(e + 1) * DH, g, :, e * DH:(e + 1) * DH], w[e]).then_inc(w_in, 16)
            sp.dma_start(state[:, :], I["state_conv"][0].rearrange("b s c -> (b s) c")).then_inc(state_in, 16)
            for j in range(LT):
                if j >= 2:
                    sp.wait_ge(y_done, j - 1)
                sp.dma_start(xp[:, j % 2, 3:XP], scratch["lx"][j][:, 0:SEQ]).then_inc(x_in[j % 2], 16)
                sp.dma_start(xs[:, j % 2, :, 3:3 + DEC_T], scratch["lx"][j][:, SEQ:NT].rearrange(
                    "p (b t) -> p b t", b=DEC_B)).then_inc(x_in[j % 2], 16)
                sp.dma_start(gl[:, j % 2, :], scratch["lg"][j]).then_inc(x_in[j % 2], 16)
                if j >= 1:
                    sp.wait_ge(y_done, j)
                    sp.dma_start(scratch["y"][j - 1], hh[:, :]).then_inc(y_out, 16)
            sp.wait_ge(y_done, LT)
            sp.dma_start(scratch["y"][LT - 1], hh[:, :]).then_inc(y_out, 16)
            sp.wait_ge(tail_copied, 1)
            sp.dma_start(O["new_conv_prompt"][0, 0], tails[0:3, :]).then_inc(tail_out, 16)
            sp.dma_start(O["new_conv_sample"][0].rearrange("b s c -> (b s) c"), tails[3:27, :]).then_inc(tail_out, 16)
            sp.dma_start(O["new_h_prompt"][0], tails[27:28, :]).then_inc(tail_out, 16)
            sp.dma_start(O["new_h_sample"][0], tails[28:36, :]).then_inc(tail_out, 16)
            sp.wait_ge(tail_out, 64)
            sp.wait_ge(y_out, 16 * LT)

        @block.tensor
        def _(pe):
            pe.wait_ge(state_in, 16)
            for j in range(LT):
                mm = pe.transpose(bank[7][:, j * 24:(j + 1) * 24], state[:, j * P:(j + 1) * P], ident[0:24, 0:24])
            mm.then_inc(state_turned, 1)
            pe.wait_ge(w_in, 64)
            for j in range(LT):
                pe.wait_ge(conv_done, j + 1)
                if j >= 1:
                    pe.wait_ge(gated, 6 * j)
                for g in range(2):
                    for c, (t0, w) in enumerate(CH):
                        pe.matmul(bank[3 * g + c][:, 0:w], wab[:, g, j, :], conv[:, t0:t0 + w], start=True,
                                  stop=True).then_inc(gates, 1)
            pe.wait_ge(y_done, LT)
            for j in range(LT):
                mm = pe.transpose(bank[6][0:36, j * P:(j + 1) * P], tail[:, j, :], ident[:, :])
            mm.then_inc(tail_turned, 1)

        @block.scalar
        def _(act):
            act.wait_ge(lam, 1)
            act.activation(sp4[:, 1, :], sp4[:, 0, :], ACT.Exp, scale=-1.0).then_inc(lam1, 1)
            for j in range(LT):
                if j >= 1:
                    act.wait_ge(y_done, j)
                for g, (dst, b) in enumerate(((r, "ba"), (ig, "bi"))):
                    for c, (t0, w) in enumerate(CH):
                        act.wait_ge(gates, 6 * j + 3 * g + c + 1)
                        act.activation(dst[:, t0:t0 + w], bank[3 * g + c][:, 0:w], ACT.Sigmoid,
                                       bias=column(b, j)).then_inc(gated, 1)
                act.wait_ge(lam, 2)
                act.wait_ge(gated, 6 * j + 6)
                act.activation(a[:, :], r[:, :], ACT.Exp, scale=sp4[:, 7, j:j + 1]).then_inc(powers, 1)
                act.activation(th[:, :], r[:, :], ACT.Tanh, scale=sp4[:, 6, j:j + 1]).then_inc(powers, 1)
                act.wait_ge(squares, j + 1)
                act.activation(th[:, :], th[:, :], ACT.Sqrt).then_inc(rooted, 1)
            act.wait_ge(tail_turned, 1)
            act.copy(tails[:, :], bank[6][0:36, :]).then_inc(tail_copied, 1)

        @block.vector
        def _(dve):
            n = [0]

            def then(ins):
                n[0] += 1
                ins.then_inc(step, 1)
                dve.wait_ge(step, n[0])

            dve.memset(wab[:, :, :, :], 0.0).then_inc(w_zero, 1)
            lamb = column("lam", 0, LT)
            then(dve.tensor_scalar(sp4[:, 2, :], lamb, -1.0, None, ALU.mult))
            dve.tensor_tensor(sp4[:, 0, :], sp4[:, 2, :], lamb, ALU.max).then_inc(lam, 1)
            then(dve.tensor_scalar(sp4[:, 2, :], sp4[:, 2, :], 0.0, None, ALU.max))
            dve.wait_ge(lam1, 1)
            then(dve.tensor_scalar(sp4[:, 3, :], sp4[:, 1, :], 2.0, None, ALU.add))
            then(dve.reciprocal(sp4[:, 3, :], sp4[:, 3, :]))
            then(dve.tensor_tensor(sp4[:, 3, :], sp4[:, 3, :], sp4[:, 1, :], ALU.mult))
            then(dve.tensor_tensor(sp4[:, 4, :], sp4[:, 3, :], sp4[:, 3, :], ALU.mult))
            then(dve.tensor_scalar(sp4[:, 5, :], sp4[:, 4, :], 1.0 / 17, 1.0 / 15, ALU.mult, ALU.add))
            for k in (13, 11, 9, 7, 5, 3, 1):
                then(dve.tensor_tensor(sp4[:, 5, :], sp4[:, 5, :], sp4[:, 4, :], ALU.mult))
                then(dve.tensor_scalar(sp4[:, 5, :], sp4[:, 5, :], 1.0 / k, None, ALU.add))
            then(dve.tensor_tensor(sp4[:, 5, :], sp4[:, 5, :], sp4[:, 3, :], ALU.mult))
            then(dve.scalar_tensor_tensor(sp4[:, 5, :], sp4[:, 5, :], 2.0, sp4[:, 2, :], ALU.mult, ALU.add))
            then(dve.tensor_scalar(sp4[:, 6, :], sp4[:, 5, :], 8.0, None, ALU.mult))
            dve.tensor_scalar(sp4[:, 7, :], sp4[:, 5, :], -8.0, None, ALU.mult).then_inc(lam, 1)

            for s in range(2):
                dve.memset(xp[:, s, 0:3], 0.0)
            dve.wait_ge(state_turned, 1)
            for j in range(LT):
                s = j % 2
                then(dve.tensor_copy(xs[:, s, :, 0:3], bank[7][:, j * 24:(j + 1) * 24].rearrange(
                    "p (b s) -> p b s", b=DEC_B)))
                dve.wait_ge(x_in[s], 48 * (j // 2 + 1))
                cs = conv[:, SEQ:NT].rearrange("p (b t) -> p b t", b=DEC_B)
                for k in range(4):
                    w = column("conv_w", 4 * k + j)
                    src = ((conv[:, 0:SEQ], xp[:, s, k:k + SEQ]), (cs, xs[:, s, :, k:k + DEC_T]))
                    for part, (dst, x) in enumerate(src):
                        if k == 0:
                            ins = dve.tensor_scalar(dst, x, w, column("conv_b", j), ALU.mult, ALU.add)
                        else:
                            ins = dve.scalar_tensor_tensor(dst, x, w, dst, ALU.mult, ALU.add)
                        if k == 3 and part == 1:
                            ins.then_inc(conv_done, 1)
                        elif part == 0:
                            n[0] += 1
                            ins.then_inc(step, 1)
                        else:
                            then(ins)
                dve.tensor_copy(tail[:, j, 0:3], xp[:, s, SEQ:XP])
                dve.tensor_copy(tail[:, j, 3:27].rearrange("p (b s) -> p b s", b=DEC_B), xs[:, s, :, DEC_T:DEC_T + 3])
                dve.wait_ge(gated, 6 * j + 6)
                dve.wait_ge(conv_done, j + 1)
                then(dve.tensor_tensor(ig[:, :], ig[:, :], conv[:, :], ALU.mult))
                dve.wait_ge(powers, 2 * j + 2)
                then(dve.tensor_tensor(r[:, :], a[:, :], a[:, :], ALU.mult))
                dve.scalar_tensor_tensor(th[:, :], r[:, :], 1.0, th[:, :], ALU.add, ALU.mult).then_inc(squares, 1)
                dve.wait_ge(rooted, j + 1)
                then(dve.tensor_tensor(ig[:, :], ig[:, :], th[:, :], ALU.mult))
                a0 = a[:, SEQ:NT].rearrange("p (b t) -> p b t", b=DEC_B)[:, :, 0]
                b0 = ig[:, SEQ:NT].rearrange("p (b t) -> p b t", b=DEC_B)[:, :, 0]
                h0 = par_columns(column("h0", 0, 32), j)
                then(dve.tensor_tensor(conv[:, 0:DEC_B], a0, h0, ALU.mult))
                then(dve.tensor_tensor(b0, b0, conv[:, 0:DEC_B], ALU.add))
                then(dve.memset(a0, 0.0))
                if j >= 1:
                    dve.wait_ge(y_out, 16 * j)
                dve.tensor_tensor_scan(hh[:, 0:SEQ], a[:, 0:SEQ], ig[:, 0:SEQ], 0.0, ALU.mult, ALU.add)
                then(dve.tensor_tensor_scan(hh[:, SEQ:NT], a[:, SEQ:NT], ig[:, SEQ:NT], 0.0, ALU.mult, ALU.add))
                dve.tensor_copy(tail[:, j, 27:28], hh[:, SEQ - 1:SEQ])
                then(dve.tensor_copy(tail[:, j, 28:36], hh[:, SEQ:NT].rearrange("p (b t) -> p b t", b=DEC_B)[
                    :, :, DEC_T - 1]))
                dve.tensor_tensor(hh[:, :], hh[:, :], gl[:, s, :], ALU.mult).then_inc(y_done, 1)
                dve.wait_ge(y_done, j + 1)


def par_columns(cols, j):
    return cols.rearrange("p (b k) -> p b k", k=LT)[:, :, j]


def memory_keys(nc, sem, mem, bank, ident, ones, column, raw, w_hi, w_lo, mkT, mv, I, O):
    at = AT_X + 16384
    m_in = mem.at("m_in", [P, 2, D], F32, at)
    mT = mem.at("mT", [P, KT, N_MEM], F32, at + 8192)
    m_hi = mem.at("m_hi", [P, KT, N_MEM], F32R, at + 16384)
    m_lo = mem.at("m_lo", [P, KT, N_MEM], F32R, at + 24576)
    sq = mem.at("mk_sq", [P, 4, N_MEM], F32, at)
    rs = mem.at("mk_rs", [P, 4, N_MEM], F32, at + 4096)
    rows = mem.at("mk_rows", [P, 2, 512], F32, at + 8192)
    eps = mem.at("mk_eps", [P, 1], F32, at + 12288)
    m_loaded, turned = sem("m_loaded"), sem("m_turned")
    evicted = [sem("m_evicted0"), sem("m_evicted1")]
    jobs = [dict(src=[m_in[:, t, (4 * half + q) * P:(4 * half + q + 1) * P] for q in range(4)],
                 dst=mT[:, 4 * half:4 * half + 4, t * P:(t + 1) * P],
                 psum=lambda b: b.rearrange("p (q n) -> p q n", q=4), needs=[(m_loaded, 16)])
            for t in range(2) for half in range(2)]
    with nc.Block() as block:
        @block.sync
        def _(sp):
            sp.dma_start(m_in[:, :, :], I["mem_prompt"][0].rearrange("(t p) d -> p t d", p=P)).then_inc(m_loaded, 16)

        @block.tensor
        def _(pe):
            transposes_pe(pe, nc, jobs, ident, bank, None, evicted, turned)

        @block.scalar
        def _(act):
            transposes_evict(act, act.copy, jobs, 0, bank, turned, evicted)

        @block.vector
        def _(dve):
            transposes_evict(dve, dve.tensor_copy, jobs, 1, bank, turned, evicted)

    with nc.Block() as block:
        norm_stage(nc, block, sem, mem, bank, mT, N_MEM, [(0, N_MEM)], column("g_mem", 0, KT), ones, m_hi, m_lo,
                   "_mem", at + 32768)

    w = I["w_mem_kv"][0].rearrange("(k p) n -> p k n", p=P)
    loaded = [sem(f"mkv_loaded{i}") for i in range(3)]
    high, low, ready, copied = sem("mkv_high"), sem("mkv_low"), sem("mkv_ready"), sem("mkv_copied")
    eps_set, squared, summed, rooted = sem("mkv_eps"), sem("mkv_squared"), sem("mkv_summed"), sem("mkv_rooted")
    inverted, normed, k_turned, k_copied, out = (sem("mkv_inverted"), sem("mkv_normed"), sem("mk_turned"),
                                                 sem("mk_copied"), sem("mkv_out"))
    N = 8
    with nc.Block() as block:
        @block.sync
        def _(sp):
            for n in range(N):
                if n >= 3:
                    sp.wait_ge(low, n - 2)
                sp.dma_start(raw[:, n % 3, :].rearrange("p (k c) -> p k c", k=KT),
                             w[:, :, n * P:(n + 1) * P]).then_inc(loaded[n % 3], 16)
            sp.wait_ge(copied, N)
            sp.dma_start(O["new_mem_v_prompt"][0, 0].rearrange("(t p) h d -> p t (h d)", p=P),
                         mv[:, :, :]).then_inc(out, 16)
            sp.wait_ge(k_copied, 2)
            sp.dma_start(O["new_mem_k_prompt"][0, 0].rearrange("(t p) h d -> p t (h d)", p=P),
                         rows[:, :, :]).then_inc(out, 16)
            sp.wait_ge(out, 32)

        @block.gpsimd
        def _(pool):
            for n in range(N):
                pool.wait_ge(high, n + 1)
                pool.tensor_tensor(w_lo[:, n % 3, :], raw[:, n % 3, :], w_hi[:, n % 3, :].bitcast(F32),
                                   ALU.subtract).then_inc(low, 1)

        @block.tensor
        def _(pe):
            for n in range(N):
                pe.wait_ge(low, n + 1)
                hi = lambda k, n=n: w_hi[:, n % 3, k * P:(k + 1) * P]
                lo = lambda k, n=n: w_lo[:, n % 3, k * P:(k + 1) * P]
                ks = [(k, k) for k in range(KT)]
                if n >= 2:
                    pe.wait_ge(copied, n - 1)
                if n < 4:
                    mm = products(pe, bank[n % 2][:, 0:N_MEM], hi, lo, lambda k: m_hi[:, k, :],
                                  lambda k: m_lo[:, k, :], ks, True, True)
                else:
                    for t in range(2):
                        mm = products(pe, bank[n % 2][:, t * P:(t + 1) * P], hi, lo,
                                      lambda k: m_hi[:, k, t * P:(t + 1) * P],
                                      lambda k: m_lo[:, k, t * P:(t + 1) * P], ks, True, True, flip=True)
                mm.then_inc(ready, 1)
            pe.wait_ge(squared, 1)
            for g in range(2):
                mm = pe.matmul(bank[2 + g][:, :], ones[:, :], sq[:, 2 * g:2 * g + 2, :].rearrange("p h n -> p (h n)"),
                               start=True, stop=True)
            mm.then_inc(summed, 1)
            pe.wait_ge(normed, 4)
            for t in range(2):
                for h in range(4):
                    mm = pe.transpose(bank[4 + t][:, h * P:(h + 1) * P], mkT[:, h, t * P:(t + 1) * P], ident[:, :])
                mm.then_inc(k_turned, 1)

        @block.scalar
        def _(act):
            def high_part(n):
                act.wait_ge(loaded[n % 3], 16 * (n // 3 + 1))
                if n >= 3:
                    act.wait_ge(ready, n - 2)
                act.copy(w_hi[:, n % 3, :], raw[:, n % 3, :]).then_inc(high, 1)
            high_part(0)
            high_part(1)
            for n in range(N):
                if n + 2 < N:
                    high_part(n + 2)
                act.wait_ge(ready, n + 1)
                if n < 4:
                    act.copy(mkT[:, n, :], bank[n % 2][:, 0:N_MEM]).then_inc(copied, 1)
                else:
                    act.copy(mv[:, :, (n - 4) * P:(n - 3) * P],
                             bank[n % 2][:, 0:2 * P].rearrange("p (t c) -> p t c", t=2)).then_inc(copied, 1)
                if n == 4:
                    act.wait_ge(copied, 4)
                    act.activation(sq[:, :, :], mkT[:, :, :], ACT.Square).then_inc(squared, 1)
            act.wait_ge(summed, 1)
            act.wait_ge(eps_set, 1)
            for g in range(2):
                act.activation(rs[:, 2 * g:2 * g + 2, :].rearrange("p h n -> p (h n)"), bank[2 + g][:, :], ACT.Sqrt,
                               bias=eps[:, 0:1], scale=1.0 / P).then_inc(rooted, 1)
            for t in range(2):
                act.wait_ge(k_turned, t + 1)
                act.copy(rows[:, t, :], bank[4 + t][:, :]).then_inc(k_copied, 1)

        @block.vector
        def _(dve):
            dve.memset(eps[:, :], EPS).then_inc(eps_set, 1)
            dve.wait_ge(rooted, 2)
            dve.reciprocal(rs[:, :, :], rs[:, :, :]).then_inc(inverted, 1)
            dve.wait_ge(inverted, 1)
            for h in range(4):
                dve.scalar_tensor_tensor(mkT[:, h, :], mkT[:, h, :], column("gmk"), rs[:, h, :], ALU.mult,
                                         ALU.mult).then_inc(normed, 1)


def attention_plan():
    jobs = []
    for i in (0, 7, 1, 6, 2, 5, 3, 4):
        jobs += [("att", i, h) for h in range(H)] + [("mem", i, h) for h in range(H_MEM)]
    slots = [
        [("kt", 0), ("kt", 1), ("kt", 2), ("kt", 3)],
        [("sc", 0), ("kt", 4), ("kt", 5), ("kt", 6), ("kt", 7)],
        [("sc", 1), ("kt", 8), ("kt", 9), ("kt", 10), ("kt", 11)],
        [("sc", 2), ("kt", 12), ("kt", 13), ("kt", 14), ("kt", 15)],
        [("sc", 3), ("sc", 4)],
        [("soft",), ("kt", 16), ("kt", 17)],
        [("msc",)],
        [("pt", 0), ("pt", 1), ("pt", 2)],
        [("pv",), ("mpt",)],
        [("mpv",), ("ot",)],
        [("mot",)],
        [],
    ]
    plan = []
    turns = 0

    def add(*entry):
        nonlocal turns
        turn = None
        if entry[0] in ("turn", "oturn", "kt", "pt", "mpt", "ot", "mot"):
            turn = turns
            turns += 1
        plan.append((entry, turn))

    n = len(jobs)
    for s in range(n + 2):
        if s < n:
            add("scores", s)
        if 0 <= s - 2:
            add("values", s - 2)
            kind, i, h = jobs[s - 2]
            if (kind, h) in (("att", H - 1), ("mem", H_MEM - 1)):
                add("oturn", s - 2)
        if 0 <= s - 1 < n:
            kind, i, h = jobs[s - 1]
            blocks = i + 1 if kind == "att" else 2
            for g in range(0, blocks, 4):
                add("turn", s - 1, g, min(4, blocks - g))
        if s < n:
            for e in slots[s % 12]:
                add(e[0], s // 12, *e[1:])
    return jobs, plan


def attention(nc, sem, mem, bank, bank_t, ident, ident16, qT, kT, qmT, mkT, mv, bias, bias_s, rep, I, O):
    jobs, plan = attention_plan()
    at = AT_X + 8192
    def place(name, shape, dt, size):
        nonlocal at
        t = mem.at(name, shape, dt, at)
        at += (size + 31) // 32 * 32
        assert at <= AT_B, (name, at - AT_B)
        return t
    KR, UP = 6, PAGES + 2
    kt4 = mem.at("kt4", [P, 2, 4, 512], F32, AT_H + 12 * NT * 4)
    v_ring = mem.at("v_ring", [P, UP, 512], F32, AT_W)
    vp = place("vp", [P, 8, 512], F32, 16384)
    k_ring = place("k_ring", [P, KR, 512], F32, KR * 2048)
    pb = place("pb", [P, 2, SEQ], F32, 8192)
    pt = place("pt", [P, 8, P], F32, 4096)
    ps = place("ps", [NS, PAST + DEC_T], F32, (PAST + DEC_T) * 4)
    pts = place("pts", [P, PAGES + 1, NS], F32, (PAGES + 1) * NS * 4)
    qbd = place("qbd", [P, DEC_B, 4, NS], F32, 8192)
    qmbd = place("qmbd", [P, DEC_B, 4, 32], F32, 4096)
    o_sb = place("o_sb", [P, 512], F32, 2048)
    os_ = place("os", [NS, 512], F32, 2048)
    om_ = place("om", [32, 512], F32, 2048)
    vn = place("vn", [DEC_T, 512], F32, 2048)
    mks = place("mks", [P, 4, N_MEM], F32, 4096)
    pm = place("pm", [32, N_MEM], F32, 1024)
    ptm = place("ptm", [P, 2, 32], F32, 256)
    stats = place("stats", [P, 12], F32, 48)
    nm, rsum, rinv = stats[:, 0:4], stats[:, 4:8], stats[:, 8:12]
    st = mem.at("st", [NS, 8], F32, AT_C + 3552)
    table = mem.at("table2", [1, DEC_B * PAGES], I32, AT_C + 3584)
    turn_bank = [bank[4], bank[7]]

    table_in, vp_in = sem("table_in"), sem("vp_in")
    k_in = [sem(f"k_in{i}") for i in range(KR)]
    v_in = [sem(f"v_in{i}") for i in range(3)]
    vn_in = sem("vn_in")
    built0, built = sem("qbd_zero"), sem("qbd_built")
    scored, maxed, exped, inverted = sem("scored"), sem("maxed"), sem("exped"), sem("inverted")
    valued, normed = sem("valued"), sem("normed")
    turned = sem("turned2")
    evicted = [sem("turn_act"), sem("turn_dve")]
    used5, freed5 = sem("used5"), sem("freed5")
    s_max, s_exp, s_inv, s_norm = sem("s_max"), sem("s_exp"), sem("s_inv"), sem("s_norm")
    m_max, m_exp, m_inv, m_norm = sem("m_max"), sem("m_exp"), sem("m_inv"), sem("m_norm")

    turn_of = {entry: turn for entry, turn in plan if turn is not None}
    use_of = {}
    for entry, _ in plan:
        if entry[0] in ("sc", "msc", "pv", "mpv"):
            use_of[entry] = len(use_of)

    def wait_turn(eng, turn):
        eng.wait_ge(evicted[turn % 2], turn // 2 + 1)

    def last_turn(s):
        blocks = jobs[s][1] + 1 if jobs[s][0] == "att" else 2
        g = (blocks - 1) // 4 * 4
        return turn_of[("turn", s, g, blocks - g)]

    def turns_of(s):
        blocks = jobs[s][1] + 1 if jobs[s][0] == "att" else 2
        return [turn_of[("turn", s, g, min(4, blocks - g))] for g in range(0, blocks, 4)]

    def evict(eng, copy, me, entry, turn):
        if turn is None or turn % 2 != me:
            return
        b = turn_bank[me]
        eng.wait_ge(turned, turn + 1)
        kind = entry[0]
        if kind == "turn":
            _, s, g, w = entry
            if s >= 1:
                eng.wait_ge(valued, s)
            copy(pt[:, g:g + w, :], b[:, 0:w * P].rearrange("p (g n) -> p g n", n=P)).then_inc(evicted[me], 1)
        elif kind == "oturn":
            s = entry[1]
            dst = qT if jobs[s][0] == "att" else qmT
            i = jobs[s][1]
            copy(dst[:, :, i * P:(i + 1) * P], b.rearrange("p (g n) -> p g n", g=4)).then_inc(evicted[me], 1)
        elif kind == "kt":
            _, b_, u = entry
            if u < PAGES:
                g = u // 4
                if 4 * b_ + g >= 2:
                    older = (b_, g - 2) if g >= 2 else (b_ - 1, g + 2)
                    eng.wait_ge(used5, use_of[("sc", *older)] + 1)
                dst = kt4[:, g % 2, :, (u % 4) * P:(u % 4 + 1) * P]
            else:
                if b_ >= 1:
                    eng.wait_ge(used5, use_of[("msc", b_ - 1)] + 1)
                dst = mks[:, :, (u - PAGES) * P:(u - PAGES + 1) * P]
            copy(dst, b.rearrange("p (g n) -> p g n", g=4)).then_inc(evicted[me], 1)
        elif kind == "pt":
            _, b_, g = entry
            if b_ >= 1:
                eng.wait_ge(used5, use_of[("pv", b_ - 1)] + 1)
            if g < 2:
                copy(pts[:, 8 * g:8 * g + 8, :], b.rearrange("p (g n) -> p g n", n=NS)).then_inc(evicted[me], 1)
            else:
                copy(pts[0:DEC_T, PAGES, :], b[0:DEC_T, 0:NS]).then_inc(evicted[me], 1)
        elif kind == "mpt":
            if entry[1] >= 1:
                eng.wait_ge(used5, use_of[("mpv", entry[1] - 1)] + 1)
            copy(ptm[:, :, :], b[:, 0:64].rearrange("p (g n) -> p g n", g=2)).then_inc(evicted[me], 1)
        elif kind == "ot":
            b_ = entry[1]
            for e in range(2):
                src = b[e * DH:(e + 1) * DH, 8 * e:8 * e + 320].rearrange("p (j c) -> p j c", c=80)[:, :, 0:DEC_T]
                ins = copy(qT[e * DH:(e + 1) * DH, :, SEQ + 8 * b_:SEQ + 8 * b_ + 8], src)
            ins.then_inc(evicted[me], 1)
        elif kind == "mot":
            b_ = entry[1]
            src = b[:, 0:160].rearrange("p (j c) -> p j c", c=40)[:, :, 0:DEC_T]
            copy(qmT[:, :, SEQ + 8 * b_:SEQ + 8 * b_ + 8], src).then_inc(evicted[me], 1)

    with nc.Block() as block:
        @block.sync
        def _(sp):
            sp.dma_start(table[:, :], I["page_table"].rearrange("b g -> (b g)").rearrange(
                "(a n) -> a n", a=1)).then_inc(table_in, 16)
            sp.dma_start(vp[:, :, :], O["new_v_prompt"][0, 0].rearrange("(t p) h d -> p t (h d)", p=P)
                         ).then_inc(vp_in, 16)
            sp.wait_ge(table_in, 16)
            for b in range(DEC_B):
                pages = {}

                def page(u):
                    if u not in pages:
                        at = b * PAGES + u
                        pages[u] = sp.value_load(table[0:1, at:at + 1], min_val=0, max_val=I["cache_k"].shape[1] - 1)
                    return pages[u]

                def source(name, mem_name, u):
                    if u < PAGES:
                        return I[name][0][bass.ds(page(u), 1)].rearrange("a p h d -> p (a h d)")
                    return I[mem_name][0][b].rearrange("(t p) h d -> t p (h d)", p=P)[u - PAGES]
                for u in range(UP):
                    n = b * UP + u
                    if n >= KR:
                        before = divmod(n - KR, UP)
                        sp.wait_ge(turned, turn_of[("kt", *before)] + 1)
                    sp.dma_start(k_ring[:, n % KR, :], source("cache_k", "cache_mem_k", u)).then_inc(k_in[n % KR], 16)
                    if u == 0 and b >= 1:
                        sp.wait_ge(used5, use_of[("pv", b - 1)] + 1)
                        sp.wait_ge(used5, use_of[("mpv", b - 1)] + 1)
                    sp.dma_start(v_ring[:, u, :], source("cache_v", "cache_mem_v", u)).then_inc(v_in[u // 8], 16)
                    if u == 0:
                        sp.dma_start(vn[:, :], O["new_v_sample"][0][b].rearrange("t h d -> t (h d)")
                                     ).then_inc(vn_in, 16)

        @block.gpsimd
        def _(pool):
            pool.memset(qbd[:, :, :, :], 0.0).then_inc(built0, 1)
            pool.memset(qmbd[:, :, :, :], 0.0).then_inc(built0, 1)
            pool.wait_ge(built0, 2)
            for j in range(4):
                for e in range(2):
                    h = 2 * j + e
                    r = slice(e * DH, (e + 1) * DH)
                    if h:
                        pool.wait_ge(built, h)
                    pool.tensor_copy(qbd[r, :, j, h * 8:h * 8 + 8],
                                     qT[r, j, SEQ:NT].rearrange("p (b t) -> p b t", b=DEC_B)).then_inc(built, 1)
            pool.wait_ge(built, H)
            for h in range(H_MEM):
                pool.tensor_copy(qmbd[:, :, h, h * 8:h * 8 + 8],
                                 qmT[:, h, SEQ:NT].rearrange("p (b t) -> p b t", b=DEC_B)).then_inc(built, 1)

        @block.tensor
        def _(pe):
            for entry, turn in plan:
                kind, s = entry[0], entry[1]
                if turn is not None and turn >= 2:
                    wait_turn(pe, turn - 2)
                tb = turn_bank[turn % 2] if turn is not None else None
                if kind == "scores":
                    what, i, h = jobs[s]
                    b0 = 2 * (s % 2)
                    if s >= 2:
                        pe.wait_ge(exped, s - 1)
                    if what == "mem":
                        mm = pe.matmul(bank[b0][:, 0:N_MEM], qmT[:, h, i * P:(i + 1) * P], mkT[:, h, :],
                                       start=True, stop=True)
                    else:
                        r = slice((h % 2) * DH, (h % 2) * DH + DH)
                        keys = (i + 1) * P
                        for c, k0 in enumerate(range(0, keys, 512)):
                            w = min(512, keys - k0)
                            out = bank[b0 + c][:, 0:w]
                            pe.matmul(out, ident16[:, :], bias[:, bias_at(i) + k0:bias_at(i) + k0 + w], start=True,
                                      stop=False)
                            mm = pe.matmul(out, qT[r, h // 2, i * P:(i + 1) * P], kT[r, h // 2, k0:k0 + w],
                                           start=False, stop=True)
                    mm.then_inc(scored, 1)
                elif kind == "turn":
                    _, s, g, w = entry
                    pe.wait_ge(exped, s + 1)
                    for q in range(w):
                        mm = pe.transpose(tb[:, q * P:(q + 1) * P], pb[:, s % 2, (g + q) * P:(g + q + 1) * P],
                                          ident[:, :])
                    mm.then_inc(turned, 1)
                elif kind == "values":
                    what, i, h = jobs[s]
                    for t in turns_of(s):
                        wait_turn(pe, t)
                    if s == 0:
                        pe.wait_ge(vp_in, 16)
                    if s >= 1:
                        pe.wait_ge(normed, s)
                    if what == "att":
                        for j in range(i + 1):
                            mm = pe.matmul(bank[6][:, h * DH:(h + 1) * DH], pt[:, j, :],
                                           vp[:, j, h * DH:(h + 1) * DH], start=(j == 0), stop=(j == i))
                    else:
                        for j in range(2):
                            mm = pe.matmul(bank[6][:, h * P:(h + 1) * P], pt[:, j, :], mv[:, j, h * P:(h + 1) * P],
                                           start=(j == 0), stop=(j == 1))
                    mm.then_inc(valued, 1)
                elif kind == "oturn":
                    pe.wait_ge(normed, s + 1)
                    for j in range(4):
                        mm = pe.transpose(tb[:, j * P:(j + 1) * P], o_sb[:, j * P:(j + 1) * P], ident[:, :])
                    mm.then_inc(turned, 1)
                elif kind == "kt":
                    n = s * UP + entry[2]
                    pe.wait_ge(k_in[n % KR], 16 * (n // KR + 1))
                    for j in range(4):
                        mm = pe.transpose(tb[:, j * P:(j + 1) * P], k_ring[:, n % KR, j * P:(j + 1) * P], ident[:, :])
                    mm.then_inc(turned, 1)
                elif kind == "sc":
                    _, b, g = entry
                    if use_of[entry]:
                        pe.wait_ge(freed5, use_of[entry])
                    if b == 0 and g == 0:
                        pe.wait_ge(built, 12)
                    w = 512 if g < 4 else DEC_T
                    out = bank[5][0:NS, 0:w]
                    if g < 4:
                        for u in range(4 * g, 4 * g + 4):
                            wait_turn(pe, turn_of[("kt", b, u)])
                    pe.matmul(out, rep[:, b, :], bias_s[:, g * 512:g * 512 + w], start=True, stop=False)
                    for j in range(4):
                        keys = kt4[:, g % 2, j, :] if g < 4 else kT[:, j, SEQ + 8 * b:SEQ + 8 * b + 8]
                        mm = pe.matmul(out, qbd[:, b, j, :], keys, start=False, stop=(j == 3))
                    mm.then_inc(used5, 1)
                elif kind == "msc":
                    pe.wait_ge(freed5, use_of[entry])
                    for u in (PAGES, PAGES + 1):
                        wait_turn(pe, turn_of[("kt", s, u)])
                    for h in range(H_MEM):
                        mm = pe.matmul(bank[5][0:32, 0:N_MEM], qmbd[:, s, h, :], mks[:, h, :], start=(h == 0),
                                       stop=(h == 3))
                    mm.then_inc(used5, 1)
                elif kind == "pt":
                    pe.wait_ge(s_exp, s + 1)
                    g = entry[2]
                    if g < 2:
                        for q in range(8):
                            k = 8 * g + q
                            mm = pe.transpose(tb[:, q * NS:(q + 1) * NS], ps[:, k * P:(k + 1) * P], ident[0:NS, 0:NS])
                    else:
                        mm = pe.transpose(tb[0:DEC_T, 0:NS], ps[:, PAST:PAST + DEC_T], ident[0:NS, 0:NS])
                    mm.then_inc(turned, 1)
                elif kind == "pv":
                    pe.wait_ge(freed5, use_of[entry])
                    for g in range(3):
                        wait_turn(pe, turn_of[("pt", s, g)])
                    pe.wait_ge(v_in[0], 128 * (s + 1))
                    pe.wait_ge(v_in[1], 128 * (s + 1))
                    pe.wait_ge(vn_in, 16 * (s + 1))
                    for k in range(PAGES):
                        pe.matmul(bank[5][0:NS, :], pts[:, k, :], v_ring[:, k, :], start=(k == 0), stop=False)
                    pe.matmul(bank[5][0:NS, :], pts[0:DEC_T, PAGES, :], vn[:, :], start=False,
                              stop=True).then_inc(used5, 1)
                elif kind == "ot":
                    pe.wait_ge(s_norm, s + 1)
                    for j in range(4):
                        mm = pe.transpose(tb[:, j * NS:(j + 1) * NS], os_[:, j * P:(j + 1) * P], ident[0:NS, 0:NS])
                    mm.then_inc(turned, 1)
                elif kind == "mpt":
                    pe.wait_ge(m_exp, s + 1)
                    for j in range(2):
                        mm = pe.transpose(tb[:, j * 32:(j + 1) * 32], pm[:, j * P:(j + 1) * P], ident[0:32, 0:32])
                    mm.then_inc(turned, 1)
                elif kind == "mpv":
                    pe.wait_ge(freed5, use_of[entry])
                    wait_turn(pe, turn_of[("mpt", s)])
                    pe.wait_ge(v_in[2], 32 * (s + 1))
                    for j in range(2):
                        mm = pe.matmul(bank[5][0:32, :], ptm[:, j, :], v_ring[:, PAGES + j, :], start=(j == 0),
                                       stop=(j == 1))
                    mm.then_inc(used5, 1)
                elif kind == "mot":
                    pe.wait_ge(m_norm, s + 1)
                    for j in range(4):
                        mm = pe.transpose(tb[:, j * 32:(j + 1) * 32], om_[:, j * P:(j + 1) * P], ident[0:32, 0:32])
                    mm.then_inc(turned, 1)

        @block.scalar
        def _(act):
            for entry, turn in plan:
                kind, s = entry[0], entry[1]
                evict(act, act.copy, 0, entry, turn)
                if kind == "scores":
                    what, i, h = jobs[s]
                    b0 = 2 * (s % 2)
                    keys = (i + 1) * P if what == "att" else N_MEM
                    act.wait_ge(maxed, s + 1)
                    if s >= 2:
                        act.wait_ge(turned, last_turn(s - 2) + 1)
                    if s >= 4:
                        act.wait_ge(inverted, s - 3)
                    act.activation(pb[:, s % 2, 0:keys], bank_t[:, b0:b0 + 2, :].rearrange("p b n -> p (b n)")[:, 0:keys],
                                   ACT.Exp, bias=nm[:, s % 4:s % 4 + 1],
                                   accum_out=rsum[:, s % 4:s % 4 + 1]).then_inc(exped, 1)
                elif kind == "sc":
                    _, b, g = entry
                    w = 512 if g < 4 else DEC_T
                    act.wait_ge(used5, use_of[entry] + 1)
                    if b >= 1:
                        act.wait_ge(turned, turn_of[("pt", b - 1, 2)] + 1)
                    act.copy(ps[:, g * 512:g * 512 + w], bank[5][0:NS, 0:w]).then_inc(freed5, 1)
                elif kind == "soft":
                    act.wait_ge(s_max, s + 1)
                    act.activation(ps[:, :], ps[:, :], ACT.Exp, bias=st[:, 0:1], accum_out=st[:, 1:2]).then_inc(s_exp, 1)
                elif kind == "msc":
                    act.wait_ge(m_max, s + 1)
                    if s >= 1:
                        act.wait_ge(turned, turn_of[("mpt", s - 1)] + 1)
                    act.activation(pm[:, :], bank[5][0:32, 0:N_MEM], ACT.Exp, bias=st[0:32, 3:4],
                                   accum_out=st[0:32, 4:5]).then_inc(m_exp, 1)
                    act.wait_ge(m_exp, s + 1)
                    act.sem_inc(freed5, 1)

        @block.vector
        def _(dve):
            for entry, turn in plan:
                kind, s = entry[0], entry[1]
                evict(dve, dve.tensor_copy, 1, entry, turn)
                if kind == "scores":
                    what, i, h = jobs[s]
                    b0 = 2 * (s % 2)
                    keys = (i + 1) * P if what == "att" else N_MEM
                    dve.wait_ge(scored, s + 1)
                    if s >= 4:
                        dve.wait_ge(exped, s - 3)
                    dve.tensor_reduce(nm[:, s % 4:s % 4 + 1], bank_t[:, b0:b0 + 2, :].rearrange(
                        "p b n -> p (b n)")[:, 0:keys], AX.X, ALU.max, negate=True).then_inc(maxed, 1)
                elif kind == "values":
                    what, i, h = jobs[s]
                    w = DH if what == "att" else P
                    dve.wait_ge(exped, s + 1)
                    dve.reciprocal(rinv[:, s % 4:s % 4 + 1], rsum[:, s % 4:s % 4 + 1]).then_inc(inverted, 1)
                    dve.wait_ge(valued, s + 1)
                    dve.wait_ge(inverted, s + 1)
                    if h == 0 and s >= 1:
                        dve.wait_ge(turned, turn_of[("oturn", s - 1)] + 1)
                    dve.tensor_scalar(o_sb[:, h * w:(h + 1) * w], bank[6][:, h * w:(h + 1) * w],
                                      rinv[:, s % 4:s % 4 + 1], None, ALU.mult).then_inc(normed, 1)
                elif kind == "soft":
                    dve.wait_ge(freed5, use_of[("sc", s, 4)] + 1)
                    if s >= 1:
                        dve.wait_ge(s_exp, s)
                    dve.tensor_reduce(st[:, 0:1], ps[:, :], AX.X, ALU.max, negate=True).then_inc(s_max, 1)
                elif kind == "msc":
                    dve.wait_ge(used5, use_of[entry] + 1)
                    dve.tensor_reduce(st[0:32, 3:4], bank[5][0:32, 0:N_MEM], AX.X, ALU.max,
                                      negate=True).then_inc(m_max, 1)
                elif kind == "pv":
                    dve.wait_ge(s_exp, s + 1)
                    dve.reciprocal(st[:, 2:3], st[:, 1:2]).then_inc(s_inv, 1)
                    dve.wait_ge(s_inv, s + 1)
                    dve.wait_ge(used5, use_of[entry] + 1)
                    if s >= 1:
                        dve.wait_ge(turned, turn_of[("ot", s - 1)] + 1)
                    dve.tensor_scalar(os_[:, :], bank[5][0:NS, :], st[:, 2:3], None, ALU.mult).then_inc(s_norm, 1)
                    dve.wait_ge(s_norm, s + 1)
                    dve.sem_inc(freed5, 1)
                elif kind == "mpv":
                    dve.wait_ge(m_exp, s + 1)
                    dve.reciprocal(st[0:32, 5:6], st[0:32, 4:5]).then_inc(m_inv, 1)
                    dve.wait_ge(m_inv, s + 1)
                    dve.wait_ge(used5, use_of[entry] + 1)
                    if s >= 1:
                        dve.wait_ge(turned, turn_of[("mot", s - 1)] + 1)
                    dve.tensor_scalar(om_[:, :], bank[5][0:32, :], st[0:32, 5:6], None, ALU.mult).then_inc(m_norm, 1)
                    dve.wait_ge(m_norm, s + 1)
                    dve.sem_inc(freed5, 1)


def merge(nc, sem, mem, bank, x, raw, w_hi, w_lo, qT, qmT, x_kept, I, scratch):
    o_hi = mem.at("mo_hi", [P, 4, NT], F32R, AT_A)
    o_lo = mem.at("mo_lo", [P, 4, NT], F32R, AT_A + 4 * NT * 4)
    oy = mem.at("oy", [P, 4, NT], F32, AT_H + 4 * NT * 4)
    gate = mem.at("gate", [P, 2, NT], F32, AT_A + 8 * NT * 4)
    gated = mem.at("gated", [P, 2, CW], F32, AT_A + 10 * NT * 4)
    m = mem.at("m", [P, KT, NT], F32, AT_X)
    m_hi = mem.at("m_hi2", [P, KT, NT], F32R, AT_H)
    m_lo = mem.at("m_lo2", [P, KT, NT], F32R, AT_H + KT * NT * 4)
    x2 = mem.at("x2", [P, KT, NT], F32, AT_A)
    branches = [("w_attn_o", qT), ("w_mem_o", qmT), ("w_lru_o", oy)]
    gate_of = [0, 2, 1]
    loaded = [sem(f"mg_loaded{i}") for i in range(3)]
    high, low, ready = sem("mg_high"), sem("mg_low"), sem("mg_ready")
    y_in, gate_in = sem("y_in"), [sem("gate_in0"), sem("gate_in1")]
    o_high, o_low = sem("o_high"), sem("o_low")
    taken, added = sem("mg_taken"), sem("mg_added")
    N = 12
    with nc.Block() as block:
        @block.sync
        def _(sp):
            sp.dma_start(oy[:, :, :], scratch["y"].rearrange("j p n -> p j n")).then_inc(y_in, 16)
            for n in range(N):
                br, u = divmod(n, 4)
                if n >= 3:
                    sp.wait_ge(low, n - 2)
                w = I[branches[br][0]][0].rearrange("(k p) n -> p k n", p=P)
                sp.dma_start(raw[:, n % 3, :].rearrange("p (k c) -> p k c", k=4),
                             w[:, :, u * 256:(u + 1) * 256]).then_inc(loaded[n % 3], 16)
                for half in range(2):
                    g = 2 * n + half
                    if g >= 2:
                        sp.wait_ge(taken, 3 * (g - 1))
                    sp.dma_start(gate[:, g % 2, :], scratch["g"][gate_of[br] * KT + 2 * u + half]
                                 ).then_inc(gate_in[g % 2], 16)

        @block.gpsimd
        def _(pool):
            for n in range(N):
                pool.wait_ge(high, n + 1)
                pool.tensor_tensor(w_lo[:, n % 3, :], raw[:, n % 3, :], w_hi[:, n % 3, :].bitcast(F32),
                                   ALU.subtract).then_inc(low, 1)

        @block.tensor
        def _(pe):
            for n in range(N):
                br, u = divmod(n, 4)
                pe.wait_ge(low, n + 1)
                pe.wait_ge(o_low, 4 * (br + 1))
                for half in range(2):
                    for c, (t0, w) in enumerate(CH):
                        q = 3 * (2 * n + half) + c
                        if q >= 6:
                            pe.wait_ge(taken, q - 5)
                        mm = products(pe, bank[q % 6][:, 0:w],
                                      lambda k: w_hi[:, n % 3, k * 256 + half * P:k * 256 + half * P + P],
                                      lambda k: w_lo[:, n % 3, k * 256 + half * P:k * 256 + half * P + P],
                                      lambda k: o_hi[:, k, t0:t0 + w], lambda k: o_lo[:, k, t0:t0 + w],
                                      [(k, k) for k in range(4)], True, True)
                        mm.then_inc(ready, 1)

        @block.scalar
        def _(act):
            def high_part(n):
                act.wait_ge(loaded[n % 3], 16 * (n // 3 + 1))
                if n >= 3:
                    act.wait_ge(ready, 6 * (n - 2))
                act.copy(w_hi[:, n % 3, :], raw[:, n % 3, :]).then_inc(high, 1)
            high_part(0)
            high_part(1)
            for n in range(N):
                br, u = divmod(n, 4)
                if u == 0:
                    if br == 2:
                        act.wait_ge(y_in, 16)
                    if br:
                        act.wait_ge(ready, 24 * br)
                    for k in range(4):
                        act.copy(o_hi[:, k, :], branches[br][1][:, k, :]).then_inc(o_high, 1)
                if n + 2 < N:
                    high_part(n + 2)

        @block.vector
        def _(dve):
            for n in range(N):
                br, u = divmod(n, 4)
                if u == 0:
                    for k in range(4):
                        dve.wait_ge(o_high, 4 * br + k + 1)
                        dve.tensor_tensor(o_lo[:, k, :], branches[br][1][:, k, :], o_hi[:, k, :].bitcast(F32),
                                          ALU.subtract).then_inc(o_low, 1)
                for half in range(2):
                    g = 2 * n + half
                    dve.wait_ge(gate_in[g % 2], 16 * (g // 2 + 1))
                    for c, (t0, w) in enumerate(CH):
                        q = 3 * g + c
                        dve.wait_ge(ready, q + 1)
                        dst = m[:, 2 * u + half, t0:t0 + w]
                        out = dst if br == 0 else gated[:, q % 2, 0:w]
                        dve.tensor_tensor(out, bank[q % 6][:, 0:w], gate[:, g % 2, t0:t0 + w],
                                          ALU.mult).then_inc(taken, 1)
                        if br:
                            dve.wait_ge(taken, q + 1)
                            dve.tensor_tensor(dst, dst, gated[:, q % 2, 0:w], ALU.add).then_inc(added, 1)

    loaded = [sem(f"wo_loaded{i}") for i in range(3)]
    high, low, ready, done = sem("wo_high"), sem("wo_low"), sem("wo_ready"), sem("wo_done")
    m_high, m_low, x_in = sem("m_high"), sem("m_low"), sem("x_in")
    w_out = I["w_out"][0].rearrange("(k p) n -> p k n", p=P)
    N2 = KT
    with nc.Block() as block:
        @block.sync
        def _(sp):
            sp.dma_start(x2[:, :, :], x_kept).then_inc(x_in, 16)
            for n in range(N2):
                if n >= 3:
                    sp.wait_ge(low, n - 2)
                sp.dma_start(raw[:, n % 3, :].rearrange("p (k c) -> p k c", k=KT),
                             w_out[:, :, n * P:(n + 1) * P]).then_inc(loaded[n % 3], 16)

        @block.gpsimd
        def _(pool):
            for n in range(N2):
                pool.wait_ge(high, n + 1)
                pool.tensor_tensor(w_lo[:, n % 3, :], raw[:, n % 3, :], w_hi[:, n % 3, :].bitcast(F32),
                                   ALU.subtract).then_inc(low, 1)

        @block.tensor
        def _(pe):
            for n in range(N2):
                pe.wait_ge(low, n + 1)
                for c, (t0, w) in enumerate(CH):
                    q = 3 * n + c
                    if q >= 6:
                        pe.wait_ge(done, q - 5)
                    for k in range(KT):
                        if n == 0 and c == 0:
                            pe.wait_ge(m_low, k + 1)
                        mm = products(pe, bank[q % 6][:, 0:w], lambda k: w_hi[:, n % 3, k * P:(k + 1) * P],
                                      lambda k: w_lo[:, n % 3, k * P:(k + 1) * P], lambda k: m_hi[:, k, t0:t0 + w],
                                      lambda k: m_lo[:, k, t0:t0 + w], [(k, k)], k == 0, k == KT - 1)
                    mm.then_inc(ready, 1)

        @block.scalar
        def _(act):
            def high_part(n):
                act.wait_ge(loaded[n % 3], 16 * (n // 3 + 1))
                if n >= 3:
                    act.wait_ge(ready, 3 * (n - 2))
                act.copy(w_hi[:, n % 3, :], raw[:, n % 3, :]).then_inc(high, 1)
            for k in range(KT):
                act.copy(m_hi[:, k, :], m[:, k, :]).then_inc(m_high, 1)
                if k < 2:
                    high_part(k)
            for n in range(2, N2):
                high_part(n)

        @block.vector
        def _(dve):
            for k in range(KT):
                dve.wait_ge(m_high, k + 1)
                dve.tensor_tensor(m_lo[:, k, :], m[:, k, :], m_hi[:, k, :].bitcast(F32),
                                  ALU.subtract).then_inc(m_low, 1)
            dve.wait_ge(m_low, KT)
            dve.wait_ge(x_in, 16)
            for n in range(N2):
                for c, (t0, w) in enumerate(CH):
                    q = 3 * n + c
                    dve.wait_ge(ready, q + 1)
                    dve.tensor_tensor(x[:, n, t0:t0 + w], bank[q % 6][:, 0:w], x2[:, n, t0:t0 + w],
                                      ALU.add).then_inc(done, 1)


OUTS = [("y_prompt", (1, SEQ, D)), ("y_sample", (DEC_B, DEC_T, D)), ("new_k_prompt", (1, 1, SEQ, H, DH)),
        ("new_v_prompt", (1, 1, SEQ, H, DH)), ("new_kidx_prompt", (1, 1, SEQ, DH)),
        ("new_mem_k_prompt", (1, 1, N_MEM, H_MEM, P)), ("new_mem_v_prompt", (1, 1, N_MEM, H_MEM, P)),
        ("new_conv_prompt", (1, 1, 3, LRU_W)), ("new_h_prompt", (1, 1, LRU_W)),
        ("new_k_sample", (1, DEC_B, DEC_T, H, DH)), ("new_v_sample", (1, DEC_B, DEC_T, H, DH)),
        ("new_kidx_sample", (1, DEC_B, DEC_T, DH)), ("new_conv_sample", (1, DEC_B, 3, LRU_W)),
        ("new_h_sample", (1, DEC_B, LRU_W))]


def kernel(**inputs):
    import concourse.bacc as bacc
    from concourse.bass_utils import run_bass_kernel_spmd
    nc = bacc.Bacc("TRN2", target_bir_lowering=False, num_devices=1)
    arrays = {name: np.ascontiguousarray(a) for name, a in inputs.items()}
    I = {name: nc.dram_tensor(f"in_{name}", a.shape, mybir.dt.from_np(a.dtype), kind="ExternalInput").ap()
         for name, a in arrays.items()}
    O = {name: nc.dram_tensor(f"out_{name}", shape, F32, kind="ExternalOutput").ap() for name, shape in OUTS}
    decoder_step(nc, I, O)
    r = run_bass_kernel_spmd(nc, [{f"in_{name}": a for name, a in arrays.items()}], core_ids=[0])
    return tuple(r.results[0][f"out_{name}"] for name, _ in OUTS)
```

```python
from contextlib import ExitStack, contextmanager

import numpy as np

import concourse.bass as bass
from concourse import mybir

F32 = mybir.dt.float32
F32R = mybir.dt.float32r
BF16 = mybir.dt.bfloat16
I32 = mybir.dt.int32
ALU = mybir.AluOpType
ACT = mybir.ActivationFunctionType
AX = mybir.AxisListType

P = 128
SEQ = 1024
DEC_B = 8
DEC_T = 8
NS = DEC_B * DEC_T
NT = SEQ + NS
D = 1024
KT = D // P
D_FF = 2816
H = 8
DH = 64
HD = H * DH
PAGE = 128
PAGES = 16
PAST = PAGE * PAGES
N_KEYS = PAST + DEC_T
TOPK = 256
H_MEM = 4
N_MEM = 256
LRU_W = 512
LT = LRU_W // P
EPS = 1e-6
BIG = -1e30
TAKEN = -3e38
BARRED = -2e38

CH = [(0, 364), (364, 362), (726, 362)]
CW = 364
TT = [(t * P, P) for t in range(SEQ // P)] + [(SEQ, NS)]

C_Q, C_K, C_V, C_QI, C_KI, C_LX, C_LG, C_QM, C_G = 0, 512, 1024, 1536, 2048, 2120, 2632, 3144, 3656

ROWS = {}
_at = 0
for _name, _n in (("g_ffn1", 8), ("g_mix", 8), ("g_ffn2", 8), ("g_mem", 8), ("conv_w", 16), ("conv_b", 4),
                  ("ba", 4), ("bi", 4), ("lam", 4), ("gq", 1), ("gk", 1), ("gmq", 1), ("gmk", 1), ("h0", 32)):
    ROWS[_name] = _at
    _at += _n
N_ROWS = _at


class Memory:

    def __init__(self, nc):
        self.nc = nc
        self.n = 0

    def at(self, name, shape, dt, offset):
        self.n += 1
        return self.nc.alloc_sbuf_tensor_at(f"{name}_{self.n}", shape, dt, offset=offset)


@contextmanager
def phase(nc):
    given = []

    def sem(name):
        given.append(nc.alloc_semaphore(name=name))
        return given[-1]

    yield sem
    nc.clear_and_free_semaphores(given)
    nc.all_engine_barrier()


AT_H = 16512
AT_W = AT_H + 2 * KT * NT * 4
AT_C = AT_W + 9 * 4096
AT_X = AT_C + 4096
AT_A = AT_X + KT * NT * 4
AT_END = 229344
AT_B = AT_END - 14592


def transposes_pe(pe, nc, jobs, ident, bank, ready, evicted, done):
    for n, job in enumerate(jobs):
        for sem, value in job["needs"]:
            pe.wait_ge(sem, value)
        if n >= len(bank):
            pe.wait_ge(evicted[n % 2], n // 2 - len(bank) // 2 + 1)
        at = 0
        for src in job["src"]:
            rows, cols = src.shape
            mm = pe.transpose(bank[n % len(bank)][0:cols, at:at + rows], src, ident[0:rows, 0:rows])
            at += job.get("step", rows)
        mm.then_inc(done, 1)


def transposes_evict(eng, copy, jobs, which, bank, done, evicted):
    for n, job in enumerate(jobs):
        if n % 2 != which:
            continue
        eng.wait_ge(done, n + 1)
        copy(job["dst"], job["psum"](bank[n % len(bank)])).then_inc(evicted[which], 1)


class Norm:

    def __init__(self, sem, mem, bank, x, width, chunks, gain, ones, hi, lo, tag, scratch):
        self.bank, self.x, self.chunks, self.gain, self.ones, self.hi, self.lo = bank, x, chunks, gain, ones, hi, lo
        self.sq = mem.at(f"sq{tag}", [P, 2, width], F32, scratch)
        self.rs = mem.at(f"rs{tag}", [P, width], F32, scratch + 2 * width * 4)
        self.hn = mem.at(f"hn{tag}", [P, 4, 512], F32, scratch + 3 * width * 4)
        self.eps = mem.at(f"eps{tag}", [P, 1], F32, scratch + 3 * width * 4 + 4 * 2048)
        self.squared, self.summed, self.rooted = sem(f"squared{tag}"), sem(f"summed{tag}"), sem(f"rooted{tag}")
        self.inverted, self.normed = sem(f"inverted{tag}"), sem(f"normed{tag}")
        self.high, self.low, self.eps_set = sem(f"high{tag}"), sem(f"low{tag}"), sem(f"eps_set{tag}")

    def steps(self):
        return [(KT * c + k, t0, w, k) for c, (t0, w) in enumerate(self.chunks) for k in range(KT)]

    def squares(self, act):
        for k in range(KT):
            if k >= 2:
                act.wait_ge(self.summed, k - 1)
            act.activation(self.sq[:, k % 2, :], self.x[:, k, :], ACT.Square).then_inc(self.squared, 1)

    def roots(self, act):
        act.wait_ge(self.summed, KT)
        act.wait_ge(self.eps_set, 1)
        for c, (t0, w) in enumerate(self.chunks):
            act.activation(self.rs[:, t0:t0 + w], self.bank[c][:, 0:w], ACT.Sqrt, bias=self.eps[:, 0:1],
                           scale=1.0 / D).then_inc(self.rooted, 1)
        for n, t0, w, k in self.steps():
            act.wait_ge(self.normed, n + 1)
            act.copy(self.hi[:, k, t0:t0 + w], self.hn[:, n % 4, 0:w]).then_inc(self.high, 1)

    def on_pe(self, pe):
        for k in range(KT):
            pe.wait_ge(self.squared, k + 1)
            for c, (t0, w) in enumerate(self.chunks):
                mm = pe.matmul(self.bank[c][:, 0:w], self.ones[:, :], self.sq[:, k % 2, t0:t0 + w],
                               start=(k == 0), stop=(k == KT - 1))
            mm.then_inc(self.summed, 1)

    def on_dve(self, dve):
        dve.memset(self.eps[:, :], EPS).then_inc(self.eps_set, 1)
        for n, t0, w, k in self.steps():
            c = n // KT
            if k == 0:
                dve.wait_ge(self.rooted, c + 1)
                dve.reciprocal(self.rs[:, t0:t0 + w], self.rs[:, t0:t0 + w]).then_inc(self.inverted, 1)
                dve.wait_ge(self.inverted, c + 1)
            if n >= 4:
                dve.wait_ge(self.low, n - 3)
            dve.scalar_tensor_tensor(self.hn[:, n % 4, 0:w], self.x[:, k, t0:t0 + w], self.gain[:, k:k + 1],
                                     self.rs[:, t0:t0 + w], ALU.mult, ALU.mult).then_inc(self.normed, 1)

    def on_pool(self, pool):
        for n, t0, w, k in self.steps():
            pool.wait_ge(self.high, n + 1)
            pool.tensor_tensor(self.lo[:, k, t0:t0 + w], self.hn[:, n % 4, 0:w],
                               self.hi[:, k, t0:t0 + w].bitcast(F32), ALU.subtract).then_inc(self.low, 1)


def products(pe, out, w_hi, w_lo, a_hi, a_lo, ks, start, stop, flip=False):
    n = len(ks)
    for i, (kw, ka) in enumerate(ks):
        for j, (w, a) in enumerate(((w_hi, a_hi), (w_hi, a_lo), (w_lo, a_hi))):
            left, right = (a(ka), w(kw)) if flip else (w(kw), a(ka))
            mm = pe.matmul(out, left, right, start=(start and i == 0 and j == 0),
                           stop=(stop and i == n - 1 and j == 2))
    return mm


def ffn(nc, sem, mem, bank, norm, x, h_hi, h_lo, raw, w_hi, w_lo, w_in, w_out, tag):
    G = D_FF // (2 * P)
    a_hi = mem.at(f"a_hi{tag}", [P, 2, NT], F32R, AT_A)
    a_lo = mem.at(f"a_lo{tag}", [P, 2, NT], F32R, AT_A + 2 * NT * 4)
    sg = mem.at(f"sg{tag}", [P, 3, CW], F32, AT_A + 4 * NT * 4)
    pr = mem.at(f"pr{tag}", [P, 3, CW], F32, AT_A + 4 * NT * 4 + 4384)
    loaded = [sem(f"unit_loaded{i}{tag}") for i in range(3)]
    high = sem(f"unit_high{tag}")
    low = sem(f"unit_low{tag}")
    gate_ready = sem(f"gate_ready{tag}")
    up_ready = sem(f"up_ready{tag}")
    silu_done = sem(f"silu_done{tag}")
    prod_done = sem(f"prod_done{tag}")
    prod_high = sem(f"prod_high{tag}")
    prod_low = sem(f"prod_low{tag}")
    out_ready = sem(f"out_ready{tag}")
    x_added = sem(f"x_added{tag}")
    RING, XC = 3, 24
    win = w_in.rearrange("(k p) n -> p k n", p=P)
    wout = w_out.rearrange("(r p) n -> p r n", p=P)

    def src(i, u):
        if u < 4:
            col = (u % 2) * D_FF + (u // 2) * P
            return win[:, :, bass.ds(i * (2 * P) + col, P)]
        return wout[:, bass.ds(i * 2 + (u - 4), 1), :]

    def wh(s):
        return lambda k: w_hi[:, s, k * P:(k + 1) * P]

    def wl(s):
        return lambda k: w_lo[:, s, k * P:(k + 1) * P]

    with nc.Block() as block:
        @block.sync
        def _(sp):
            with sp.Fori(0, G) as i:
                for u in range(6):
                    sp.wait_ge(low, i * 6 + u + 1)
                    dst = raw[:, u % 3, :]
                    dst = dst.rearrange("p (k n) -> p k n", k=KT) if u < 4 else \
                        dst.rearrange("p (a n) -> p a n", a=1)
                    sp.dma_start(dst, src(i, u)).then_inc(loaded[u % 3], 16)

        @block.gpsimd
        def _(pool):
            def low_part(i, u):
                pool.wait_ge(high, i * 6 + u + 1)
                pool.tensor_tensor(w_lo[:, u % 3, :], raw[:, u % 3, :], w_hi[:, u % 3, :].bitcast(F32),
                                   ALU.subtract).then_inc(low, 1)

            pool.sem_inc(low, RING)
            low_part(0, 0)
            low_part(0, 1)
            norm.on_pool(pool)
            with pool.Fori(0, G - 1) as i:
                for u in range(2, 6):
                    low_part(i, u)
                for u in range(2):
                    low_part(i + 1, u)
            for u in range(2, 6):
                low_part(G - 1, u)

        @block.tensor
        def _(pe):
            pe.sem_inc(out_ready, XC)
            norm.on_pe(pe)
            with pe.Fori(0, G) as i:
                for t in range(2):
                    for half, (ready, free) in enumerate(((gate_ready, silu_done), (up_ready, prod_done))):
                        u = 2 * t + half
                        pe.wait_ge(low, i * 6 + u + 1 + RING)
                        for c, (t0, w) in enumerate(CH):
                            if u == 0:
                                pe.wait_ge(norm.low, KT * (c + 1))
                            pe.wait_ge(free, i * 6 + 3 * t + c + 1)
                            mm = products(pe, bank[3 * half + c][:, 0:w], wh(u % 3), wl(u % 3),
                                          lambda k: h_hi[:, k, t0:t0 + w], lambda k: h_lo[:, k, t0:t0 + w],
                                          [(k, k) for k in range(KT)], True, True)
                            mm.then_inc(ready, 1)
                pe.wait_ge(low, i * 6 + 6 + RING)
                for c, (t0, w) in enumerate(CH):
                    pe.wait_ge(prod_low, i * 6 + 3 + c + 1)
                    for j in range(KT):
                        n = 8 * c + j
                        pe.wait_ge(x_added, i * XC + n - 1 + XC)
                        o = bank[6 + n % 2][:, 0:w]
                        products(pe, o, lambda k: w_hi[:, 1, j * P:(j + 1) * P],
                                 lambda k: w_lo[:, 1, j * P:(j + 1) * P],
                                 lambda k: a_hi[:, 0, t0:t0 + w], lambda k: a_lo[:, 0, t0:t0 + w],
                                 [(0, 0)], True, False)
                        mm = products(pe, o, lambda k: w_hi[:, 2, j * P:(j + 1) * P],
                                      lambda k: w_lo[:, 2, j * P:(j + 1) * P],
                                      lambda k: a_hi[:, 1, t0:t0 + w], lambda k: a_lo[:, 1, t0:t0 + w],
                                      [(0, 0)], False, True)
                        mm.then_inc(out_ready, 1)

        def high_part(act, i, u, first=False):
            if u in (1, 2):
                act.wait_ge(out_ready, i * XC + XC)
            elif u in (3, 5):
                act.wait_ge(gate_ready, i * 6 + (3 if u == 3 else 6))
            elif u == 4:
                act.wait_ge(up_ready, i * 6 + 3)
            elif not first:
                act.wait_ge(up_ready, i * 6)
            act.wait_ge(loaded[u % 3], i * 32 + 16 * (u // 3 + 1))
            act.copy(w_hi[:, u % 3, :], raw[:, u % 3, :]).then_inc(high, 1)

        def act_round(act, i, last):
            for u in range(6):
                if not last or u < 4:
                    high_part(act, i + (u + 2) // 6, (u + 2) % 6)
                t = u // 2
                if u < 4 and u % 2 == 0:
                    for c, (t0, w) in enumerate(CH):
                        act.wait_ge(gate_ready, i * 6 + 3 * t + c + 1)
                        act.wait_ge(prod_done, i * 6 + 3 * t + c + 1)
                        act.activation(sg[:, c, 0:w], bank[c][:, 0:w], ACT.Silu).then_inc(silu_done, 1)
                elif u < 4:
                    for c, (t0, w) in enumerate(CH):
                        act.wait_ge(prod_done, i * 6 + 3 * t + c + 1 + RING)
                        act.wait_ge(out_ready, i * XC + XC)
                        act.copy(a_hi[:, t, t0:t0 + w], pr[:, c, 0:w]).then_inc(prod_high, 1)

        @block.scalar
        def _(act):
            act.sem_inc(silu_done, RING)
            norm.squares(act)
            high_part(act, 0, 0, True)
            high_part(act, 0, 1)
            norm.roots(act)
            with act.Fori(0, G - 1) as i:
                act_round(act, i, False)
            act_round(act, G - 1, True)

        @block.vector
        def _(dve):
            dve.sem_inc(prod_done, RING)
            dve.sem_inc(x_added, XC)
            norm.on_dve(dve)
            with dve.Fori(0, G) as i:
                for t in range(2):
                    def product(c):
                        t0, w = CH[c]
                        dve.wait_ge(silu_done, i * 6 + 3 * t + c + 1 + RING)
                        dve.wait_ge(up_ready, i * 6 + 3 * t + c + 1)
                        dve.tensor_tensor(pr[:, c, 0:w], sg[:, c, 0:w], bank[3 + c][:, 0:w],
                                          ALU.mult).then_inc(prod_done, 1)

                    def low_part(c):
                        t0, w = CH[c]
                        dve.wait_ge(prod_high, i * 6 + 3 * t + c + 1)
                        dve.tensor_tensor(a_lo[:, t, t0:t0 + w], pr[:, c, 0:w],
                                          a_hi[:, t, t0:t0 + w].bitcast(F32),
                                          ALU.subtract).then_inc(prod_low, 1)
                    product(0)
                    product(1)
                    low_part(0)
                    low_part(1)
                    product(2)
                    low_part(2)
                for c, (t0, w) in enumerate(CH):
                    for j in range(KT):
                        n = 8 * c + j
                        dve.wait_ge(out_ready, i * XC + n + 1 + XC)
                        dve.wait_ge(x_added, i * XC + n + 1)
                        dve.scalar_tensor_tensor(x[:, j, t0:t0 + w], bank[6 + n % 2][:, 0:w], 0.5,
                                                 x[:, j, t0:t0 + w], ALU.mult, ALU.add).then_inc(x_added, 1)


def decoder_step(nc, I, O):
    ctx = ExitStack()
    with ctx:
        mem = Memory(nc)

        bank_t = ctx.enter_context(nc.psum_tensor("bank", [P, 8, 512], F32))
        bank = [bank_t[:, b, :] for b in range(8)]
        h_hi = mem.at("h_hi", [P, KT, NT], F32R, AT_H)
        h_lo = mem.at("h_lo", [P, KT, NT], F32R, AT_H + KT * NT * 4)
        raw = mem.at("raw", [P, 3, 1024], F32, AT_W)
        w_hi = mem.at("w_hi", [P, 3, 1024], F32R, AT_W + 3 * 4096)
        w_lo = mem.at("w_lo", [P, 3, 1024], F32R, AT_W + 6 * 4096)
        x = mem.at("x", [P, KT, NT], F32, AT_X)
        ident = mem.at("ident", [P, P], F32, AT_C)
        ones = mem.at("ones", [P, P], F32, AT_C + 512)
        ones_half = mem.at("ones_half", [P, P], F32, AT_C + 1024)
        ident16 = mem.at("ident16", [P, P], BF16, AT_C + 1536)
        par = mem.at("par", [P, N_ROWS], F32, AT_C + 1792)

        def column(name, k=0, n=1):
            return par[:, ROWS[name] + k:ROWS[name] + k + n]

        misc = dict(cb=mem.at("cb", [P, P], F32, AT_C + 2208), cb16=mem.at("cb16", [P, P], BF16, AT_C + 2720),
                    t8=mem.at("t8", [NS, DEC_T], F32, AT_C + 2976), cb8=mem.at("cb8", [NS, DEC_T], F32, AT_C + 3008),
                    b8=mem.at("b8", [NS, NS], F32, AT_C + 3040),
                    spread=mem.at("spread", [P, NS], F32, AT_C + 3296))
        bias = mem.at("bias", [P, 36 * P], BF16, AT_B)
        bias_s = mem.at("bias_s", [NS, PAST + DEC_T], BF16, AT_B + 9216)
        rep = mem.at("rep", [NS, DEC_B, NS], BF16, AT_B + 9216 + 4128)

        def dram(name, shape):
            return nc.dram_tensor(name, shape, F32, kind="Internal").ap()
        x_kept = dram("x_kept", (P, KT, NT))
        scratch = {name: dram(f"kept_{name}", (n, P, NT)) for name, n in
                   (("q", 4), ("k", 4), ("qm", 4), ("lx", 4), ("lg", 4), ("y", 4), ("g", 24))}

        with phase(nc) as sem:
            setup(nc, sem, mem, bank, x, ident, ones, ones_half, ident16, par, misc, I)

        def feed_forward(n):
            with phase(nc) as sem:
                norm = Norm(sem, mem, bank, x, NT, CH, column(f"g_ffn{n}", 0, KT), ones, h_hi, h_lo, f"_ffn{n}",
                            AT_A + 27648)
                ffn(nc, sem, mem, bank, norm, x, h_hi, h_lo, raw, w_hi, w_lo, I[f"w_ffn{n}_in"][0],
                    I[f"w_ffn{n}_out"][0], f"_ffn{n}")

        feed_forward(1)
        with phase(nc) as sem:
            norm = Norm(sem, mem, bank, x, NT, CH, column("g_mix", 0, KT), ones, h_hi, h_lo, "_mix", AT_A)
            mixing_inputs(nc, sem, mem, bank, norm, x, x_kept, h_hi, h_lo, raw, w_hi, w_lo, ident, I, O, scratch, bias, bias_s,
                          rep, misc)
        qT = mem.at("qT", [P, 4, NT], F32, AT_H)
        kT = mem.at("kT", [P, 4, NT], F32, AT_H + 4 * NT * 4)
        qmT = mem.at("qmT", [P, 4, NT], F32, AT_H + 8 * NT * 4)
        mkT = mem.at("mkT", [P, H_MEM, N_MEM], F32, AT_X)
        mv = mem.at("mv", [P, 2, 512], F32, AT_X + 4096)
        with phase(nc) as sem:
            mem_hi, mem_lo = memory_input(nc, sem, mem, bank, ident, ones, column, I)
            mk = MemoryKeys(sem, mem, bank, ident, ones, column, raw, w_hi, w_lo, mem_hi, mem_lo, mkT, mv, I, O)
            recurrence(nc, sem, mem, bank, ident, column, mk, I, O, scratch)
        with phase(nc) as sem:
            head_norms(nc, sem, mem, bank, ident, ones, ones_half, column, qT, kT, qmT, O, scratch)
        with phase(nc) as sem:
            attention(nc, sem, mem, bank, bank_t, ident, ident16, qT, kT, qmT, mkT, mv, bias, bias_s, rep, I, O)
        with phase(nc) as sem:
            merge(nc, sem, mem, bank, x, raw, w_hi, w_lo, qT, qmT, x_kept, I, scratch)
        feed_forward(2)
        with phase(nc) as sem:
            results(nc, sem, mem, bank, x, ident, O)


def setup(nc, sem, mem, bank, x, ident, ones, ones_half, ident16, par, misc, I):
    xin = mem.at("xin", [P, 9, D], F32, AT_A)
    prow = mem.at("prow", [N_ROWS, P], F32, AT_A + 9 * D * 4)
    rows_loaded = sem("rows_loaded")
    x_loaded = [sem(f"x_loaded{t}") for t in range(9)]
    cleared = sem("cleared")
    zeroed = sem("zeroed")
    boxed = sem("boxed")
    cb, cb16, t8, cb8, b8 = misc["cb"], misc["cb16"], misc["t8"], misc["cb8"], misc["b8"]
    u8 = mem.at("u8", [NS, NS], F32, AT_A + 9 * D * 4 + 512)
    made = sem("made")
    turned = sem("turned")
    evicted = [sem("evicted_act"), sem("evicted_dve")]
    x_rows = I["x_prompt"][0].rearrange("(t p) d -> t p d", p=P)
    s_rows = I["x_sample"].rearrange("b t d -> (b t) d")
    params = [(ROWS[name], n, I[key][0].rearrange(how, c=P) if how else I[key]) for name, n, key, how in (
        ("g_ffn1", 8, "norm_ffn1_g", "(k c) -> k c"), ("g_mix", 8, "norm_mix_g", "(k c) -> k c"),
        ("g_ffn2", 8, "norm_ffn2_g", "(k c) -> k c"), ("g_mem", 8, "norm_mem_g", "(k c) -> k c"),
        ("conv_w", 16, "conv_w", "w (k c) -> (w k) c"), ("conv_b", 4, "conv_b", "(k c) -> k c"),
        ("ba", 4, "lru_ba", "(k c) -> k c"), ("bi", 4, "lru_bi", "(k c) -> k c"),
        ("lam", 4, "lru_lambda", "(k c) -> k c"), ("gmq", 1, "mem_q_norm_g", None),
        ("gmk", 1, "mem_k_norm_g", None), ("h0", 32, "state_h", "b (k c) -> (b k) c"))]
    jobs = [dict(src=[prow[:, :]], dst=par[:, :], psum=lambda b: b[:, 0:N_ROWS],
                 needs=[(made, 5), (rows_loaded, 16 * (len(params) + 4))])]
    for t, (t0, w) in enumerate(TT):
        for half in range(2):
            jobs.append(dict(
                src=[xin[0:w, t, (4 * half + q) * P:(4 * half + q + 1) * P] for q in range(4)],
                dst=x[:, 4 * half:4 * half + 4, t0:t0 + w],
                psum=lambda b, w=w: b[:, 0:4 * w].rearrange("p (q n) -> p q n", q=4),
                needs=[(x_loaded[t], 16)]))

    with nc.Block() as block:
        @block.sync
        def _(sp):
            for r, n, src in params:
                sp.dma_start(prow[r:r + n, :], src).then_inc(rows_loaded, 16)
            for name, key in (("gq", "q_norm_g"), ("gk", "k_norm_g")):
                for half in range(2):
                    sp.dma_start(prow[ROWS[name]:ROWS[name] + 1, half * DH:(half + 1) * DH],
                                 I[key]).then_inc(rows_loaded, 16)

        @block.gpsimd
        def _(pool):
            pool.memset(ident[:, :], 0.0).then_inc(cleared, 1)
            pool.memset(ident16[:, :], 0.0).then_inc(cleared, 1)
            pool.memset(ones[:, :], 1.0).then_inc(made, 1)
            pool.wait_ge(cleared, 2)
            for m in (ident, ident16):
                pool.affine_select(out=m[:, :], in_=m[:, :], compare_op=ALU.not_equal, fill=1.0, base=0,
                                   pattern=[[-1, P]], channel_multiplier=1).then_inc(made, 1)
            pool.memset(cb[:, :], 0.0).then_inc(cleared, 1)
            pool.memset(cb16[:, :], 0.0).then_inc(cleared, 1)
            pool.memset(b8[:, :], 1.0).then_inc(cleared, 1)
            pool.wait_ge(cleared, 5)
            for m, fill in ((cb, BARRED), (cb16, BIG)):
                pool.affine_select(out=m[:, :], in_=m[:, :], compare_op=ALU.is_ge, fill=fill, base=0,
                                   pattern=[[-1, P]], channel_multiplier=1)
            b8v = b8[:, :]
            pool.affine_select(out=b8v, in_=b8v, compare_op=ALU.is_ge, fill=0.0, base=0,
                               pattern=[[-8, DEC_B], [0, DEC_T]], channel_multiplier=1).then_inc(boxed, 1)
            pool.wait_ge(boxed, 1)
            pool.affine_select(out=b8v, in_=b8v, compare_op=ALU.is_ge, fill=0.0, base=7,
                               pattern=[[8, DEC_B], [0, DEC_T]], channel_multiplier=-1).then_inc(boxed, 1)
            pool.wait_ge(boxed, 2)
            pool.affine_select(out=u8[:, :], in_=b8v, compare_op=ALU.is_gt, fill=0.0, base=0,
                               pattern=[[1, NS]], channel_multiplier=-1).then_inc(boxed, 1)

        @block.tensor
        def _(pe):
            transposes_pe(pe, nc, jobs, ident, bank, None, evicted, turned)

        @block.scalar
        def _(act):
            for t, (t0, w) in enumerate(TT):
                act.dma_start(xin[0:w, t, :], x_rows[t] if t < 8 else s_rows).then_inc(x_loaded[t], 16)
            transposes_evict(act, act.copy, jobs, 0, bank, turned, evicted)

        @block.vector
        def _(dve):
            dve.memset(ones_half[:, :], 0.0).then_inc(zeroed, 1)
            dve.wait_ge(zeroed, 1)
            dve.memset(ones_half[0:DH, 0:DH], 1.0).then_inc(made, 1)
            dve.memset(ones_half[DH:P, DH:P], 1.0).then_inc(made, 1)
            dve.wait_ge(boxed, 3)
            dve.wait_ge(made, 5)
            dve.tensor_copy(misc["spread"][DH:DH + H, :].rearrange("p (h t) -> p h t", h=H),
                            ident[DH:DH + H, DH:DH + H].unsqueeze(2).to_broadcast([H, H, DEC_T]))
            dve.tensor_reduce(t8[:, :], ident[0:NS, 0:NS].rearrange("p (b t) -> p t b", b=DEC_B), AX.X, ALU.add)
            dve.tensor_reduce(cb8[:, :], u8[:, :].rearrange("p (b t) -> p t b", b=DEC_B), AX.X,
                              ALU.add).then_inc(zeroed, 1)
            dve.wait_ge(zeroed, 2)
            dve.tensor_scalar(cb8[:, :], cb8[:, :], BARRED, None, ALU.mult)
            transposes_evict(dve, dve.tensor_copy, jobs, 1, bank, turned, evicted)


def results(nc, sem, mem, bank, x, ident, O):
    rows = mem.at("rows", [P, 9, D], F32, AT_A)
    turned = sem("y_turned")
    evicted = [sem("y_evicted_act"), sem("y_evicted_dve")]
    written = sem("y_written")
    y_rows = O["y_prompt"][0].rearrange("(t p) d -> t p d", p=P)
    s_rows = O["y_sample"].rearrange("b t d -> (b t) d")
    jobs = [dict(src=[x[:, 4 * half + q, t0:t0 + w] for q in range(4)], step=P,
                 dst=rows[0:w, t, half * 512:(half + 1) * 512], psum=lambda b, w=w: b[0:w, :], needs=[])
            for t, (t0, w) in enumerate(TT) for half in range(2)]

    with nc.Block() as block:
        @block.tensor
        def _(pe):
            transposes_pe(pe, nc, jobs, ident, bank, None, evicted, turned)

        @block.scalar
        def _(act):
            transposes_evict(act, act.copy, jobs, 0, bank, turned, evicted)

        @block.vector
        def _(dve):
            transposes_evict(dve, dve.tensor_copy, jobs, 1, bank, turned, evicted)

        @block.sync
        def _(sp):
            for t, (t0, w) in enumerate(TT):
                sp.wait_ge(evicted[0], t + 1)
                sp.wait_ge(evicted[1], t + 1)
                sp.dma_start(y_rows[t] if t < 8 else s_rows, rows[0:w, t, :]).then_inc(written, 16)
            sp.wait_ge(written, 16 * len(TT))


class Indexer:

    def __init__(self):
        self.order = [7, 6, 5, 4, 3, 2, "S"]
        window = {7: (15, 25), 6: (26, 44), 5: (44, 60), 4: (60, 73), 3: (73, 83), 2: (83, 91)}
        self.jobs = []
        self.slots = {}
        self.of_block = {}
        for i in (7, 6, 5, 4, 3, 2):
            keys = (i + 1) * P
            mine = [(i, h, k0, min(512, keys - k0)) for h in range(H) for k0 in range(0, keys, 512)]
            a, b = window[i]
            self.of_block[i] = range(len(self.jobs), len(self.jobs) + len(mine))
            for n, job in enumerate(mine):
                self.slots.setdefault(a + n * (b - a) // len(mine), []).append(len(self.jobs))
                self.jobs.append(job)
        self.sample_first = 15
        self.sample_jobs = 4 * DEC_B

    def sample_step(self, q):
        s = q - self.sample_first
        return s // 2 if s >= 0 and s % 2 == 0 else -1 - self.sample_jobs


V_TILES = ((0, 4), (4, 8), (8, 9))


def bias_at(i):
    return i * (i + 1) // 2 * P


def mixing_inputs(nc, sem, mem, bank, norm, x, x_kept, h_hi, h_lo, raw, w_hi, w_lo, ident, I, O, scratch, bias, bias_s, rep, misc):
    w_in = I["w_in"][0].rearrange("(k p) n -> p k n", p=P)
    ix = Indexer()
    units = [("kw", 0, C_KI)] + [("qi", j, C_QI + j * P) for j in range(4)]
    for kind, col, n in (("lx", C_LX, 4), ("lg", C_LG, 4), ("q", C_Q, 4), ("k", C_K, 4), ("qm", C_QM, 4),
                         ("g", C_G, 24), ("v", C_V, 4)):
        units += [(kind, j, col + j * P) for j in range(n)]
    N = len(units)
    first_free = [n for n, (kind, _, _) in enumerate(units) if kind not in ("kw", "qi")][0]
    staged = [n for n in range(N) if n >= first_free]

    at = AT_X
    def place(name, shape, dt, size):
        nonlocal at
        t = mem.at(name, shape, dt, at)
        at += (size + 31) // 32 * 32
        assert at <= AT_B
        return t
    qi = place("qi", [P, 4, NT], F32, 4 * NT * 4)
    kw = place("kw", [P, NT], F32, NT * 4)
    ki2 = place("ki2", [P, NT], F32, NT * 4)
    kw_rows = place("kw_rows", [P, 9, DH + H], F32, 9 * (DH + H) * 4)
    stage = place("stage", [P, 2, 9 * P], F32, 2 * 9 * P * 4)
    S = place("S", [P, 2, SEQ], F32, 2 * SEQ * 4)
    S_s = place("S_s", [NS, PAST + DEC_T], F32, (PAST + DEC_T) * 4)
    relu = place("relu", [P, 4, 512], F32, 4 * 2048)
    relu_s = place("relu_s", [NS, 2, 512], F32, 2 * 2048)
    kx = place("kx", [P, 8, 4, DH], F32, 8 * 4 * DH * 4)
    kxT = place("kxT", [P, 2, 2, P], F32, 2 * 2 * P * 4)
    qi_s = place("qi_s", [P, 2, DEC_B, H, DEC_T], F32, 2 * DEC_B * NS * 4)
    wsel = place("wsel", [NS, DEC_B, NS], F32, DEC_B * NS * 4)
    qi_x = place("qi_x", [P, 4, NS], F32, 4 * NS * 4)
    top8 = place("top8", [P, 8], F32, 32)
    table = place("table", [1, DEC_B * PAGES], I32, DEC_B * PAGES * 4)
    cb, cb16, t8, cb8, b8 = misc["cb"], misc["cb16"], misc["t8"], misc["cb8"], misc["b8"]

    loaded = [sem(f"mix_loaded{i}") for i in range(3)]
    high, low = sem("mix_high"), sem("mix_low")
    ready = sem("mix_ready")
    evicted = sem("mix_evicted")
    stored = [sem(f"mix_stored{i}") for i in range(2)]
    kw_turned, kw_copied, kw_moved = sem("kw_turned"), sem("kw_copied"), sem("kw_moved")
    table_loaded = sem("table_loaded")
    kx_loaded = [sem(f"kx_loaded{i}") for i in range(8)]
    kx_turned, kx_copied = sem("kx_turned"), sem("kx_copied")
    sdots, srelu, ssum = sem("sdots"), sem("srelu"), sem("ssum")
    wsel_made = sem("wsel_made")
    v_turned, v_copied = sem("v_turned"), sem("v_copied")
    qi_placed = sem("qi_placed")
    weighed = sem("weighed")
    dots, relued, summed = sem("idx_dots"), sem("idx_relu"), sem("idx_sum")
    s_evicted = sem("s_evicted")
    sel = sem("selection")
    masked = sem("masked")

    def dst_of(n):
        kind, j, _ = units[n]
        s = (n - first_free) % 2
        if kind == "v":
            full = stage[:, s, :].rearrange("p (t c) -> p t c", c=P)
            vp = O["new_v_prompt"][0, 0].rearrange("(t p) h d -> p t (h d)", p=P)
            vs = O["new_v_sample"][0].rearrange("b t h d -> (b t) (h d)")
            return [(vp[:, :, j * P:(j + 1) * P], full[:, 0:8, :]),
                    (vs[:, j * P:(j + 1) * P], stage[0:NS, s, 8 * P:9 * P])]
        return [(scratch[kind][j], stage[:, s, 0:NT])]

    stores_before = []
    counts = [0, 0]
    for n in staged:
        s = (n - first_free) % 2
        stores_before.append(counts[s])
        counts[s] += len(dst_of(n))

    kept = sem("kept")

    with nc.Block() as block:
        @block.sync
        def _(sp):
            sp.dma_start(x_kept, x[:, :, :]).then_inc(kept, 16)
            def store(n):
                for dst, src in dst_of(n):
                    sp.dma_start(dst, src).then_inc(stored[(n - first_free) % 2], 16)

            for n in range(N + 3):
                if n < N:
                    if n >= 3:
                        sp.wait_ge(low, n - 2)
                    sp.dma_start(raw[:, n % 3, :].rearrange("p (k c) -> p k c", k=KT),
                                 w_in[:, :, units[n][2]:units[n][2] + P]).then_inc(loaded[n % 3], 16)
                if n == 5:
                    sp.wait_ge(evicted, 3)
                    sp.dma_start(ki2[DH:P, :], kw[0:DH, :]).then_inc(kw_moved, 16)
                    sp.wait_ge(kw_copied, 9)
                    sp.dma_start(O["new_kidx_prompt"][0, 0].rearrange("(t p) d -> p t d", p=P),
                                 kw_rows[:, 0:8, 0:DH]).then_inc(kw_moved, 16)
                    sp.dma_start(O["new_kidx_sample"][0].rearrange("b t d -> (b t) d"),
                                 kw_rows[0:NS, 8, 0:DH]).then_inc(kw_moved, 16)
                if n == 6:
                    sp.wait_ge(evicted, 15)
                    for half in range(2):
                        o = (1 - half) * DH
                        sp.dma_start(qi_x[half * DH:(half + 1) * DH, :, :], qi[o:o + DH, :, SEQ:NT]
                                     ).then_inc(kw_moved, 16)
                if n - 3 >= first_free:
                    kind, j, _ = units[n - 3]
                    if kind == "v":
                        sp.wait_ge(v_copied, 3 * (j + 1))
                    else:
                        sp.wait_ge(evicted, 3 * (n - 2))
                    store(n - 3)
            for s in range(2):
                sp.wait_ge(stored[s], 16 * counts[s])
            sp.wait_ge(kw_moved, 16 * (1 + 2 + 2))

        @block.gpsimd
        def _(pool):
            pool.dma_start(table[:, :], I["page_table"].rearrange("b g -> (b g)").rearrange(
                "(a n) -> a n", a=1)).then_inc(table_loaded, 16)

            def kidx_pages(job):
                c, b = divmod(job, DEC_B)
                if job >= 8:
                    pool.wait_ge(kx_turned, job - 7)
                for g in range(4):
                    at = b * PAGES + 4 * c + g
                    page = pool.value_load(table[0:1, at:at + 1], min_val=0,
                                         max_val=I["cache_kidx"].shape[1] - 1)
                    pool.dma_start(kx[:, job % 8, g, :],
                                 I["cache_kidx"][0][bass.ds(page, 1)].rearrange("a p d -> p (a d)")
                                 ).then_inc(kx_loaded[job % 8], 16)

            for n in range(N):
                if n == 2:
                    norm.on_pool(pool)
                    pool.wait_ge(kept, 16)
                pool.wait_ge(high, n + 1)
                pool.tensor_tensor(w_lo[:, n % 3, :], raw[:, n % 3, :], w_hi[:, n % 3, :].bitcast(F32),
                                   ALU.subtract).then_inc(low, 1)
                if n == 2:
                    pool.wait_ge(table_loaded, 16)
                if 2 <= n < 6:
                    for job in range(2 * (n - 2), 2 * (n - 1)):
                        kidx_pages(job)
                if 7 <= n:
                    for job in range(8 + 3 * (n - 7) // 2, min(8 + 3 * (n - 6) // 2, ix.sample_jobs)):
                        kidx_pages(job)

        @block.tensor
        def _(pe):
            def sample_turn(job):
                pe.wait_ge(kx_loaded[job % 8], 64 * (job // 8 + 1))
                if job == 0:
                    pe.wait_ge(wsel_made, DEC_B)
                else:
                    pe.wait_ge(kx_copied, job)
                for g in range(2):
                    mm = pe.transpose(bank[7][:, g * P:(g + 1) * P],
                                      kx[:, job % 8, 2 * g:2 * g + 2, :].rearrange("p g d -> p (g d)"), ident[:, :])
                mm.then_inc(kx_turned, 1)

            def sample_dots(job):
                b = job % DEC_B
                pe.wait_ge(kx_copied, job + 1)
                if job == 0:
                    pe.wait_ge(qi_placed, 2 * H)
                else:
                    pe.wait_ge(srelu, job)
                for g in range(4):
                    mm = pe.matmul(bank[6][0:NS, g * P:(g + 1) * P],
                                   qi_s[:, g % 2, b, :, :].rearrange("p h t -> p (h t)"),
                                   kxT[:, job % 2, g // 2, :], start=True, stop=True)
                mm.then_inc(sdots, 1)

            def sample_sum(job):
                c, b = divmod(job, DEC_B)
                pe.wait_ge(srelu, job + 1)
                if job == 0:
                    pe.wait_ge(wsel_made, DEC_B)
                elif b == 0:
                    pe.wait_ge(s_evicted, c)
                pe.matmul(bank[5][0:NS, :], wsel[:, b, :], relu_s[:, job % 2, :], start=(b == 0),
                          stop=(b == DEC_B - 1)).then_inc(ssum, 1)

            def new_dots():
                pe.wait_ge(srelu, ix.sample_jobs)
                for b in range(DEC_B):
                    mm = pe.matmul(bank[6][0:NS, 8 * b:8 * b + 8], qi_s[0:DH, 0, b, :, :].rearrange("p h t -> p (h t)"),
                                   kw[0:DH, SEQ + 8 * b:SEQ + 8 * b + 8], start=True, stop=True)
                mm.then_inc(sdots, 1)

            def new_sum():
                pe.wait_ge(srelu, ix.sample_jobs + 1)
                pe.wait_ge(s_evicted, 4)
                for b in range(DEC_B):
                    mm = pe.matmul(bank[5][0:NS, 0:DEC_T], wsel[:, b, :], relu_s[:, 0, 8 * b:8 * b + 8],
                                   start=(b == 0), stop=(b == DEC_B - 1))
                mm.then_inc(ssum, 1)

            def prompt_dots(m):
                i, h, k0, w = ix.jobs[m]
                r = (h % 2) * DH
                if m >= 2:
                    pe.wait_ge(relued, m - 1)
                if m == 0:
                    pe.wait_ge(kw_moved, 16 * (1 + 2 + 2))
                keys = (kw if r == 0 else ki2)[r:r + DH, k0:k0 + w]
                pe.matmul(bank[3 + m % 2][:, 0:w], qi[r:r + DH, h // 2, i * P:(i + 1) * P], keys,
                          start=True, stop=True).then_inc(dots, 1)

            def turn_v(n):
                j = units[n][1]
                pe.wait_ge(evicted, 3 * (n + 1))
                if j == 0:
                    pe.wait_ge(relued, len(ix.jobs))
                    pe.wait_ge(s_evicted, 5)
                else:
                    pe.wait_ge(v_copied, 3 * j)
                for g, (a, b) in enumerate(V_TILES):
                    for t in range(a, b):
                        t0, w = TT[t]
                        mm = pe.transpose(bank[3 + g][0:w, (t - a) * P:(t - a + 1) * P], qi[:, j, t0:t0 + w],
                                          ident[:, :])
                    mm.then_inc(v_turned, 1)

            norm.on_pe(pe)
            for n, (kind, j, _) in enumerate(units):
                pe.wait_ge(low, n + 1)
                hi = lambda k, n=n: w_hi[:, n % 3, k * P:(k + 1) * P]
                lo = lambda k, n=n: w_lo[:, n % 3, k * P:(k + 1) * P]
                for c, (t0, w) in enumerate(CH):
                    q = 3 * n + c
                    if n == 0:
                        pe.wait_ge(norm.low, KT * (c + 1))
                    if q >= 3:
                        pe.wait_ge(evicted, q - 2)
                    ks = [(k, k) for k in range(KT)]
                    mm = products(pe, bank[c][:, 0:w], hi, lo, lambda k: h_hi[:, k, t0:t0 + w],
                                  lambda k: h_lo[:, k, t0:t0 + w], ks, True, True)
                    mm.then_inc(ready, 1)
                    if n == 1 and c == 0:
                        pe.wait_ge(evicted, 3)
                        for t, (a, rows) in enumerate(TT):
                            if t % 2 == 0 and t >= 4:
                                pe.wait_ge(kw_copied, t - 2)
                            pe.transpose(bank[3 + t % 4][0:rows, 0:P], kw[:, a:a + rows],
                                         ident[:, :]).then_inc(kw_turned, 1)
                        pe.matmul(bank[7][0:NS, 0:NS], misc["spread"][DH:DH + H, :], kw[DH:DH + H, SEQ:NT], start=True, stop=True).then_inc(kw_turned, 1)
                    s = ix.sample_step(q)
                    if 0 <= s - 2 < ix.sample_jobs:
                        sample_sum(s - 2)
                    if s - 2 == ix.sample_jobs:
                        new_sum()
                    if 0 <= s - 1 < ix.sample_jobs:
                        sample_dots(s - 1)
                    if s - 1 == ix.sample_jobs:
                        new_dots()
                    if 0 <= s < ix.sample_jobs:
                        sample_turn(s)
                    for m in ix.slots.get(q, []):
                        prompt_dots(m)
                    if c == 0 and n >= 1 and units[n - 1][0] == "v":
                        turn_v(n - 1)
            turn_v(N - 1)

        @block.scalar
        def _(act):
            def high_part(n):
                act.wait_ge(loaded[n % 3], 16 * (n // 3 + 1))
                if n >= 3:
                    act.wait_ge(ready, 3 * (n - 2))
                act.copy(w_hi[:, n % 3, :], raw[:, n % 3, :]).then_inc(high, 1)

            def v_rows(n):
                j, m = units[n][1], n - first_free
                act.wait_ge(stored[m % 2], 16 * stores_before[m])
                for g, (a, b) in enumerate(V_TILES):
                    rows = P if b <= 8 else NS
                    act.wait_ge(v_turned, 3 * j + g + 1)
                    act.copy(stage[0:rows, m % 2, a * P:b * P], bank[3 + g][0:rows, 0:(b - a) * P]
                             ).then_inc(v_copied, 1)

            norm.squares(act)
            high_part(0)
            high_part(1)
            norm.roots(act)
            act.wait_ge(norm.low, KT * len(CH))
            act.wait_ge(kept, 16)
            for n, (kind, j, _) in enumerate(units):
                if n + 2 < N:
                    high_part(n + 2)
                for c, (t0, w) in enumerate(CH):
                    q = 3 * n + c
                    act.wait_ge(ready, q + 1)
                    if kind == "kw":
                        dst, src, f = kw[:, t0:t0 + w], bank[c][:, 0:w], ACT.Copy
                    elif kind in ("qi", "v"):
                        dst, src, f = qi[:, j, t0:t0 + w], bank[c][:, 0:w], ACT.Copy
                    else:
                        m = n - first_free
                        if c == 0 and m >= 2:
                            act.wait_ge(stored[m % 2], 16 * (stores_before[m]))
                        f = {"g": ACT.Sigmoid, "lg": ACT.Gelu_apprx_tanh}.get(kind, ACT.Copy)
                        dst, src = stage[:, m % 2, t0:t0 + w], bank[c][:, 0:w]
                    if f == ACT.Copy:
                        act.copy(dst, src).then_inc(evicted, 1)
                    else:
                        act.activation(dst, src, f).then_inc(evicted, 1)
                    if n == 1 and c == 0:
                        for t, (a, rows) in enumerate(TT):
                            act.wait_ge(kw_turned, t + 1)
                            act.copy(kw_rows[0:rows, t, :], bank[3 + t % 4][0:rows, 0:DH + H]).then_inc(kw_copied, 1)
                    s = ix.sample_step(q)
                    if 0 <= s - 1 < ix.sample_jobs + 1:
                        job = s - 1
                        act.wait_ge(sdots, job + 1)
                        if job >= 2:
                            act.wait_ge(ssum, job - 1)
                        w2 = 512 if job < ix.sample_jobs else NS
                        act.activation(relu_s[:, job % 2, 0:w2], bank[6][0:NS, 0:w2], ACT.Relu).then_inc(srelu, 1)
                    if 0 <= s - 2 <= ix.sample_jobs and (s - 2) % DEC_B == DEC_B - 1 or s - 2 == ix.sample_jobs:
                        c4 = (s - 2) // DEC_B
                        w4 = 512 if c4 < 4 else DEC_T
                        act.wait_ge(ssum, s - 1)
                        act.copy(S_s[:, c4 * 512:c4 * 512 + w4], bank[5][0:NS, 0:w4]).then_inc(s_evicted, 1)
                    if 0 <= s < ix.sample_jobs:
                        act.wait_ge(kx_turned, s + 1)
                        if s >= 2:
                            act.wait_ge(sdots, s - 1)
                        act.copy(kxT[:, s % 2, :, :].rearrange("p g n -> p (g n)"),
                                 bank[7][:, 0:2 * P]).then_inc(kx_copied, 1)
                    for m in ix.slots.get(q, []):
                        w2 = ix.jobs[m][3]
                        act.wait_ge(dots, m + 1)
                        if m >= 4:
                            act.wait_ge(summed, m - 3)
                        act.activation(relu[:, m % 4, 0:w2], bank[3 + m % 2][:, 0:w2], ACT.Relu).then_inc(relued, 1)
                    if c == 0 and n >= 1 and units[n - 1][0] == "v":
                        v_rows(n - 1)
            v_rows(N - 1)

        @block.vector
        def _(dve):
            steps = [0]

            def after(ins):
                ins.then_inc(sel, 1)
                steps[0] += 1

            norm.on_dve(dve)
            dve.wait_ge(norm.low, KT * len(CH))
            dve.wait_ge(kept, 16)
            scale = H ** -0.5 * DH ** -0.5
            dve.memset(qi_s[:, :, :, :, :], 0.0).then_inc(weighed, 1)
            dve.memset(wsel[:, :, :], 0.0).then_inc(weighed, 1)
            dve.wait_ge(kw_copied, 9)
            dve.tensor_scalar(kw_rows[:, 0:8, DH:DH + H], kw_rows[:, 0:8, DH:DH + H], scale, None,
                              ALU.mult).then_inc(weighed, 1)
            dve.wait_ge(kw_turned, 10)
            dve.wait_ge(weighed, 3)
            for b in range(DEC_B):
                dve.scalar_tensor_tensor(wsel[:, b, 8 * b:8 * b + 8], bank[7][0:NS, 8 * b:8 * b + 8], scale,
                                         t8[:, :], ALU.mult, ALU.mult).then_inc(wsel_made, 1)
            for i in range(2):
                if i:
                    dve.memset(bias[:, bias_at(i):bias_at(i) + i * P], 0.0)
                dve.tensor_copy(bias[:, bias_at(i) + i * P:bias_at(i + 1)], cb16[:, :])

            dve.wait_ge(evicted, 15)
            dve.wait_ge(kw_moved, 16 * (1 + 2 + 2))
            dve.wait_ge(weighed, 2)
            for h in range(H):
                for half in range(2):
                    rows = slice(half * DH, (half + 1) * DH)
                    src = qi[rows, h // 2, SEQ:NT] if h % 2 == half else qi_x[rows, h // 2, :]
                    dve.tensor_copy(qi_s[half * DH:(half + 1) * DH, half, :, h, :],
                                    src.rearrange("p (b t) -> p b t", b=DEC_B)).then_inc(qi_placed, 1)

            def add_head(i, m):
                _, h, k0, w = ix.jobs[m]
                dst = S[:, i % 2, k0:k0 + w]
                weight = kw_rows[:, i, DH + h:DH + h + 1]
                dve.wait_ge(relued, m + 1)
                if h == 0:
                    ins = dve.tensor_scalar(dst, relu[:, m % 4, 0:w], weight, None, ALU.mult)
                else:
                    dve.wait_ge(summed, m - (ix.of_block[i][-1] + 1 - ix.of_block[i][0]) // H + 1)
                    ins = dve.scalar_tensor_tensor(dst, relu[:, m % 4, 0:w], weight, dst, ALU.mult, ALU.add)
                ins.then_inc(summed, 1)

            def bar(i):
                dve.wait_ge(summed, ix.of_block[i][-1] + 1)
                d = S[:, i % 2, i * P:(i + 1) * P]
                after(dve.tensor_tensor(d, d, cb[:, :], ALU.add))

            def sample_bar():
                dve.wait_ge(s_evicted, 5)
                new = S_s[:, PAST:PAST + DEC_T]
                after(dve.tensor_tensor(new, new, cb8[:, :], ALU.add))

            def add_jobs(p):
                if p == "S":
                    return [(sample_bar, ())]
                return [(add_head, (p, m)) for m in ix.of_block[p]] + [(bar, (p,))]

            for f, args in add_jobs(ix.order[0]):
                f(*args)
            for n, p in enumerate(ix.order):
                scores = S_s[:, :] if p == "S" else S[:, p % 2, 0:(p + 1) * P]
                rows = NS if p == "S" else P
                following = add_jobs(ix.order[n + 1]) if n + 1 < len(ix.order) else []
                rounds = TOPK // 8
                for r in range(rounds):
                    if steps[0]:
                        dve.wait_ge(sel, steps[0])
                    after(dve.max(top8[0:rows, :], scores))
                    dve.wait_ge(sel, steps[0])
                    after(dve.match_replace(scores, top8[0:rows, :], scores, TAKEN))
                    for f, args in following[len(following) * r // rounds:len(following) * (r + 1) // rounds]:
                        f(*args)
                dve.wait_ge(sel, steps[0])
                dst = bias_s[:, :] if p == "S" else bias[:, bias_at(p):bias_at(p + 1)]
                after(dve.tensor_scalar(dst, scores, BARRED * 1.25, BIG, ALU.is_gt, ALU.mult))
            for b in range(DEC_B):
                dve.tensor_scalar(rep[:, b, :].rearrange("p (h t) -> p h t", h=H),
                                  t8[:, :].unsqueeze(1).to_broadcast([NS, H, DEC_T]), b8[:, 8 * b:8 * b + 1], None,
                                  ALU.mult)
            dve.wait_ge(sel, steps[0])


def head_norms(nc, sem, mem, bank, ident, ones, ones_half, column, qT, kT, qmT, O, scratch):
    tiles = [("k", j) for j in range(4)] + [("q", j) for j in range(4)] + [("qm", j) for j in range(4)]
    N = len(tiles)
    R = 2 * N
    sq = mem.at("hsq", [P, 2, NT], F32, AT_X + 8192)
    rs = mem.at("hrs", [R, NT], F32, AT_X + 8192 + 2 * NT * 4)
    rows = mem.at("k_rows", [P, 2, 9, P], F32, AT_X + 8192 + 4 * NT * 4)
    gains = mem.at("gains", [P, 4], F32, AT_X + 8192 + 4 * NT * 4 + 2 * 9 * P * 4)
    eps = mem.at("head_eps", [R, 1], F32, AT_X + 8192 + 4 * NT * 4 + 2 * 9 * P * 4 + 32)
    gather = mem.at("gather", [P, N, R], F32, AT_X + 8192 + 4 * NT * 4 + 2 * 9 * P * 4 + 64)
    spread = mem.at("head_spread", [R, N, P], F32, AT_X + 8192 + 4 * NT * 4 + 2 * 9 * P * 4 + 64 + N * R * 4)
    place = {"k": kT, "q": qT, "qm": qmT}
    loaded = [sem(f"head_loaded{n}") for n in range(N)]
    cleared, set_up, squared, summed = sem("head_cleared"), sem("head_set"), sem("head_squared"), sem("head_summed")
    rooted, inverted, sent, normed = sem("head_rooted"), sem("head_inverted"), sem("head_sent"), sem("head_normed")
    turned, evicted = sem("k_turned"), sem("k_evicted")
    stored = [sem("k_stored0"), sem("k_stored1")]
    SETS = 1 + 1 + 2 + 3

    with nc.Block() as block:
        @block.sync
        def _(sp):
            for n, (kind, j) in enumerate(tiles):
                sp.dma_start(place[kind][:, j, :], scratch[kind][j]).then_inc(loaded[n], 16)
            kp = O["new_k_prompt"][0, 0].rearrange("(t p) h d -> p t (h d)", p=P)
            ks = O["new_k_sample"][0].rearrange("b t h d -> (b t) (h d)")
            for j in range(4):
                sp.wait_ge(evicted, 3 * (j + 1))
                sp.dma_start(kp[:, :, j * P:(j + 1) * P], rows[:, j % 2, 0:8, :]).then_inc(stored[j % 2], 16)
                sp.dma_start(ks[:, j * P:(j + 1) * P], rows[0:NS, j % 2, 8, :]).then_inc(stored[j % 2], 16)
            for s in range(2):
                sp.wait_ge(stored[s], 64)

        @block.scalar
        def _(act):
            for n, (kind, j) in enumerate(tiles):
                act.wait_ge(loaded[n], 16)
                if n >= 2:
                    act.wait_ge(summed, n - 1)
                act.activation(sq[:, n % 2, :], place[kind][:, j, :], ACT.Square).then_inc(squared, 1)
            act.wait_ge(summed, N)
            act.wait_ge(set_up, SETS)
            for c, (t0, w) in enumerate(CH):
                act.activation(rs[:, t0:t0 + w], bank[c][0:R, 0:w], ACT.Sqrt, bias=eps[:, 0:1]).then_inc(rooted, 1)
            for j in range(4):
                if j >= 2:
                    act.wait_ge(stored[j % 2], 32)
                for g, (a, b) in enumerate(V_TILES):
                    act.wait_ge(turned, 3 * j + g + 1)
                    r = P if g < 2 else NS
                    act.copy(rows[0:r, j % 2, a:b, :], bank[6 + (3 * j + g) % 2][0:r, 0:(b - a) * P].rearrange(
                        "p (t c) -> p t c", c=P)).then_inc(evicted, 1)

        @block.tensor
        def _(pe):
            pe.wait_ge(set_up, SETS)
            for n in range(N):
                pe.wait_ge(squared, n + 1)
                for c, (t0, w) in enumerate(CH):
                    mm = pe.matmul(bank[c][0:R, 0:w], gather[:, n, :], sq[:, n % 2, t0:t0 + w], start=(n == 0),
                                   stop=(n == N - 1))
                mm.then_inc(summed, 1)
            for n in range(N + 1):
                if n < N:
                    for c, (t0, w) in enumerate(CH):
                        q = 3 * n + c
                        if n == 0:
                            pe.wait_ge(inverted, c + 1)
                        if q >= 6:
                            pe.wait_ge(normed, q - 5)
                        pe.matmul(bank[q % 6][:, 0:w], spread[:, n, :], rs[:, t0:t0 + w], start=True,
                                  stop=True).then_inc(sent, 1)
                if 1 <= n <= 4:
                    m = n - 1
                    pe.wait_ge(normed, 3 * (m + 1))
                    for g, (a, b) in enumerate(V_TILES):
                        if 3 * m + g >= 2:
                            pe.wait_ge(evicted, 3 * m + g - 1)
                        for t in range(a, b):
                            t0, w = TT[t]
                            mm = pe.transpose(bank[6 + (3 * m + g) % 2][0:w, (t - a) * P:(t - a + 1) * P],
                                              kT[:, m, t0:t0 + w], ident[:, :])
                        mm.then_inc(turned, 1)

        @block.vector
        def _(dve):
            dve.memset(gather[:, :, :], 0.0).then_inc(cleared, 1)
            dve.memset(eps[:, :], EPS).then_inc(set_up, 1)
            dve.tensor_scalar(gains[:, 0:1], column("gq"), DH ** -0.5, None, ALU.mult).then_inc(set_up, 1)
            dve.tensor_scalar(gains[:, 1:2], column("gmq"), P ** -0.5, None, ALU.mult).then_inc(set_up, 1)
            dve.wait_ge(cleared, 1)
            for n, (kind, j) in enumerate(tiles):
                for e in range(2):
                    if kind == "qm":
                        ins = dve.memset(gather[:, n, 2 * n + e:2 * n + e + 1], 1.0 / P)
                    else:
                        ins = dve.memset(gather[e * DH:(e + 1) * DH, n, 2 * n + e:2 * n + e + 1], 1.0 / DH)
            ins.then_inc(set_up, 1)
            dve.tensor_copy(spread[:, :, :].rearrange("r n (e p) -> r (n e) p", e=2),
                            ident[0:R, 0:R].unsqueeze(2).to_broadcast([R, R, DH])).then_inc(set_up, 3)
            dve.wait_ge(set_up, SETS)
            for c, (t0, w) in enumerate(CH):
                dve.wait_ge(rooted, c + 1)
                dve.reciprocal(rs[:, t0:t0 + w], rs[:, t0:t0 + w]).then_inc(inverted, 1)
            for n, (kind, j) in enumerate(tiles):
                gain = {"k": column("gk"), "q": gains[:, 0:1], "qm": gains[:, 1:2]}[kind]
                dve.wait_ge(squared, n + 1)
                for c, (t0, w) in enumerate(CH):
                    q = 3 * n + c
                    dve.wait_ge(sent, q + 1)
                    t = place[kind][:, j, t0:t0 + w]
                    dve.scalar_tensor_tensor(t, t, gain, bank[q % 6][:, 0:w], ALU.mult, ALU.mult
                                             ).then_inc(normed, 1)


def recurrence(nc, sem, mem, bank, ident, column, mk, I, O, scratch):
    at = AT_A
    def place(name, shape, size):
        nonlocal at
        t = mem.at(name, shape, F32, at)
        at += (size + 31) // 32 * 32
        assert at <= AT_B
        return t
    XP = 3 + SEQ
    xp = place("xp", [P, 2, XP], 2 * XP * 4)
    xs = place("xs", [P, 2, DEC_B, 3 + DEC_T], 2 * 88 * 4)
    conv2 = place("conv", [P, 2, NT], 2 * NT * 4)
    r2 = place("r", [P, 2, NT], 2 * NT * 4)
    a2 = place("a", [P, 2, NT], 2 * NT * 4)
    hh = place("hh", [P, NT], NT * 4)
    gl = place("gl", [P, 2, NT], 2 * NT * 4)
    wab = place("wab", [P, 2, 4, P], 8 * P * 4)
    at = AT_H + 8 * 4096
    ig2 = place("ig", [P, 2, NT], 2 * NT * 4)
    th2 = place("th", [P, 2, NT], 2 * NT * 4)
    assert at <= AT_W
    at = AT_X + 8192
    h0a = place("h0a", [P, DEC_B], DEC_B * 4)
    states = place("states", [P, LT * 24], LT * 24 * 4)
    state = place("state", [24, LRU_W], LRU_W * 4)
    tail = place("tail", [P, LT, 36], LT * 36 * 4)
    tails = place("tails", [36, LRU_W], LRU_W * 4)
    sp4 = place("sp4", [P, 8, LT], 8 * LT * 4)
    x_in = [sem("lx_in0"), sem("lx_in1")]
    gl_in = [sem("lg_in0"), sem("lg_in1")]
    x_used = sem("lx_used")
    w_in, w_zero = sem("lru_w_in"), sem("lru_w_zero")
    state_in, state_turned, state_out = sem("state_in"), sem("state_turned"), sem("state_out")
    lam1, lam = sem("lam_exp"), sem("lam")
    step = sem("lru_step")
    conv_done, gates, gated, powers, rooted, y_done, y_out = (sem("conv_done"), sem("lru_gates"), sem("lru_gated"),
                                                              sem("lru_powers"), sem("lru_rooted"), sem("y_done"),
                                                              sem("y_out"))
    squares, states_copied = sem("lru_squares"), sem("states_copied")
    tail_turned, tail_copied, tail_out = sem("tail_turned"), sem("tail_copied"), sem("tail_out")

    with nc.Block() as block:
        @block.sync
        def _(sp):
            sp.wait_ge(w_zero, 1)
            for g, name in enumerate(("lru_wa", "lru_wi")):
                w = I[name][0].rearrange("(j e) i o -> e i j o", e=2)
                for e in range(2):
                    sp.dma_start(wab[e * DH:(e + 1) * DH, g, :, e * DH:(e + 1) * DH], w[e]).then_inc(w_in, 16)
            sp.dma_start(state[:, :], I["state_conv"][0].rearrange("b s c -> (b s) c")).then_inc(state_in, 16)
            for j in range(LT + 2):
                if j < LT:
                    if j >= 2:
                        sp.wait_ge(x_used, j - 1)
                    sp.dma_start(xp[:, j % 2, 3:XP], scratch["lx"][j][:, 0:SEQ]).then_inc(x_in[j % 2], 16)
                    sp.dma_start(xs[:, j % 2, :, 3:3 + DEC_T], scratch["lx"][j][:, SEQ:NT].rearrange(
                        "p (b t) -> p b t", b=DEC_B)).then_inc(x_in[j % 2], 16)
                if 1 <= j <= LT:
                    if j >= 3:
                        sp.wait_ge(y_done, j - 2)
                    sp.dma_start(gl[:, (j - 1) % 2, :], scratch["lg"][j - 1]).then_inc(gl_in[(j - 1) % 2], 16)
                if j >= 2:
                    sp.wait_ge(y_done, j - 1)
                    sp.dma_start(scratch["y"][j - 2], hh[:, :]).then_inc(y_out, 16)
            sp.wait_ge(tail_copied, 1)
            sp.dma_start(O["new_conv_prompt"][0, 0], tails[0:3, :]).then_inc(tail_out, 16)
            sp.dma_start(O["new_conv_sample"][0].rearrange("b s c -> (b s) c"), tails[3:27, :]).then_inc(tail_out, 16)
            sp.dma_start(O["new_h_prompt"][0], tails[27:28, :]).then_inc(tail_out, 16)
            sp.dma_start(O["new_h_sample"][0], tails[28:36, :]).then_inc(tail_out, 16)
            sp.wait_ge(tail_out, 64)
            sp.wait_ge(y_out, 16 * LT)
            mk.store(sp)

        @block.gpsimd
        def _(pool):
            for n in range(3):
                mk.load(pool, n)
            for n in range(mk.N):
                mk.split_low(pool, n)
                if n + 3 < mk.N:
                    mk.load(pool, n + 3)

        @block.tensor
        def _(pe):
            pe.wait_ge(state_in, 16)
            for j in range(LT):
                mm = pe.transpose(bank[7][:, j * 24:(j + 1) * 24], state[:, j * P:(j + 1) * P], ident[0:24, 0:24])
            mm.then_inc(state_turned, 1)
            pe.wait_ge(w_in, 64)
            for j in range(LT):
                pe.wait_ge(conv_done, j + 1)
                if j >= 1:
                    pe.wait_ge(gated, 6 * j)
                for g in range(2):
                    for c, (t0, w) in enumerate(CH):
                        pe.matmul(bank[3 * g + c][:, 0:w], wab[:, g, j, :], conv2[:, j % 2, t0:t0 + w], start=True,
                                  stop=True).then_inc(gates, 1)
                if j == 0:
                    pe.wait_ge(states_copied, 1)
                for n in (2 * j, 2 * j + 1):
                    mk.multiply(pe, n)
                if j == 2:
                    mk.sums(pe)
            pe.wait_ge(gated, 6 * LT)
            mk.turn(pe)
            pe.wait_ge(y_done, LT)
            pe.wait_ge(mk.copied, mk.N)
            for j in range(LT):
                mm = pe.transpose(bank[6][0:36, j * P:(j + 1) * P], tail[:, j, :], ident[:, :])
            mm.then_inc(tail_turned, 1)

        @block.scalar
        def _(act):
            for n in range(2):
                mk.split_high(act, n)
            act.wait_ge(lam, 1)
            act.activation(sp4[:, 1, :], sp4[:, 0, :], ACT.Exp, scale=-1.0).then_inc(lam1, 1)
            for j in range(LT + 1):
                if j < LT:
                    r, ig, a, th = (t[:, j % 2, :] for t in (r2, ig2, a2, th2))
                    if j >= 2:
                        act.wait_ge(y_done, j - 1)
                    for g, (dst, b) in enumerate(((r, "ba"), (ig, "bi"))):
                        for c, (t0, w) in enumerate(CH):
                            act.wait_ge(gates, 6 * j + 3 * g + c + 1)
                            act.activation(dst[:, t0:t0 + w], bank[3 * g + c][:, 0:w], ACT.Sigmoid,
                                           bias=column(b, j)).then_inc(gated, 1)
                    act.wait_ge(lam, 2)
                    act.wait_ge(gated, 6 * j + 6)
                    act.activation(a, r, ACT.Exp, scale=sp4[:, 7, j:j + 1]).then_inc(powers, 1)
                    act.activation(th, r, ACT.Tanh, scale=sp4[:, 6, j:j + 1]).then_inc(powers, 1)
                if j >= 1:
                    act.wait_ge(squares, j)
                    th = th2[:, (j - 1) % 2, :]
                    act.activation(th, th, ACT.Sqrt).then_inc(rooted, 1)
                if j < LT:
                    for n in (2 * j, 2 * j + 1):
                        if n + 2 < mk.N:
                            mk.split_high(act, n + 2)
                        mk.copy(act, n)
                    if j == 1:
                        mk.square(act)
                    if j == 2:
                        mk.roots(act)
            mk.copy_rows(act)
            act.wait_ge(tail_turned, 1)
            act.copy(tails[:, :], bank[6][0:36, :]).then_inc(tail_copied, 1)

        @block.vector
        def _(dve):
            n = [0]

            def then(ins):
                n[0] += 1
                ins.then_inc(step, 1)
                dve.wait_ge(step, n[0])

            dve.memset(wab[:, :, :, :], 0.0).then_inc(w_zero, 1)
            for s in range(2):
                dve.memset(xp[:, s, 0:3], 0.0)
            dve.wait_ge(state_turned, 1)
            dve.tensor_copy(states[:, :], bank[7][:, 0:LT * 24]).then_inc(states_copied, 1)
            dve.wait_ge(states_copied, 1)

            def convolve(j):
                s, conv = j % 2, conv2[:, j % 2, :]
                then(dve.tensor_copy(xs[:, s, :, 0:3], states[:, j * 24:(j + 1) * 24].rearrange(
                    "p (b s) -> p b s", b=DEC_B)))
                dve.wait_ge(x_in[s], 32 * (j // 2 + 1))
                cs = conv[:, SEQ:NT].rearrange("p (b t) -> p b t", b=DEC_B)
                for k in range(4):
                    w = column("conv_w", 4 * k + j)
                    src = ((conv[:, 0:SEQ], xp[:, s, k:k + SEQ]), (cs, xs[:, s, :, k:k + DEC_T]))
                    for part, (dst, x) in enumerate(src):
                        if k == 0:
                            ins = dve.tensor_scalar(dst, x, w, column("conv_b", j), ALU.mult, ALU.add)
                        else:
                            ins = dve.scalar_tensor_tensor(dst, x, w, dst, ALU.mult, ALU.add)
                        if k == 3 and part == 1:
                            ins.then_inc(conv_done, 1)
                        elif part == 0:
                            n[0] += 1
                            ins.then_inc(step, 1)
                        else:
                            then(ins)
                dve.tensor_copy(tail[:, j, 0:3], xp[:, s, SEQ:XP])
                dve.tensor_copy(tail[:, j, 3:27].rearrange("p (b s) -> p b s", b=DEC_B),
                                xs[:, s, :, DEC_T:DEC_T + 3]).then_inc(x_used, 1)

            def inputs(j):
                r, ig, a, th, conv = (t[:, j % 2, :] for t in (r2, ig2, a2, th2, conv2))
                dve.wait_ge(gated, 6 * j + 6)
                dve.wait_ge(conv_done, j + 1)
                then(dve.tensor_tensor(ig, ig, conv, ALU.mult))
                dve.wait_ge(powers, 2 * j + 2)
                then(dve.tensor_tensor(r, a, a, ALU.mult))
                dve.scalar_tensor_tensor(th, r, 1.0, th, ALU.add, ALU.mult).then_inc(squares, 1)

            def scan(j):
                s = j % 2
                ig, a, th = (t[:, s, :] for t in (ig2, a2, th2))
                dve.wait_ge(rooted, j + 1)
                then(dve.tensor_tensor(ig, ig, th, ALU.mult))
                a0 = a[:, SEQ:NT].rearrange("p (b t) -> p b t", b=DEC_B)[:, :, 0]
                b0 = ig[:, SEQ:NT].rearrange("p (b t) -> p b t", b=DEC_B)[:, :, 0]
                then(dve.tensor_tensor(h0a[:, :], a0, par_columns(column("h0", 0, 32), j), ALU.mult))
                then(dve.tensor_tensor(b0, b0, h0a[:, :], ALU.add))
                then(dve.memset(a0, 0.0))
                if j >= 1:
                    dve.wait_ge(y_out, 16 * j)
                dve.tensor_tensor_scan(hh[:, 0:SEQ], a[:, 0:SEQ], ig[:, 0:SEQ], 0.0, ALU.mult, ALU.add)
                then(dve.tensor_tensor_scan(hh[:, SEQ:NT], a[:, SEQ:NT], ig[:, SEQ:NT], 0.0, ALU.mult, ALU.add))
                dve.tensor_copy(tail[:, j, 27:28], hh[:, SEQ - 1:SEQ])
                then(dve.tensor_copy(tail[:, j, 28:36], hh[:, SEQ:NT].rearrange("p (b t) -> p b t", b=DEC_B)[
                    :, :, DEC_T - 1]))
                dve.wait_ge(gl_in[s], 16 * (j // 2 + 1))
                dve.tensor_tensor(hh[:, :], hh[:, :], gl[:, s, :], ALU.mult).then_inc(y_done, 1)
                dve.wait_ge(y_done, j + 1)

            dve.memset(mk.eps[:, :], EPS).then_inc(mk.eps_set, 1)
            convolve(0)
            lamb = column("lam", 0, LT)
            then(dve.tensor_scalar(sp4[:, 2, :], lamb, -1.0, None, ALU.mult))
            dve.tensor_tensor(sp4[:, 0, :], sp4[:, 2, :], lamb, ALU.max).then_inc(lam, 1)
            then(dve.tensor_scalar(sp4[:, 2, :], sp4[:, 2, :], 0.0, None, ALU.max))
            dve.wait_ge(lam1, 1)
            then(dve.tensor_scalar(sp4[:, 3, :], sp4[:, 1, :], 2.0, None, ALU.add))
            then(dve.reciprocal(sp4[:, 3, :], sp4[:, 3, :]))
            then(dve.tensor_tensor(sp4[:, 3, :], sp4[:, 3, :], sp4[:, 1, :], ALU.mult))
            then(dve.tensor_tensor(sp4[:, 4, :], sp4[:, 3, :], sp4[:, 3, :], ALU.mult))
            then(dve.tensor_scalar(sp4[:, 5, :], sp4[:, 4, :], 1.0 / 17, 1.0 / 15, ALU.mult, ALU.add))
            for k in (13, 11, 9, 7, 5, 3, 1):
                then(dve.tensor_tensor(sp4[:, 5, :], sp4[:, 5, :], sp4[:, 4, :], ALU.mult))
                then(dve.tensor_scalar(sp4[:, 5, :], sp4[:, 5, :], 1.0 / k, None, ALU.add))
            then(dve.tensor_tensor(sp4[:, 5, :], sp4[:, 5, :], sp4[:, 3, :], ALU.mult))
            then(dve.scalar_tensor_tensor(sp4[:, 5, :], sp4[:, 5, :], 2.0, sp4[:, 2, :], ALU.mult, ALU.add))
            then(dve.tensor_scalar(sp4[:, 6, :], sp4[:, 5, :], 8.0, None, ALU.mult))
            dve.tensor_scalar(sp4[:, 7, :], sp4[:, 5, :], -8.0, None, ALU.mult).then_inc(lam, 1)

            for j in range(LT + 1):
                if j + 1 < LT:
                    convolve(j + 1)
                if j < LT:
                    inputs(j)
                if j >= 1:
                    scan(j - 1)
                if j == 3:
                    mk.norm(dve)


def par_columns(cols, j):
    return cols.rearrange("p (b k) -> p b k", k=LT)[:, :, j]


def memory_input(nc, sem, mem, bank, ident, ones, column, I):
    at = AT_H
    m_in = mem.at("m_in", [P, 2, D], F32, at)
    mT = mem.at("mT", [P, KT, N_MEM], F32, at + 8192)
    m_hi = mem.at("m_hi", [P, KT, N_MEM], F32R, at + 16384)
    m_lo = mem.at("m_lo", [P, KT, N_MEM], F32R, at + 24576)
    m_loaded, turned = sem("m_loaded"), sem("m_turned")
    evicted = [sem("m_evicted0"), sem("m_evicted1")]
    jobs = [dict(src=[m_in[:, t, (4 * half + q) * P:(4 * half + q + 1) * P] for q in range(4)],
                 dst=mT[:, 4 * half:4 * half + 4, t * P:(t + 1) * P],
                 psum=lambda b: b.rearrange("p (q n) -> p q n", q=4), needs=[(m_loaded, 16)])
            for t in range(2) for half in range(2)]
    with nc.Block() as block:
        @block.sync
        def _(sp):
            sp.dma_start(m_in[:, :, :], I["mem_prompt"][0].rearrange("(t p) d -> p t d", p=P)).then_inc(m_loaded, 16)

        @block.tensor
        def _(pe):
            transposes_pe(pe, nc, jobs, ident, bank, None, evicted, turned)

        @block.scalar
        def _(act):
            transposes_evict(act, act.copy, jobs, 0, bank, turned, evicted)

        @block.vector
        def _(dve):
            transposes_evict(dve, dve.tensor_copy, jobs, 1, bank, turned, evicted)

    norm = Norm(sem, mem, bank, mT, N_MEM, [(0, N_MEM)], column("g_mem", 0, KT), ones, m_hi, m_lo, "_mem", at + 32768)
    with nc.Block() as block:
        @block.tensor
        def _(pe):
            norm.on_pe(pe)

        @block.scalar
        def _(act):
            norm.squares(act)
            norm.roots(act)

        @block.vector
        def _(dve):
            norm.on_dve(dve)

        @block.gpsimd
        def _(pool):
            norm.on_pool(pool)
    return m_hi, m_lo


class MemoryKeys:

    def __init__(self, sem, mem, bank, ident, ones, column, raw, w_hi, w_lo, m_hi, m_lo, mkT, mv, I, O):
        self.bank, self.ident, self.ones, self.column = bank, ident, ones, column
        self.raw, self.w_hi, self.w_lo, self.m_hi, self.m_lo = raw, w_hi, w_lo, m_hi, m_lo
        self.mkT, self.mv, self.I, self.O = mkT, mv, I, O
        self.sq = mem.at("mk_sq", [P, 4, N_MEM], F32, AT_H)
        self.rs = mem.at("mk_rs", [P, 4, N_MEM], F32, AT_H + 4096)
        self.rows = mem.at("mk_rows", [P, 2, 512], F32, AT_H + 8192)
        self.eps = mem.at("mk_eps", [P, 1], F32, AT_H + 12288)
        self.loaded = [sem(f"mkv_loaded{i}") for i in range(3)]
        self.high, self.low, self.ready, self.copied = (sem("mkv_high"), sem("mkv_low"), sem("mkv_ready"),
                                                        sem("mkv_copied"))
        self.eps_set, self.squared, self.summed, self.rooted = (sem("mkv_eps"), sem("mkv_squared"),
                                                                sem("mkv_summed"), sem("mkv_rooted"))
        self.inverted, self.normed, self.k_turned, self.k_copied, self.out = (
            sem("mkv_inverted"), sem("mkv_normed"), sem("mk_turned"), sem("mk_copied"), sem("mkv_out"))
        self.N = 8

    def load(self, pool, n):
        w = self.I["w_mem_kv"][0].rearrange("(k p) n -> p k n", p=P)
        if n >= 3:
            pool.wait_ge(self.low, n - 2)
        pool.dma_start(self.raw[:, n % 3, :].rearrange("p (k c) -> p k c", k=KT),
                       w[:, :, n * P:(n + 1) * P]).then_inc(self.loaded[n % 3], 16)

    def split_low(self, pool, n):
        pool.wait_ge(self.high, n + 1)
        pool.tensor_tensor(self.w_lo[:, n % 3, :], self.raw[:, n % 3, :], self.w_hi[:, n % 3, :].bitcast(F32),
                           ALU.subtract).then_inc(self.low, 1)

    def split_high(self, act, n):
        act.wait_ge(self.loaded[n % 3], 16 * (n // 3 + 1))
        if n >= 3:
            act.wait_ge(self.ready, n - 2)
        act.copy(self.w_hi[:, n % 3, :], self.raw[:, n % 3, :]).then_inc(self.high, 1)

    def multiply(self, pe, n):
        pe.wait_ge(self.low, n + 1)
        if n >= 2:
            pe.wait_ge(self.copied, n - 1)
        if n == 6:
            pe.wait_ge(self.rooted, 2)
        hi = lambda k: self.w_hi[:, n % 3, k * P:(k + 1) * P]
        lo = lambda k: self.w_lo[:, n % 3, k * P:(k + 1) * P]
        ks = [(k, k) for k in range(KT)]
        out = self.bank[6 + n % 2]
        if n < 4:
            mm = products(pe, out[:, 0:N_MEM], hi, lo, lambda k: self.m_hi[:, k, :], lambda k: self.m_lo[:, k, :],
                          ks, True, True)
        else:
            for t in range(2):
                mm = products(pe, out[:, t * P:(t + 1) * P], hi, lo, lambda k: self.m_hi[:, k, t * P:(t + 1) * P],
                              lambda k: self.m_lo[:, k, t * P:(t + 1) * P], ks, True, True, flip=True)
        mm.then_inc(self.ready, 1)

    def copy(self, act, n):
        act.wait_ge(self.ready, n + 1)
        if n < 4:
            act.copy(self.mkT[:, n, :], self.bank[6 + n % 2][:, 0:N_MEM]).then_inc(self.copied, 1)
        else:
            act.copy(self.mv[:, :, (n - 4) * P:(n - 3) * P],
                     self.bank[6 + n % 2][:, 0:2 * P].rearrange("p (t c) -> p t c", t=2)).then_inc(self.copied, 1)

    def square(self, act):
        act.wait_ge(self.copied, 4)
        act.activation(self.sq[:, :, :], self.mkT[:, :, :], ACT.Square).then_inc(self.squared, 1)

    def sums(self, pe):
        pe.wait_ge(self.squared, 1)
        pe.wait_ge(self.copied, 6)
        for g in range(2):
            mm = pe.matmul(self.bank[6 + g][:, :], self.ones[:, :],
                           self.sq[:, 2 * g:2 * g + 2, :].rearrange("p h n -> p (h n)"), start=True, stop=True)
        mm.then_inc(self.summed, 1)

    def roots(self, act):
        act.wait_ge(self.summed, 1)
        act.wait_ge(self.eps_set, 1)
        for g in range(2):
            act.activation(self.rs[:, 2 * g:2 * g + 2, :].rearrange("p h n -> p (h n)"), self.bank[6 + g][:, :],
                           ACT.Sqrt, bias=self.eps[:, 0:1], scale=1.0 / P).then_inc(self.rooted, 1)

    def norm(self, dve):
        dve.wait_ge(self.rooted, 2)
        dve.reciprocal(self.rs[:, :, :], self.rs[:, :, :]).then_inc(self.inverted, 1)
        dve.wait_ge(self.inverted, 1)
        for h in range(4):
            dve.scalar_tensor_tensor(self.mkT[:, h, :], self.mkT[:, h, :], self.column("gmk"), self.rs[:, h, :],
                                     ALU.mult, ALU.mult).then_inc(self.normed, 1)

    def turn(self, pe):
        pe.wait_ge(self.normed, 4)
        for t in range(2):
            for h in range(4):
                mm = pe.transpose(self.bank[4 + t][:, h * P:(h + 1) * P], self.mkT[:, h, t * P:(t + 1) * P],
                                  self.ident[:, :])
            mm.then_inc(self.k_turned, 1)

    def copy_rows(self, act):
        for t in range(2):
            act.wait_ge(self.k_turned, t + 1)
            act.copy(self.rows[:, t, :], self.bank[4 + t][:, :]).then_inc(self.k_copied, 1)

    def store(self, sp):
        sp.wait_ge(self.copied, self.N)
        sp.dma_start(self.O["new_mem_v_prompt"][0, 0].rearrange("(t p) h d -> p t (h d)", p=P),
                     self.mv[:, :, :]).then_inc(self.out, 16)
        sp.wait_ge(self.k_copied, 2)
        sp.dma_start(self.O["new_mem_k_prompt"][0, 0].rearrange("(t p) h d -> p t (h d)", p=P),
                     self.rows[:, :, :]).then_inc(self.out, 16)
        sp.wait_ge(self.out, 32)


def attention_plan():
    jobs = []
    for i in (0, 7, 1, 6, 2, 5, 3, 4):
        jobs += [("att", i, h) for h in range(H)] + [("mem", i, h) for h in range(H_MEM)]
    slots = [
        [("kt", 0), ("kt", 1), ("kt", 2), ("kt", 3)],
        [("sc", 0), ("kt", 4), ("kt", 5), ("kt", 6), ("kt", 7)],
        [("sc", 1), ("kt", 8), ("kt", 9), ("kt", 10), ("kt", 11)],
        [("sc", 2), ("kt", 12), ("kt", 13), ("kt", 14), ("kt", 15)],
        [("sc", 3), ("sc", 4)],
        [("soft",), ("kt", 16), ("kt", 17)],
        [("scale",), ("msc",)],
        [("pt", 0), ("pt", 1), ("pt", 2)],
        [("pv",), ("mpt",)],
        [("mpv",), ("ot",)],
        [("mot",)],
        [],
    ]
    plan = []
    turns = 0

    def add(*entry):
        nonlocal turns
        turn = None
        if entry[0] in ("turn", "oturn", "kt", "pt", "mpt", "ot", "mot"):
            turn = turns
            turns += 1
        plan.append((entry, turn))

    n = len(jobs)
    for s in range(n + 2):
        if s < n:
            add("scores", s)
        if 0 <= s - 2:
            add("values", s - 2)
            kind, i, h = jobs[s - 2]
            if (kind, h) in (("att", H - 1), ("mem", H_MEM - 1)):
                add("oturn", s - 2)
        if 0 <= s - 1 < n:
            kind, i, h = jobs[s - 1]
            blocks = i + 1 if kind == "att" else 2
            for g in range(0, blocks, 4):
                add("turn", s - 1, g, min(4, blocks - g))
        if s < n:
            add("exp", s)
            for e in slots[s % 12]:
                add(e[0], s // 12, *e[1:])
    return jobs, plan


def attention(nc, sem, mem, bank, bank_t, ident, ident16, qT, kT, qmT, mkT, mv, bias, bias_s, rep, I, O):
    jobs, plan = attention_plan()
    at = AT_X + 8192
    def place(name, shape, dt, size):
        nonlocal at
        t = mem.at(name, shape, dt, at)
        at += (size + 31) // 32 * 32
        assert at <= AT_B, (name, at - AT_B)
        return t
    KR, UP = 6, PAGES + 2
    kt4 = mem.at("kt4", [P, 2, 4, 512], F32, AT_H + 12 * NT * 4)
    v_ring = mem.at("v_ring", [P, UP, 512], F32, AT_W)
    vp = place("vp", [P, 8, 512], F32, 16384)
    k_ring = place("k_ring", [P, KR, 512], F32, KR * 2048)
    pb = place("pb", [P, 2, SEQ], F32, 8192)
    pt = place("pt", [P, 8, P], F32, 4096)
    ps = place("ps", [P, PAST + DEC_T], F32, (PAST + DEC_T) * 4)
    own = place("own", [P, NS], F32, NS * 4)
    pts = place("pts", [P, PAGES + 1, NS], F32, (PAGES + 1) * NS * 4)
    qbd = place("qbd", [P, DEC_B, 4, NS], F32, 8192)
    qmbd = place("qmbd", [P, DEC_B, 4, 32], F32, 4096)
    o_sb = place("o_sb", [P, 512], F32, 2048)
    os_ = place("os", [P, P], F32, P * 4)
    om_ = place("om", [32, 512], F32, 2048)
    vn = place("vn", [DEC_T, 512], F32, 2048)
    mks = place("mks", [P, 4, N_MEM], F32, 4096)
    pm = place("pm", [32, N_MEM], F32, 1024)
    ptm = place("ptm", [P, 2, 32], F32, 256)
    stats = place("stats", [P, 12], F32, 48)
    nm, rsum, rinv = stats[:, 0:4], stats[:, 4:8], stats[:, 8:12]
    st = mem.at("st", [P, 8], F32, AT_C + 3552)
    table = mem.at("table2", [1, DEC_B * PAGES], I32, AT_C + 3584)
    turn_bank = [bank[4], bank[7]]

    table_in, vp_in = sem("table_in"), sem("vp_in")
    k_in = [sem(f"k_in{i}") for i in range(KR)]
    v_in = [sem(f"v_in{i}") for i in range(3)]
    vn_in = sem("vn_in")
    built0, built = sem("qbd_zero"), sem("qbd_built")
    scored, maxed, exped, inverted = sem("scored"), sem("maxed"), sem("exped"), sem("inverted")
    valued, normed = sem("valued"), sem("normed")
    turned = sem("turned2")
    evicted = [sem("turn_act"), sem("turn_dve")]
    used5, freed5 = sem("used5"), sem("freed5")
    s_scaled, own_made = sem("s_scaled"), sem("own_made")
    s_max, s_exp, s_inv, s_norm = sem("s_max"), sem("s_exp"), sem("s_inv"), sem("s_norm")
    m_max, m_exp, m_inv, m_norm = sem("m_max"), sem("m_exp"), sem("m_inv"), sem("m_norm")

    turn_of = {entry: turn for entry, turn in plan if turn is not None}
    use_of = {}
    for entry, _ in plan:
        if entry[0] in ("sc", "msc", "pv", "mpv"):
            use_of[entry] = len(use_of)

    def wait_turn(eng, turn):
        eng.wait_ge(evicted[turn % 2], turn // 2 + 1)

    def last_turn(s):
        blocks = jobs[s][1] + 1 if jobs[s][0] == "att" else 2
        g = (blocks - 1) // 4 * 4
        return turn_of[("turn", s, g, blocks - g)]

    def turns_of(s):
        blocks = jobs[s][1] + 1 if jobs[s][0] == "att" else 2
        return [turn_of[("turn", s, g, min(4, blocks - g))] for g in range(0, blocks, 4)]

    def evict(eng, copy, me, entry, turn):
        if turn is None or turn % 2 != me:
            return
        b = turn_bank[me]
        eng.wait_ge(turned, turn + 1)
        kind = entry[0]
        if kind == "turn":
            _, s, g, w = entry
            if s >= 1:
                eng.wait_ge(valued, s)
            copy(pt[:, g:g + w, :], b[:, 0:w * P].rearrange("p (g n) -> p g n", n=P)).then_inc(evicted[me], 1)
        elif kind == "oturn":
            s = entry[1]
            dst = qT if jobs[s][0] == "att" else qmT
            i = jobs[s][1]
            copy(dst[:, :, i * P:(i + 1) * P], b.rearrange("p (g n) -> p g n", g=4)).then_inc(evicted[me], 1)
        elif kind == "kt":
            _, b_, u = entry
            if u < PAGES:
                g = u // 4
                if 4 * b_ + g >= 2:
                    older = (b_, g - 2) if g >= 2 else (b_ - 1, g + 2)
                    eng.wait_ge(used5, use_of[("sc", *older)] + 1)
                dst = kt4[:, g % 2, :, (u % 4) * P:(u % 4 + 1) * P]
            else:
                if b_ >= 1:
                    eng.wait_ge(used5, use_of[("msc", b_ - 1)] + 1)
                dst = mks[:, :, (u - PAGES) * P:(u - PAGES + 1) * P]
            copy(dst, b.rearrange("p (g n) -> p g n", g=4)).then_inc(evicted[me], 1)
        elif kind == "pt":
            _, b_, g = entry
            if b_ >= 1:
                eng.wait_ge(used5, use_of[("pv", b_ - 1)] + 1)
            if g < 2:
                copy(pts[:, 8 * g:8 * g + 8, :], b.rearrange("p (g n) -> p g n", n=NS)).then_inc(evicted[me], 1)
            else:
                copy(pts[0:DEC_T, PAGES, :], b[0:DEC_T, 0:NS]).then_inc(evicted[me], 1)
        elif kind == "mpt":
            if entry[1] >= 1:
                eng.wait_ge(used5, use_of[("mpv", entry[1] - 1)] + 1)
            copy(ptm[:, :, :], b[:, 0:64].rearrange("p (g n) -> p g n", g=2)).then_inc(evicted[me], 1)
        elif kind == "ot":
            b_ = entry[1]
            for e in range(2):
                r, at = slice(e * DH, (e + 1) * DH), SEQ + 8 * b_
                src = b[r, 0:96].rearrange("p (j c) -> p j c", c=32)[:, :, 8 * e:8 * e + DEC_T]
                copy(qT[r, 0:3, at:at + 8], src)
                ins = copy(qT[r, 3, at:at + 8], b[r, 112 + 8 * e:120 + 8 * e])
            ins.then_inc(evicted[me], 1)
        elif kind == "mot":
            b_ = entry[1]
            src = b[:, 0:160].rearrange("p (j c) -> p j c", c=40)[:, :, 0:DEC_T]
            copy(qmT[:, :, SEQ + 8 * b_:SEQ + 8 * b_ + 8], src).then_inc(evicted[me], 1)

    with nc.Block() as block:
        @block.sync
        def _(sp):
            sp.dma_start(table[:, :], I["page_table"].rearrange("b g -> (b g)").rearrange(
                "(a n) -> a n", a=1)).then_inc(table_in, 16)
            sp.dma_start(vp[:, :, :], O["new_v_prompt"][0, 0].rearrange("(t p) h d -> p t (h d)", p=P)
                         ).then_inc(vp_in, 16)
            sp.wait_ge(table_in, 16)
            for b in range(DEC_B):
                pages = {}

                def page(u):
                    if u not in pages:
                        at = b * PAGES + u
                        pages[u] = sp.value_load(table[0:1, at:at + 1], min_val=0, max_val=I["cache_k"].shape[1] - 1)
                    return pages[u]

                def source(name, mem_name, u):
                    if u < PAGES:
                        return I[name][0][bass.ds(page(u), 1)].rearrange("a p h d -> p (a h d)")
                    return I[mem_name][0][b].rearrange("(t p) h d -> t p (h d)", p=P)[u - PAGES]
                for u in range(UP):
                    n = b * UP + u
                    if n >= KR:
                        before = divmod(n - KR, UP)
                        sp.wait_ge(turned, turn_of[("kt", *before)] + 1)
                    sp.dma_start(k_ring[:, n % KR, :], source("cache_k", "cache_mem_k", u)).then_inc(k_in[n % KR], 16)
                    if u == 0 and b >= 1:
                        sp.wait_ge(used5, use_of[("pv", b - 1)] + 1)
                        sp.wait_ge(used5, use_of[("mpv", b - 1)] + 1)
                    sp.dma_start(v_ring[:, u, :], source("cache_v", "cache_mem_v", u)).then_inc(v_in[u // 8], 16)
                    if u == 0:
                        sp.dma_start(vn[:, :], O["new_v_sample"][0][b].rearrange("t h d -> t (h d)")
                                     ).then_inc(vn_in, 16)

        @block.gpsimd
        def _(pool):
            pool.memset(qbd[:, :, :, :], 0.0).then_inc(built0, 1)
            pool.memset(qmbd[:, :, :, :], 0.0).then_inc(built0, 1)
            pool.wait_ge(built0, 2)
            for j in range(4):
                for e in range(2):
                    h = 2 * j + e
                    r = slice(e * DH, (e + 1) * DH)
                    if h:
                        pool.wait_ge(built, h)
                    pool.tensor_copy(qbd[r, :, j, h * 8:h * 8 + 8],
                                     qT[r, j, SEQ:NT].rearrange("p (b t) -> p b t", b=DEC_B)).then_inc(built, 1)
            pool.wait_ge(built, H)
            for h in range(H_MEM):
                pool.tensor_copy(qmbd[:, :, h, h * 8:h * 8 + 8],
                                 qmT[:, h, SEQ:NT].rearrange("p (b t) -> p b t", b=DEC_B)).then_inc(built, 1)

        @block.tensor
        def _(pe):
            for entry, turn in plan:
                kind, s = entry[0], entry[1]
                if turn is not None and turn >= 2:
                    wait_turn(pe, turn - 2)
                tb = turn_bank[turn % 2] if turn is not None else None
                if kind == "scores":
                    what, i, h = jobs[s]
                    b0 = 2 * (s % 2)
                    if s >= 2:
                        pe.wait_ge(exped, s - 1)
                    if what == "mem":
                        mm = pe.matmul(bank[b0][:, 0:N_MEM], qmT[:, h, i * P:(i + 1) * P], mkT[:, h, :],
                                       start=True, stop=True)
                    else:
                        r = slice((h % 2) * DH, (h % 2) * DH + DH)
                        keys = (i + 1) * P
                        for c, k0 in enumerate(range(0, keys, 512)):
                            w = min(512, keys - k0)
                            out = bank[b0 + c][:, 0:w]
                            pe.matmul(out, ident16[:, :], bias[:, bias_at(i) + k0:bias_at(i) + k0 + w], start=True,
                                      stop=False)
                            mm = pe.matmul(out, qT[r, h // 2, i * P:(i + 1) * P], kT[r, h // 2, k0:k0 + w],
                                           start=False, stop=True)
                    mm.then_inc(scored, 1)
                elif kind == "turn":
                    _, s, g, w = entry
                    pe.wait_ge(exped, s + 1)
                    for q in range(w):
                        mm = pe.transpose(tb[:, q * P:(q + 1) * P], pb[:, s % 2, (g + q) * P:(g + q + 1) * P],
                                          ident[:, :])
                    mm.then_inc(turned, 1)
                elif kind == "values":
                    what, i, h = jobs[s]
                    for t in turns_of(s):
                        wait_turn(pe, t)
                    if s == 0:
                        pe.wait_ge(vp_in, 16)
                    if s >= 1:
                        pe.wait_ge(normed, s)
                    if what == "att":
                        for j in range(i + 1):
                            mm = pe.matmul(bank[6][:, h * DH:(h + 1) * DH], pt[:, j, :],
                                           vp[:, j, h * DH:(h + 1) * DH], start=(j == 0), stop=(j == i))
                    else:
                        for j in range(2):
                            mm = pe.matmul(bank[6][:, h * P:(h + 1) * P], pt[:, j, :], mv[:, j, h * P:(h + 1) * P],
                                           start=(j == 0), stop=(j == 1))
                    mm.then_inc(valued, 1)
                elif kind == "oturn":
                    pe.wait_ge(normed, s + 1)
                    for j in range(4):
                        mm = pe.transpose(tb[:, j * P:(j + 1) * P], o_sb[:, j * P:(j + 1) * P], ident[:, :])
                    mm.then_inc(turned, 1)
                elif kind == "kt":
                    n = s * UP + entry[2]
                    pe.wait_ge(k_in[n % KR], 16 * (n // KR + 1))
                    for j in range(4):
                        mm = pe.transpose(tb[:, j * P:(j + 1) * P], k_ring[:, n % KR, j * P:(j + 1) * P], ident[:, :])
                    mm.then_inc(turned, 1)
                elif kind == "sc":
                    _, b, g = entry
                    if use_of[entry]:
                        pe.wait_ge(freed5, use_of[entry])
                    if b == 0 and g == 0:
                        pe.wait_ge(built, 12)
                    w = 512 if g < 4 else DEC_T
                    if g < 4:
                        for u in range(4 * g, 4 * g + 4):
                            wait_turn(pe, turn_of[("kt", b, u)])
                    for j in range(4):
                        a = min(16 * j, 32)
                        pe.matmul(bank[5][32 * j:32 * j + 32, 0:w], rep[:, b, a:a + 32],
                                  bias_s[:, g * 512:g * 512 + w], start=True, stop=False, tile_position=(0, 32 * j))
                    for j in range(4):
                        a = min(16 * j, 32)
                        keys = kt4[:, g % 2, j, :] if g < 4 else kT[:, j, SEQ + 8 * b:SEQ + 8 * b + 8]
                        mm = pe.matmul(bank[5][32 * j:32 * j + 32, 0:w], qbd[:, b, j, a:a + 32], keys, start=False,
                                       stop=True, tile_position=(0, 32 * j))
                    mm.then_inc(used5, 1)
                elif kind == "msc":
                    pe.wait_ge(freed5, use_of[entry])
                    for u in (PAGES, PAGES + 1):
                        wait_turn(pe, turn_of[("kt", s, u)])
                    for h in range(H_MEM):
                        mm = pe.matmul(bank[5][0:32, 0:N_MEM], qmbd[:, s, h, :], mks[:, h, :], start=(h == 0),
                                       stop=(h == 3))
                    mm.then_inc(used5, 1)
                elif kind == "pt":
                    pe.wait_ge(own_made, 1)
                    pe.wait_ge(s_scaled, s + 1)
                    g = entry[2]
                    if g < 2:
                        for q in range(8):
                            k = 8 * g + q
                            mm = pe.matmul(tb[:, q * NS:(q + 1) * NS], ps[:, k * P:(k + 1) * P], own[:, :],
                                           start=True, stop=True)
                    else:
                        mm = pe.matmul(tb[0:DEC_T, 0:NS], ps[:, PAST:PAST + DEC_T], own[:, :], start=True, stop=True)
                    mm.then_inc(turned, 1)
                elif kind == "pv":
                    pe.wait_ge(freed5, use_of[entry])
                    for g in range(3):
                        wait_turn(pe, turn_of[("pt", s, g)])
                    pe.wait_ge(v_in[0], 128 * (s + 1))
                    pe.wait_ge(v_in[1], 128 * (s + 1))
                    pe.wait_ge(vn_in, 16 * (s + 1))
                    for k in range(PAGES + 1):
                        for j in range(4):
                            a = min(16 * j, 32)
                            left, right = (pts[:, k, a:a + 32], v_ring[:, k, j * P:(j + 1) * P]) if k < PAGES else \
                                (pts[0:DEC_T, k, a:a + 32], vn[:, j * P:(j + 1) * P])
                            mm = pe.matmul(bank[5][32 * j:32 * j + 32, 0:P], left, right, start=(k == 0),
                                           stop=(k == PAGES), tile_position=(0, 32 * j))
                    mm.then_inc(used5, 1)
                elif kind == "ot":
                    pe.wait_ge(s_norm, s + 1)
                    pe.transpose(tb[:, 0:P], os_[:, :], ident[:, :]).then_inc(turned, 1)
                elif kind == "mpt":
                    pe.wait_ge(m_exp, s + 1)
                    for j in range(2):
                        mm = pe.transpose(tb[:, j * 32:(j + 1) * 32], pm[:, j * P:(j + 1) * P], ident[0:32, 0:32])
                    mm.then_inc(turned, 1)
                elif kind == "mpv":
                    pe.wait_ge(freed5, use_of[entry])
                    wait_turn(pe, turn_of[("mpt", s)])
                    pe.wait_ge(v_in[2], 32 * (s + 1))
                    for j in range(2):
                        mm = pe.matmul(bank[5][0:32, :], ptm[:, j, :], v_ring[:, PAGES + j, :], start=(j == 0),
                                       stop=(j == 1))
                    mm.then_inc(used5, 1)
                elif kind == "mot":
                    pe.wait_ge(m_norm, s + 1)
                    for j in range(4):
                        mm = pe.transpose(tb[:, j * 32:(j + 1) * 32], om_[:, j * P:(j + 1) * P], ident[0:32, 0:32])
                    mm.then_inc(turned, 1)

        @block.scalar
        def _(act):
            for entry, turn in plan:
                kind, s = entry[0], entry[1]
                evict(act, act.copy, 0, entry, turn)
                if kind == "exp":
                    what, i, h = jobs[s]
                    b0 = 2 * (s % 2)
                    keys = (i + 1) * P if what == "att" else N_MEM
                    act.wait_ge(maxed, s + 1)
                    if s >= 2:
                        act.wait_ge(turned, last_turn(s - 2) + 1)
                    if s >= 4:
                        act.wait_ge(inverted, s - 3)
                    act.activation(pb[:, s % 2, 0:keys], bank_t[:, b0:b0 + 2, :].rearrange("p b n -> p (b n)")[:, 0:keys],
                                   ACT.Exp, bias=nm[:, s % 4:s % 4 + 1],
                                   accum_out=rsum[:, s % 4:s % 4 + 1]).then_inc(exped, 1)
                elif kind == "sc":
                    _, b, g = entry
                    w = 512 if g < 4 else DEC_T
                    act.wait_ge(used5, use_of[entry] + 1)
                    if b >= 1:
                        act.wait_ge(turned, turn_of[("pt", b - 1, 2)] + 1)
                    act.copy(ps[:, g * 512:g * 512 + w], bank[5][:, 0:w]).then_inc(freed5, 1)
                elif kind == "soft":
                    act.wait_ge(s_max, s + 1)
                    act.activation(ps[:, :], ps[:, :], ACT.Exp, bias=st[:, 0:1], accum_out=st[:, 1:2]).then_inc(s_exp, 1)
                elif kind == "msc":
                    act.wait_ge(m_max, s + 1)
                    if s >= 1:
                        act.wait_ge(turned, turn_of[("mpt", s - 1)] + 1)
                    act.activation(pm[:, :], bank[5][0:32, 0:N_MEM], ACT.Exp, bias=st[0:32, 3:4],
                                   accum_out=st[0:32, 4:5]).then_inc(m_exp, 1)
                    act.wait_ge(m_exp, s + 1)
                    act.sem_inc(freed5, 1)

        @block.vector
        def _(dve):
            dve.tensor_copy(own[:, 0:48].rearrange("p (j c) -> p j c", c=16),
                            ident[:, 0:96].rearrange("p (j c) -> p j c", c=32)[:, :, 0:16])
            dve.tensor_copy(own[:, 48:NS], ident[:, 112:P]).then_inc(own_made, 1)
            for entry, turn in plan:
                kind, s = entry[0], entry[1]
                evict(dve, dve.tensor_copy, 1, entry, turn)
                if kind == "scores":
                    what, i, h = jobs[s]
                    b0 = 2 * (s % 2)
                    keys = (i + 1) * P if what == "att" else N_MEM
                    dve.wait_ge(scored, s + 1)
                    if s >= 4:
                        dve.wait_ge(exped, s - 3)
                    dve.tensor_reduce(nm[:, s % 4:s % 4 + 1], bank_t[:, b0:b0 + 2, :].rearrange(
                        "p b n -> p (b n)")[:, 0:keys], AX.X, ALU.max, negate=True).then_inc(maxed, 1)
                elif kind == "values":
                    what, i, h = jobs[s]
                    w = DH if what == "att" else P
                    dve.wait_ge(exped, s + 1)
                    dve.reciprocal(rinv[:, s % 4:s % 4 + 1], rsum[:, s % 4:s % 4 + 1]).then_inc(inverted, 1)
                    dve.wait_ge(valued, s + 1)
                    dve.wait_ge(inverted, s + 1)
                    if h == 0 and s >= 1:
                        dve.wait_ge(turned, turn_of[("oturn", s - 1)] + 1)
                    dve.tensor_scalar(o_sb[:, h * w:(h + 1) * w], bank[6][:, h * w:(h + 1) * w],
                                      rinv[:, s % 4:s % 4 + 1], None, ALU.mult).then_inc(normed, 1)
                elif kind == "soft":
                    dve.wait_ge(freed5, use_of[("sc", s, 4)] + 1)
                    if s >= 1:
                        dve.wait_ge(s_exp, s)
                    dve.tensor_reduce(st[:, 0:1], ps[:, :], AX.X, ALU.max, negate=True).then_inc(s_max, 1)
                elif kind == "scale":
                    dve.wait_ge(s_exp, s + 1)
                    dve.reciprocal(st[:, 2:3], st[:, 1:2]).then_inc(s_inv, 1)
                    dve.wait_ge(s_inv, s + 1)
                    dve.tensor_scalar(ps[:, :], ps[:, :], st[:, 2:3], None, ALU.mult).then_inc(s_scaled, 1)
                elif kind == "msc":
                    dve.wait_ge(used5, use_of[entry] + 1)
                    dve.tensor_reduce(st[0:32, 3:4], bank[5][0:32, 0:N_MEM], AX.X, ALU.max,
                                      negate=True).then_inc(m_max, 1)
                elif kind == "pv":
                    dve.wait_ge(used5, use_of[entry] + 1)
                    if s >= 1:
                        dve.wait_ge(turned, turn_of[("ot", s - 1)] + 1)
                    dve.tensor_copy(os_[:, :], bank[5][:, 0:P]).then_inc(s_norm, 1)
                    dve.wait_ge(s_norm, s + 1)
                    dve.sem_inc(freed5, 1)
                elif kind == "mpv":
                    dve.wait_ge(m_exp, s + 1)
                    dve.reciprocal(st[0:32, 5:6], st[0:32, 4:5]).then_inc(m_inv, 1)
                    dve.wait_ge(m_inv, s + 1)
                    dve.wait_ge(used5, use_of[entry] + 1)
                    if s >= 1:
                        dve.wait_ge(turned, turn_of[("mot", s - 1)] + 1)
                    dve.tensor_scalar(om_[:, :], bank[5][0:32, :], st[0:32, 5:6], None, ALU.mult).then_inc(m_norm, 1)
                    dve.wait_ge(m_norm, s + 1)
                    dve.sem_inc(freed5, 1)


def merge(nc, sem, mem, bank, x, raw, w_hi, w_lo, qT, qmT, x_kept, I, scratch):
    T4 = 4 * NT * 4
    o_hi = [mem.at(f"mo_hi{br}", [P, 4, NT], F32R, at) for br, at in enumerate((AT_A, AT_H + 3 * T4, AT_H + 2 * T4))]
    o_lo = [mem.at(f"mo_lo{br}", [P, 4, NT], F32R, at) for br, at in enumerate((AT_A + T4, AT_H, AT_A + T4))]
    oy = mem.at("oy", [P, 4, NT], F32, AT_H + 4 * NT * 4)
    gate = mem.at("gate", [P, 2, NT], F32, AT_A + 8 * NT * 4)
    gated = mem.at("gated", [P, 2, CW], F32, AT_A + 10 * NT * 4)
    m = mem.at("m", [P, KT, NT], F32, AT_X)
    m_hi = mem.at("m_hi2", [P, KT, NT], F32R, AT_H)
    m_lo = mem.at("m_lo2", [P, KT, NT], F32R, AT_H + KT * NT * 4)
    x2 = mem.at("x2", [P, KT, NT], F32, AT_A)
    branches = [("w_attn_o", qT), ("w_mem_o", qmT), ("w_lru_o", oy)]
    gate_of = [0, 2, 1]
    loaded = [sem(f"mg_loaded{i}") for i in range(3)]
    high, low, ready = sem("mg_high"), sem("mg_low"), sem("mg_ready")
    y_in, gate_in = sem("y_in"), [sem("gate_in0"), sem("gate_in1")]
    o_high, o_low = sem("o_high"), sem("o_low")
    taken, added = sem("mg_taken"), sem("mg_added")
    N = 12
    with nc.Block() as block:
        @block.sync
        def _(sp):
            for n in range(N):
                br, u = divmod(n, 4)
                if n == 3:
                    sp.dma_start(oy[:, :, :], scratch["y"].rearrange("j p n -> p j n")).then_inc(y_in, 16)
                if n >= 3:
                    sp.wait_ge(low, n - 2)
                w = I[branches[br][0]][0].rearrange("(k p) n -> p k n", p=P)
                sp.dma_start(raw[:, n % 3, :].rearrange("p (k c) -> p k c", k=4),
                             w[:, :, u * 256:(u + 1) * 256]).then_inc(loaded[n % 3], 16)
                for half in range(2):
                    g = 2 * n + half
                    if g >= 2:
                        sp.wait_ge(taken, 3 * (g - 1))
                    sp.dma_start(gate[:, g % 2, :], scratch["g"][gate_of[br] * KT + 2 * u + half]
                                 ).then_inc(gate_in[g % 2], 16)

        @block.gpsimd
        def _(pool):
            for n in range(N):
                pool.wait_ge(high, n + 1)
                pool.tensor_tensor(w_lo[:, n % 3, :], raw[:, n % 3, :], w_hi[:, n % 3, :].bitcast(F32),
                                   ALU.subtract).then_inc(low, 1)

        @block.tensor
        def _(pe):
            for n in range(N):
                br, u = divmod(n, 4)
                pe.wait_ge(low, n + 1)
                pe.wait_ge(o_low, 4 * (br + 1))
                for half in range(2):
                    for c, (t0, w) in enumerate(CH):
                        q = 3 * (2 * n + half) + c
                        if q >= 6:
                            pe.wait_ge(taken, q - 5)
                        mm = products(pe, bank[q % 6][:, 0:w],
                                      lambda k: w_hi[:, n % 3, k * 256 + half * P:k * 256 + half * P + P],
                                      lambda k: w_lo[:, n % 3, k * 256 + half * P:k * 256 + half * P + P],
                                      lambda k: o_hi[br][:, k, t0:t0 + w], lambda k: o_lo[br][:, k, t0:t0 + w],
                                      [(k, k) for k in range(4)], True, True)
                        mm.then_inc(ready, 1)

        @block.scalar
        def _(act):
            def high_part(n):
                act.wait_ge(loaded[n % 3], 16 * (n // 3 + 1))
                if n >= 3:
                    act.wait_ge(ready, 6 * (n - 2))
                act.copy(w_hi[:, n % 3, :], raw[:, n % 3, :]).then_inc(high, 1)
            def split(br):
                if br == 2:
                    act.wait_ge(y_in, 16)
                if br:
                    act.wait_ge(o_low, 4 * br)
                for k in range(4):
                    act.copy(o_hi[br][:, k, :], branches[br][1][:, k, :]).then_inc(o_high, 1)
            split(0)
            high_part(0)
            high_part(1)
            for n in range(N):
                br, u = divmod(n, 4)
                if u == 1 and br < 2:
                    split(br + 1)
                if n + 2 < N:
                    high_part(n + 2)

        @block.vector
        def _(dve):
            def split(br):
                if br == 2:
                    dve.wait_ge(ready, 24)
                for k in range(4):
                    dve.wait_ge(o_high, 4 * br + k + 1)
                    dve.tensor_tensor(o_lo[br][:, k, :], branches[br][1][:, k, :], o_hi[br][:, k, :].bitcast(F32),
                                      ALU.subtract).then_inc(o_low, 1)
            split(0)
            for n in range(N):
                br, u = divmod(n, 4)
                if u == 1 and br < 2:
                    split(br + 1)
                for half in range(2):
                    g = 2 * n + half
                    dve.wait_ge(gate_in[g % 2], 16 * (g // 2 + 1))
                    for c, (t0, w) in enumerate(CH):
                        q = 3 * g + c
                        dve.wait_ge(ready, q + 1)
                        dst = m[:, 2 * u + half, t0:t0 + w]
                        out = dst if br == 0 else gated[:, q % 2, 0:w]
                        dve.tensor_tensor(out, bank[q % 6][:, 0:w], gate[:, g % 2, t0:t0 + w],
                                          ALU.mult).then_inc(taken, 1)
                        if br:
                            dve.wait_ge(taken, q + 1)
                            dve.tensor_tensor(dst, dst, gated[:, q % 2, 0:w], ALU.add).then_inc(added, 1)

    loaded = [sem(f"wo_loaded{i}") for i in range(3)]
    high, low, ready, done = sem("wo_high"), sem("wo_low"), sem("wo_ready"), sem("wo_done")
    m_high, m_low, x_in = sem("m_high"), sem("m_low"), sem("x_in")
    w_out = I["w_out"][0].rearrange("(k p) n -> p k n", p=P)
    N2 = KT
    with nc.Block() as block:
        @block.sync
        def _(sp):
            for n in range(N2):
                if n == 3:
                    sp.dma_start(x2[:, :, :], x_kept).then_inc(x_in, 16)
                if n >= 3:
                    sp.wait_ge(low, n - 2)
                sp.dma_start(raw[:, n % 3, :].rearrange("p (k c) -> p k c", k=KT),
                             w_out[:, :, n * P:(n + 1) * P]).then_inc(loaded[n % 3], 16)

        @block.gpsimd
        def _(pool):
            for n in range(N2):
                pool.wait_ge(high, n + 1)
                pool.tensor_tensor(w_lo[:, n % 3, :], raw[:, n % 3, :], w_hi[:, n % 3, :].bitcast(F32),
                                   ALU.subtract).then_inc(low, 1)

        @block.tensor
        def _(pe):
            for n in range(N2):
                pe.wait_ge(low, n + 1)
                for c, (t0, w) in enumerate(CH):
                    q = 3 * n + c
                    if q >= 6:
                        pe.wait_ge(done, q - 5)
                    for k in range(KT):
                        if n == 0 and c == 0:
                            pe.wait_ge(m_low, k + 1)
                        mm = products(pe, bank[q % 6][:, 0:w], lambda k: w_hi[:, n % 3, k * P:(k + 1) * P],
                                      lambda k: w_lo[:, n % 3, k * P:(k + 1) * P], lambda k: m_hi[:, k, t0:t0 + w],
                                      lambda k: m_lo[:, k, t0:t0 + w], [(k, k)], k == 0, k == KT - 1)
                    mm.then_inc(ready, 1)

        @block.scalar
        def _(act):
            def high_part(n):
                act.wait_ge(loaded[n % 3], 16 * (n // 3 + 1))
                if n >= 3:
                    act.wait_ge(ready, 3 * (n - 2))
                act.copy(w_hi[:, n % 3, :], raw[:, n % 3, :]).then_inc(high, 1)
            for k in range(KT):
                act.copy(m_hi[:, k, :], m[:, k, :]).then_inc(m_high, 1)
                if k < 2:
                    high_part(k)
            for n in range(2, N2):
                high_part(n)

        @block.vector
        def _(dve):
            for k in range(KT):
                dve.wait_ge(m_high, k + 1)
                dve.tensor_tensor(m_lo[:, k, :], m[:, k, :], m_hi[:, k, :].bitcast(F32),
                                  ALU.subtract).then_inc(m_low, 1)
            dve.wait_ge(m_low, KT)
            dve.wait_ge(x_in, 16)
            for n in range(N2):
                for c, (t0, w) in enumerate(CH):
                    q = 3 * n + c
                    dve.wait_ge(ready, q + 1)
                    dve.tensor_tensor(x[:, n, t0:t0 + w], bank[q % 6][:, 0:w], x2[:, n, t0:t0 + w],
                                      ALU.add).then_inc(done, 1)


OUTS = [("y_prompt", (1, SEQ, D)), ("y_sample", (DEC_B, DEC_T, D)), ("new_k_prompt", (1, 1, SEQ, H, DH)),
        ("new_v_prompt", (1, 1, SEQ, H, DH)), ("new_kidx_prompt", (1, 1, SEQ, DH)),
        ("new_mem_k_prompt", (1, 1, N_MEM, H_MEM, P)), ("new_mem_v_prompt", (1, 1, N_MEM, H_MEM, P)),
        ("new_conv_prompt", (1, 1, 3, LRU_W)), ("new_h_prompt", (1, 1, LRU_W)),
        ("new_k_sample", (1, DEC_B, DEC_T, H, DH)), ("new_v_sample", (1, DEC_B, DEC_T, H, DH)),
        ("new_kidx_sample", (1, DEC_B, DEC_T, DH)), ("new_conv_sample", (1, DEC_B, 3, LRU_W)),
        ("new_h_sample", (1, DEC_B, LRU_W))]


def kernel(**inputs):
    import concourse.bacc as bacc
    from concourse.bass_utils import run_bass_kernel_spmd
    nc = bacc.Bacc("TRN2", target_bir_lowering=False, num_devices=1)
    arrays = {name: np.ascontiguousarray(a) for name, a in inputs.items()}
    I = {name: nc.dram_tensor(f"in_{name}", a.shape, mybir.dt.from_np(a.dtype), kind="ExternalInput").ap()
         for name, a in arrays.items()}
    O = {name: nc.dram_tensor(f"out_{name}", shape, F32, kind="ExternalOutput").ap() for name, shape in OUTS}
    decoder_step(nc, I, O)
    r = run_bass_kernel_spmd(nc, [{f"in_{name}": a for name, a in arrays.items()}], core_ids=[0])
    return tuple(r.results[0][f"out_{name}"] for name, _ in OUTS)
```
